# Optimizing a Trainium2 kernel written in Bass

```python
import math
import jax, jax.numpy as jnp
from jax import lax
import numpy as np

D_MODEL = 1024
BATCH = 1
SEQ = 1024
DEPTH = 1
DEC_BATCH = 8
DEC_SEQ = 4
PAST_LEN = 256
PAGE_SIZE = 128

H_A = 4
DK_A = 128
DV_A = 128
CONV_A = 4
DELTA_CHUNK = 64
QKV_A = 2 * H_A * DK_A + H_A * DV_A
H_B = 4
DH_B = 64
DV_B = 2 * DH_B
Q_BLOCK = 128
NUM_BUCKETS = 32
MAX_DISTANCE = 128
NEG_INF = -1e30
BRANCH_W = H_A * DV_A
D_FF = 2816
CONV_F = 3
EPS = 1e-6
SPLIT_SIZES = (QKV_A, H_A * DV_A, H_A, H_A, H_B * 2 * DH_B, H_B * 2 * DH_B, H_B * DV_B, D_MODEL, D_MODEL)
N_IN = QKV_A + H_A * DV_A + 2 * H_A + 2 * H_B * 2 * DH_B + H_B * DV_B + 2 * D_MODEL

kernel_name = 'hybrid_gdn_diffattn_convffn_step'

def split_points():
    return [int(s) for s in np.cumsum(np.array(SPLIT_SIZES))[:-1]]

def rmsnorm(x, w):
    xf = x.astype(jnp.float32)
    y = xf * lax.rsqrt(jnp.mean(xf * xf, axis=-1, keepdims=True) + EPS)
    return (y * w.astype(jnp.float32)).astype(x.dtype)

def l2norm(x):
    xf = x.astype(jnp.float32)
    return (xf * lax.rsqrt(jnp.sum(xf * xf, axis=-1, keepdims=True) + EPS)).astype(x.dtype)

def causal_dwconv(x, buf, w):
    width = w.shape[0]
    t = x.shape[1]
    xp = jnp.concatenate([buf.astype(x.dtype), x], axis=1)
    y = sum(xp[:, i:i + t] * w[i] for i in range(width))
    return y, xp[:, t:]

def t5_bucket(rel):
    n = jnp.maximum(rel, 0)
    max_exact = NUM_BUCKETS // 2
    nf = jnp.maximum(n, 1).astype(jnp.float32)
    large = max_exact + (jnp.log(nf / max_exact) / math.log(MAX_DISTANCE / max_exact)
                         * (NUM_BUCKETS - max_exact)).astype(jnp.int32)
    large = jnp.minimum(large, NUM_BUCKETS - 1)
    return jnp.where(n < max_exact, n, large)

def gated_delta_chunked(q, k, v, beta, g, s0):
    b, t, h, _ = q.shape
    dv = v.shape[-1]
    c = DELTA_CHUNK if t >= DELTA_CHUNK else t
    pad = (-t) % c
    n = (t + pad) // c
    f32 = jnp.float32

    def prep(a):
        a = jnp.pad(a.astype(f32), [(0, 0), (0, pad)] + [(0, 0)] * (a.ndim - 2))
        a = jnp.moveaxis(a, 2, 1)
        return a.reshape(a.shape[:2] + (n, c) + a.shape[3:])

    q, k, v, beta, g = prep(q), prep(k), prep(v), prep(beta), prep(g)
    gc = jnp.cumsum(g, axis=-1)
    incl = jnp.tril(jnp.ones((c, c), bool))
    strict = jnp.tril(jnp.ones((c, c), bool), -1)
    diff = gc[..., :, None] - gc[..., None, :]
    decay = jnp.where(incl, jnp.exp(jnp.where(incl, diff, 0.0)), 0.0)
    kb = k * beta[..., None]
    vb = v * beta[..., None]
    m = jnp.where(strict, jnp.einsum('bhnid,bhnjd->bhnij', kb, k) * decay, 0.0)
    eye = jnp.eye(c, dtype=f32)
    t_mat = lax.linalg.triangular_solve(eye + m, jnp.broadcast_to(eye, m.shape), left_side=True, lower=True)
    u = jnp.einsum('bhnij,bhnjv->bhniv', t_mat, vb)
    w = jnp.einsum('bhnij,bhnjd->bhnid', t_mat, kb * jnp.exp(gc)[..., None])
    a_intra = jnp.where(incl, jnp.einsum('bhnid,bhnjd->bhnij', q, k) * decay, 0.0)
    q_g = q * jnp.exp(gc)[..., None]
    k_d = k * jnp.exp(gc[..., -1:] - gc)[..., None]
    g_last = jnp.exp(gc[..., -1])

    def step(s, xs):
        w_c, u_c, q_c, k_c, a_c, gl = xs
        v_new = u_c - jnp.einsum('bhcd,bhdv->bhcv', w_c, s)
        o = jnp.einsum('bhcd,bhdv->bhcv', q_c, s) + jnp.einsum('bhij,bhjv->bhiv', a_c, v_new)
        s = s * gl[..., None, None] + jnp.einsum('bhcd,bhcv->bhdv', k_c, v_new)
        return s, o

    xs = tuple(jnp.moveaxis(a, 2, 0) for a in (w, u, q_g, k_d, a_intra, g_last))
    s_fin, o = lax.scan(step, s0.astype(f32), xs)
    o = jnp.moveaxis(o, 0, 2).reshape(b, h, t + pad, dv)[:, :, :t]
    return jnp.moveaxis(o, 1, 2), s_fin.astype(s0.dtype)

def diff_attention(q1, q2, k1, k2, v, q_pos, k_pos, rel_bias, lam):
    b, tq, h, _ = q1.shape
    qb = Q_BLOCK if tq % Q_BLOCK == 0 else tq
    nb = tq // qb
    scale = DH_B ** -0.5

    def to_blocks(a):
        return jnp.moveaxis(a.reshape((b, nb, qb) + a.shape[2:]), 1, 0)

    def block(args):
        q1b, q2b, qp = args
        rel = qp[:, None] - k_pos[None, :]
        bias = jnp.moveaxis(rel_bias[t5_bucket(rel)], -1, 0).astype(jnp.float32)
        visible = rel >= 0

        def probs(qx, kx):
            s = jnp.einsum('bqhd,bkhd->bhqk', qx, kx).astype(jnp.float32) * scale + bias
            return jax.nn.softmax(jnp.where(visible, s, NEG_INF), axis=-1)

        p = probs(q1b, k1) - lam * probs(q2b, k2)
        return jnp.einsum('bhqk,bkhv->bqhv', p.astype(v.dtype), v)

    o = lax.map(block, (to_blocks(q1), to_blocks(q2), q_pos.reshape(nb, qb)))
    return jnp.moveaxis(o, 0, 1).reshape(b, tq, h, v.shape[-1])

def trunk_layer(x, q_pos, k_past, v_past, conv_a_buf, s0, conv_f_buf, li, rel_bias,
                norm_mix, w_in, conv_a, a_log, dt_bias, onorm_a, qnorm_b, knorm_b,
                lam_q1, lam_k1, lam_q2, lam_k2, subln_b, w_branch, w_o,
                norm_ffn, w_up, conv_f, conv_f_b, w_down):
    b, t, _ = x.shape
    f32 = jnp.float32
    h = rmsnorm(x, norm_mix)
    proj = h @ w_in
    qkv_a, z_a, b_a, a_a, q_b, k_b, v_b, g_a, g_b = jnp.split(proj, split_points(), axis=-1)

    qkv_a, conv_a_new = causal_dwconv(qkv_a, conv_a_buf, conv_a)
    qkv_a = jax.nn.silu(qkv_a)
    q_a, k_a, v_a = jnp.split(qkv_a, [H_A * DK_A, 2 * H_A * DK_A], axis=-1)
    q_a = l2norm(q_a.reshape(b, t, H_A, DK_A)) * (DK_A ** -0.5)
    k_a = l2norm(k_a.reshape(b, t, H_A, DK_A))
    v_a = v_a.reshape(b, t, H_A, DV_A)
    beta = jax.nn.sigmoid(b_a.astype(f32))
    g = -jnp.exp(a_log.astype(f32)) * jax.nn.softplus(a_a.astype(f32) + dt_bias.astype(f32))
    o_a, s_new = gated_delta_chunked(q_a, k_a, v_a, beta, g, s0)
    o_a = rmsnorm(o_a.astype(x.dtype), onorm_a) * jax.nn.silu(z_a.reshape(b, t, H_A, DV_A))
    o_a = o_a.reshape(b, t, H_A * DV_A)

    lam_init = 0.8 - 0.6 * math.exp(-0.3 * li)
    q_b = rmsnorm(q_b.reshape(b, t, H_B, 2, DH_B), qnorm_b)
    k_b = rmsnorm(k_b.reshape(b, t, H_B, 2, DH_B), knorm_b)
    v_b = v_b.reshape(b, t, H_B, DV_B)
    k_rows = k_b.reshape(b, t, H_B, 2 * DH_B)
    if k_past is None:
        k_all, v_all = k_rows, v_b
    else:
        k_all = jnp.concatenate([k_past.astype(k_rows.dtype), k_rows], axis=1)
        v_all = jnp.concatenate([v_past.astype(v_b.dtype), v_b], axis=1)
    tk = k_all.shape[1]
    k_all = k_all.reshape(b, tk, H_B, 2, DH_B)
    k_pos = jnp.arange(tk, dtype=jnp.int32)
    lam = (jnp.exp(jnp.sum(lam_q1.astype(f32) * lam_k1.astype(f32)))
           - jnp.exp(jnp.sum(lam_q2.astype(f32) * lam_k2.astype(f32))) + lam_init)
    o_b = diff_attention(q_b[..., 0, :], q_b[..., 1, :], k_all[..., 0, :], k_all[..., 1, :],
                         v_all, q_pos, k_pos, rel_bias, lam)
    o_b = (rmsnorm(o_b, subln_b) * (1.0 - lam_init)).reshape(b, t, H_B * DV_B)

    mixed = jax.nn.sigmoid(g_a) * (o_a @ w_branch[0]) + jax.nn.sigmoid(g_b) * (o_b @ w_branch[1])
    x = x + mixed @ w_o

    hf = rmsnorm(x, norm_ffn)
    u, conv_f_new = causal_dwconv(hf @ w_up, conv_f_buf, conv_f)
    u = u + conv_f_b
    gate, val = jnp.split(u, 2, axis=-1)
    x = x + (jax.nn.silu(gate) * val) @ w_down
    return x, k_rows, v_b, s_new, conv_a_new, conv_f_new

def setup_inputs(seed: int = 0) -> dict:
    key = jax.random.key(seed)
    nxt = iter(list(jax.random.split(key, 40)))
    f32 = jnp.float32

    def nrm(shape, scale):
        return jax.random.normal(next(nxt), shape, f32) * scale

    def gain(shape):
        return 1.0 + nrm(shape, 0.02)

    n_pages = PAST_LEN // PAGE_SIZE
    n_used = DEC_BATCH * n_pages
    n_pool = n_used + n_used // 4
    perm = jax.random.permutation(next(nxt), n_pool)
    page_table = perm[:n_used].reshape(DEC_BATCH, n_pages).astype(jnp.int32)

    x_prompt = nrm((BATCH, SEQ, D_MODEL), 1.0)
    x_sample = nrm((DEC_BATCH, DEC_SEQ, D_MODEL), 1.0)
    cache_k = nrm((DEPTH, n_pool, PAGE_SIZE, H_B, 2 * DH_B), 1.0)
    cache_v = nrm((DEPTH, n_pool, PAGE_SIZE, H_B, DV_B), 1.0)
    state_delta = nrm((DEPTH, DEC_BATCH, H_A, DK_A, DV_A), 0.1)
    state_conv_a = nrm((DEPTH, DEC_BATCH, CONV_A - 1, QKV_A), 1.0)
    state_conv_ffn = nrm((DEPTH, DEC_BATCH, CONV_F - 1, 2 * D_FF), 1.0)

    rel_bias = nrm((NUM_BUCKETS, H_B), 0.5)
    norm_mix = gain((DEPTH, D_MODEL))
    w_in = nrm((DEPTH, D_MODEL, N_IN), D_MODEL ** -0.5)
    conv_a = nrm((DEPTH, CONV_A, QKV_A), CONV_A ** -0.5)
    a_log = jnp.log(jax.random.uniform(next(nxt), (DEPTH, H_A), f32, 1.0, 16.0))
    dt = jnp.exp(jax.random.uniform(next(nxt), (DEPTH, H_A), f32, math.log(0.001), math.log(0.1)))
    dt_bias = dt + jnp.log(-jnp.expm1(-dt))
    onorm_a = gain((DEPTH, DV_A))
    qnorm_b = gain((DEPTH, DH_B))
    knorm_b = gain((DEPTH, DH_B))
    lam_q1 = nrm((DEPTH, DH_B), 0.1)
    lam_k1 = nrm((DEPTH, DH_B), 0.1)
    lam_q2 = nrm((DEPTH, DH_B), 0.1)
    lam_k2 = nrm((DEPTH, DH_B), 0.1)
    subln_b = gain((DEPTH, DV_B))
    w_branch = nrm((DEPTH, 2, BRANCH_W, D_MODEL), BRANCH_W ** -0.5)
    w_o = nrm((DEPTH, D_MODEL, D_MODEL), D_MODEL ** -0.5)
    norm_ffn = gain((DEPTH, D_MODEL))
    w_up = nrm((DEPTH, D_MODEL, 2 * D_FF), D_MODEL ** -0.5)
    conv_f = nrm((DEPTH, CONV_F, 2 * D_FF), CONV_F ** -0.5)
    conv_f_b = nrm((DEPTH, 2 * D_FF), 0.01)
    w_down = nrm((DEPTH, D_FF, D_MODEL), D_FF ** -0.5)
    return {'x_prompt': x_prompt, 'x_sample': x_sample, 'cache_k': cache_k, 'cache_v': cache_v,
            'state_delta': state_delta, 'state_conv_a': state_conv_a, 'state_conv_ffn': state_conv_ffn,
            'page_table': page_table, 'rel_bias': rel_bias, 'norm_mix': norm_mix, 'w_in': w_in,
            'conv_a': conv_a, 'a_log': a_log, 'dt_bias': dt_bias, 'onorm_a': onorm_a,
            'qnorm_b': qnorm_b, 'knorm_b': knorm_b, 'lam_q1': lam_q1, 'lam_k1': lam_k1,
            'lam_q2': lam_q2, 'lam_k2': lam_k2, 'subln_b': subln_b, 'w_branch': w_branch, 'w_o': w_o,
            'norm_ffn': norm_ffn, 'w_up': w_up, 'conv_f': conv_f, 'conv_f_b': conv_f_b, 'w_down': w_down}

def reference(x_prompt, x_sample, cache_k, cache_v, state_delta, state_conv_a, state_conv_ffn,
              page_table, rel_bias, norm_mix, w_in, conv_a, a_log, dt_bias, onorm_a, qnorm_b, knorm_b,
              lam_q1, lam_k1, lam_q2, lam_k2, subln_b, w_branch, w_o, norm_ffn, w_up, conv_f,
              conv_f_b, w_down):
    n_pages = page_table.shape[1]
    pos_prompt = jnp.arange(SEQ, dtype=jnp.int32)
    pos_sample = PAST_LEN + jnp.arange(DEC_SEQ, dtype=jnp.int32)
    xp, xs = x_prompt, x_sample
    kp_l, vp_l, sp_l, cap_l, cfp_l = [], [], [], [], []
    ks_l, vs_l, ss_l, cas_l, cfs_l = [], [], [], [], []
    for li in range(DEPTH):
        weights = (norm_mix[li], w_in[li], conv_a[li], a_log[li], dt_bias[li], onorm_a[li],
                   qnorm_b[li], knorm_b[li], lam_q1[li], lam_k1[li], lam_q2[li], lam_k2[li],
                   subln_b[li], w_branch[li], w_o[li], norm_ffn[li], w_up[li], conv_f[li],
                   conv_f_b[li], w_down[li])
        zero_conv_a = jnp.zeros((BATCH, CONV_A - 1, QKV_A), xp.dtype)
        zero_delta = jnp.zeros((BATCH, H_A, DK_A, DV_A), state_delta.dtype)
        zero_conv_f = jnp.zeros((BATCH, CONV_F - 1, 2 * D_FF), xp.dtype)
        xp, kp, vp, sp, cap, cfp = trunk_layer(xp, pos_prompt, None, None, zero_conv_a, zero_delta,
                                               zero_conv_f, li, rel_bias, *weights)
        k_past = cache_k[li][page_table].reshape(DEC_BATCH, n_pages * PAGE_SIZE, H_B, 2 * DH_B)
        v_past = cache_v[li][page_table].reshape(DEC_BATCH, n_pages * PAGE_SIZE, H_B, DV_B)
        xs, ks, vs, ss, cas, cfs = trunk_layer(xs, pos_sample, k_past, v_past, state_conv_a[li],
                                               state_delta[li], state_conv_ffn[li], li, rel_bias, *weights)
        kp_l.append(kp); vp_l.append(vp); sp_l.append(sp); cap_l.append(cap); cfp_l.append(cfp)
        ks_l.append(ks); vs_l.append(vs); ss_l.append(ss); cas_l.append(cas); cfs_l.append(cfs)
    k_prompt = jnp.stack(kp_l)
    v_prompt = jnp.stack(vp_l)
    delta_prompt = jnp.stack(sp_l)
    conv_a_prompt = jnp.stack(cap_l)
    conv_ffn_prompt = jnp.stack(cfp_l)
    k_sample = jnp.stack(ks_l)
    v_sample = jnp.stack(vs_l)
    delta_sample = jnp.stack(ss_l)
    conv_a_sample = jnp.stack(cas_l)
    conv_ffn_sample = jnp.stack(cfs_l)
    return (xp, xs, k_prompt, v_prompt, delta_prompt, conv_a_prompt, conv_ffn_prompt,
            k_sample, v_sample, delta_sample, conv_a_sample, conv_ffn_sample)


_drawn_inputs = setup_inputs


def setup_inputs(seed=0):
    import zlib

    import numpy as np

    out = dict(_drawn_inputs(seed))
    spreads = {}
    factors = {'onorm_a': 8.0,
     'qnorm_b': 7.066,
     'lam_k1': 5.114,
     'lam_q2': 5.701,
     'lam_k2': 8.0,
     'subln_b': 6.522,
     'norm_ffn': 2.909,
     'conv_f_b': 8.0}
    for name, (base, spread) in spreads.items():
        noise = np.random.default_rng([zlib.crc32(name.encode()), seed]).standard_normal(out[name].shape)
        drawn = base * np.exp(spread * noise) if base else spread * noise
        out[name] = __import__('jax').numpy.asarray(drawn.astype(out[name].dtype))
    for name, factor in factors.items():
        out[name] = (out[name] * factor).astype(out[name].dtype)
    return out
```

```python
import math
from contextlib import ExitStack

import numpy as np

import concourse.bass as bass
from concourse import mybir

F32 = mybir.dt.float32
I32 = mybir.dt.int32
ALU = mybir.AluOpType
ACT = mybir.ActivationFunctionType
AX = mybir.AxisListType

P = 128
D = 1024
KC = D // P
SEQ = 1024
NSEQ, QN = 8, 4
NS = NSEQ * QN
T = SEQ + NS
PT = SEQ // P
NB, BW = 3, T // 3
H = 4
DH = 128
W = H * DH
QKV = 3 * W
CA = QKV // P
TA = 4
DFF = 2816
CF = DFF // P
TF = 3
PAST, PAGE = 256, 128
PAGES = PAST // PAGE
BUCKETS, MAXD = 32, 128
EPS = 1e-6
LAM0 = 0.8 - 0.6 * math.exp(-0.3 * 0)
NEG = -1e30
C_BA = QKV + W
C_Q = C_BA + 2 * H
C_K, C_V = C_Q + W, C_Q + 2 * W
C_GA = C_Q + 3 * W
C_GB = C_GA + D
LEVELS = 7
SLEVELS = 2
MLO, ML = -(PAST + QN - 1), 388
RSQRT_MAGIC = float(0x5F3759DF)
RSQRT_LINKS = 11


def rel_buckets():
    rel = -(MLO + np.arange(ML))
    n = np.maximum(rel, 0)
    half = BUCKETS // 2
    nf = np.maximum(n, 1).astype(np.float32)
    large = half + (np.log(nf / np.float32(half)) / np.float32(math.log(MAXD / half)) * (BUCKETS - half)).astype(np.int32)
    return rel, np.where(n < half, n, np.minimum(large, BUCKETS - 1))


def constants():
    i = np.arange(P)[:, None]
    j = np.arange(P)[None, :]
    blk = (i // QN == j // QN) & (i < NS) & (j < NS)
    parts = {"ident": i == j, "ones": i >= 0 * j, "triu": i <= j, "neglow": -1.0 * (j < i)}
    for b in range(LEVELS):
        low = (i >> (b + 1) == j >> (b + 1)) & (i >> b & 1 == 1) & (j >> b & 1 == 0)
        parts[f"low{b}"], parts[f"up{b}"] = low, low.T
    parts["s_triu"] = (blk & (i <= j))[:, :NS]
    parts["s_same"] = blk[:, :NS]
    parts["s_neglow"] = (-1.0 * (blk & (j < i)))[:, :NS]
    parts["s_seq"] = (i // QN == np.arange(NSEQ)[None, :]) & (i < NS)
    rel, bucket = rel_buckets()
    hot = np.zeros((P, ML), np.float32)
    seen = np.nonzero(rel >= 0)[0]
    hot[bucket[seen], seen] = 8.0
    hot[BUCKETS - 1, seen] -= 8.0
    hot[BUCKETS, rel < 0] = 8.0
    parts["hot"] = hot
    h, m, q = i // 8 % 4, i // 4 % 2, i % 4
    parts["m0"], parts["m1"] = m == 0, m == 1
    parts["spread"] = (j // 8 % 4 == i // QN) & (j % 4 == i % QN) & (i < 4 * QN)
    parts["s_cross"] = np.concatenate(
        [np.where(i // 32 + 4 * g == np.arange(NSEQ)[None, :], 0.0, 8 * NEG) for g in range(2)], 1)
    at, cols, n = {}, [], 0
    for name, a in parts.items():
        a = np.broadcast_to(a, (P, a.shape[1])).astype(np.float32)
        at[name] = (n, n + a.shape[1])
        cols.append(a)
        n += a.shape[1]
    return np.ascontiguousarray(np.concatenate(cols, 1)), at


CONSTS, CONST_AT = constants()


class Links:

    def __init__(self, eng, sem, base=0):
        self.eng, self.sem, self.base, self.n = eng, sem, base, 0

    def __call__(self, ins):
        self.n += 1
        ins.then_inc(self.sem, 1)
        self.eng.wait_ge(self.sem, self.base + self.n)


def loop(eng, n, body):
    body(0, True)
    with eng.Fori(1, n) as i:
        body(i, False)


def at(i, n=1):
    return bass.ds(i, n)


def over(ap, n):
    return ap.unsqueeze(2).to_broadcast([ap.shape[0], ap.shape[1], n])


def repeat(ap, n):
    return ap.unsqueeze(1).to_broadcast([ap.shape[0], n, ap.shape[1]])


def hd(ap, h=H):
    return ap.rearrange("p (h n) -> p h n", h=h)


def rsqrt(dve, link, out, x, work):
    link(dve.tensor_scalar(work.bitcast(I32), x.bitcast(I32), 1, None, ALU.logical_shift_right))
    link(dve.tensor_scalar(out.bitcast(I32), work.bitcast(I32), -1.0, RSQRT_MAGIC, ALU.mult, ALU.add))
    for _ in range(3):
        link(dve.scalar_tensor_tensor(work, out, -0.5, out, ALU.mult, ALU.mult))
        link(dve.tensor_tensor(work, work, x, ALU.mult))
        link(dve.scalar_tensor_tensor(out, work, 1.5, out, ALU.add, ALU.mult))


def hold(eng, sem, value, held):
    eng.wait_ge(sem, value)
    eng.sem_inc(held, 1)


class Core:

    def __init__(self, nc, dram):
        self.nc, self.d, self.sems = nc, dram, []

    def sb(self, ctx, name, shape, dt=F32):
        return ctx.enter_context(self.nc.sbuf_tensor(name, shape, dt))

    def ps(self, ctx, name, banks=1):
        shape = [P, 512] if banks == 1 else [P, banks, 512]
        return ctx.enter_context(self.nc.psum_tensor(name, shape, F32))

    def sem(self, name):
        self.sems.append(self.nc.alloc_semaphore(name=name))
        return self.sems[-1]

    def clear(self):
        self.nc.clear_and_free_semaphores(self.sems)
        self.sems = []
        self.nc.all_engine_barrier()

    def c(self, name, n=P):
        a, b = CONST_AT[name]
        return self.const[0:n, a:b]


def load_stage(k):
    nc, d = k.nc, k.d
    with ExitStack() as ctx:
        sem = lambda n: k.sem(n)
        const_in, x_in, small_in, bias_rows_out, bias_in = (
            sem(n) for n in ("const_in", "x_in", "small_in", "bias_rows_out", "bias_in"))
        table_ready, rows_done, rows_sb, steps, lam_e, b16_done, b16_sb = (
            sem(n) for n in ("table_ready", "rows_done", "rows_sb", "ld_steps", "lam_e", "b16_done", "b16_sb"))
        rel = k.sb(ctx, "rel", [BUCKETS + 1, H])
        relb = k.sb(ctx, "relb", [BUCKETS + 1, H, P])
        lams = k.sb(ctx, "lams", [P, 4, 64])
        prod = k.sb(ctx, "prod", [P, 2, 64])
        dots = k.sb(ctx, "dots", [P, 2])
        rows = k.sb(ctx, "rows", [P, H, ML])
        b16 = k.sb(ctx, "b16", [4 * QN, PAST + QN])
        prow = [k.ps(ctx, f"prow{h}") for h in range(H)]
        p16 = k.ps(ctx, "p16")
        scratch = nc.dram_tensor("bias_rows", (H, P, ML), F32, kind="Internal").ap()
        block = ctx.enter_context(nc.Block())

        @block.sync
        def _(sp):
            sp.dma_start(k.const[:, :], d["consts"]).then_inc(const_in, 16)
            xs = d["x_prompt"].rearrange("b (t p) n -> p (b t) n", p=P)
            sp.dma_start(k.x[:, 0:PT // 2, :], xs[:, 0:PT // 2, :]).then_inc(x_in, 16)
            sp.dma_start(k.x[:, PT // 2:PT, :], xs[:, PT // 2:PT, :]).then_inc(x_in, 16)
            sp.dma_start(k.x[0:NS, PT, :], d["x_sample"].rearrange("b q n -> (b q) n")).then_inc(x_in, 16)
            sp.wait_ge(x_in, 48)

        @block.scalar
        def _(act):
            act.dma_start(rel[0:BUCKETS, :], d["rel_bias"]).then_inc(small_in, 16)
            for n, name in enumerate(("lam_q1", "lam_k1", "lam_q2", "lam_k2")):
                act.dma_start(lams[:, n, :], d[name].partition_broadcast(P).rearrange("p a n -> p (a n)")).then_inc(small_in, 16)
            for buf, name in ((k.qw, "qnorm_b"), (k.kw, "knorm_b"), (k.alog, "a_log"), (k.dtb, "dt_bias")):
                act.dma_start(buf[:, :], d[name].partition_broadcast(P).rearrange("p a n -> p (a n)")).then_inc(small_in, 16)
            with nc.allow_non_contiguous_dma(reason="a few columns"):
                act.dma_start(k.wmix[:, :], d["norm_mix"].rearrange("a (c p) -> p (a c)", p=P)).then_inc(small_in, 16)
                act.dma_start(k.wffn[:, :], d["norm_ffn"].rearrange("a (c p) -> p (a c)", p=P)).then_inc(small_in, 16)
                act.dma_start(k.onorm[:, :], d["onorm_a"].rearrange("a (c p) -> p (a c)", p=P)).then_inc(small_in, 16)
                act.dma_start(k.subln[:, :], d["subln_b"].rearrange("a (c p) -> p (a c)", p=P)).then_inc(small_in, 16)
            act.wait_ge(small_in, 16 * 13)
            act.wait_ge(steps, 4)
            act.activation(dots[:, :], dots[:, :], ACT.Exp).then_inc(lam_e, 1)
            for h in range(H):
                act.wait_ge(rows_done, h + 1)
                act.activation(rows[:, h, :], prow[h][:, 0:ML], ACT.Copy).then_inc(rows_sb, 1)
            for h in range(H):
                act.wait_ge(rows_sb, H)
                act.dma_start(scratch[h], rows[:, h, :]).then_inc(bias_rows_out, 16)
            act.wait_ge(bias_rows_out, 16 * H)
            with nc.allow_non_contiguous_dma(reason="a skewed read"):
                for h in range(H):
                    skew = bass.AP(scratch.tensor, h * P * ML + (-P - MLO), [[ML - 1, P], [1, 2 * P]])
                    act.dma_start(k.bias[:, h, :], skew).then_inc(bias_in, 16)
                for h in range(H):
                    skew = bass.AP(scratch.tensor, h * P * ML + (-PAST - MLO), [[ML - 1, QN], [1, PAST + QN]])
                    act.dma_start(b16[QN * h:QN * h + QN, :], skew).then_inc(bias_in, 16)
            act.wait_ge(bias_in, 16 * 2 * H)
            act.wait_ge(b16_done, 1)
            act.activation(k.sbias[:, :], p16[:, 0:PAST + QN], ACT.Copy).then_inc(b16_sb, 1)

        @block.vector
        def _(dve):
            link = Links(dve, steps)
            link(dve.memset(rel[BUCKETS:BUCKETS + 1, :], NEG))
            dve.wait_ge(small_in, 16 * 13)
            link(dve.tensor_tensor(prod[:, :, :], lams[:, 0:4:2, :], lams[:, 1:4:2, :], ALU.mult))
            link(dve.tensor_reduce(dots[:, :], prod[:, :, :], AX.X, ALU.add))
            link(dve.tensor_copy(relb[:, :, :], over(rel[:, :], P)))
            dve.wait_ge(lam_e, 1)
            link(dve.scalar_tensor_tensor(k.lam[:, :], dots[:, 1:2], -1.0, dots[:, 0:1], ALU.mult, ALU.add))
            link(dve.tensor_scalar(k.lam[:, :], k.lam[:, :], LAM0, None, ALU.add))
            link(dve.tensor_scalar(k.subln[:, :], k.subln[:, :], 1.0 - LAM0, None, ALU.mult))

        @block.tensor
        def _(pe):
            pe.wait_ge(const_in, 16)
            pe.wait_ge(steps, 4)
            for h in range(H):
                pe.matmul(prow[h][:, 0:ML], relb[:, h, :], k.c("hot", BUCKETS + 1), start=True, stop=True).then_inc(rows_done, 1)
            pe.wait_ge(bias_in, 16 * 2 * H)
            pe.matmul(p16[:, 0:PAST + QN], k.c("spread", 4 * QN), b16[:, :], start=True, stop=True).then_inc(b16_done, 1)


def norm_stage(k, name, weight):
    nc = k.nc
    with ExitStack() as ctx:
        sem = lambda n: k.sem(f"{name}_{n}")
        sums_done, steps, scaled, turned, stored = (sem(n) for n in ("sums", "steps", "scaled", "turned", "stored"))
        junk = k.sb(ctx, f"{name}_junk", [P, 2, D])
        ss = k.sb(ctx, f"{name}_ss", [P, PT + 1])
        r = k.sb(ctx, f"{name}_r", [P, PT + 1])
        work = k.sb(ctx, f"{name}_work", [P, PT + 1])
        h = k.sb(ctx, f"{name}_h", [P, 2, D])
        pt = k.ps(ctx, f"{name}_pt", 4)
        block = ctx.enter_context(nc.Block())

        @block.scalar
        def _(act):
            act.wait_ge(steps, 1)
            for t in range(PT + 1):
                n = P if t < PT else NS
                if t >= 2:
                    act.wait_ge(sums_done, t - 1)
                act.activation(junk[0:n, t % 2, :], k.x[0:n, t, :], ACT.Square, accum_out=ss[0:n, t:t + 1]).then_inc(sums_done, 1)

            def tile(t, u, n, first):
                act.wait_ge(steps, 2 + RSQRT_LINKS)
                if not first:
                    act.wait_ge(turned, t - 1)
                act.activation(h[0:n, u, :], k.x[0:n, at(t), :].rearrange("p a n -> p (a n)"), ACT.Copy,
                               scale=r[0:n, at(t)]).then_inc(scaled, 1)

            loop(act, PT // 2, lambda i, first: [tile(2 * i + u, u, P, first) for u in range(2)])
            tile(PT, 0, NS, False)

        @block.vector
        def _(dve):
            link = Links(dve, steps)
            link(dve.memset(ss[:, :], 1.0))
            dve.wait_ge(sums_done, PT + 1)
            link(dve.tensor_scalar(ss[:, :], ss[:, :], 1.0 / D, EPS, ALU.mult, ALU.add))
            rsqrt(dve, link, r[:, :], ss[:, :], work[:, :])

            def tile(t, u, n, first):
                dve.wait_ge(turned, t + 1)
                for half in range(2):
                    c = slice(4 * half, 4 * half + 4)
                    ins = dve.tensor_tensor(k.hT[:, c, at(t * P, n)], hd(pt[:, 2 * u + half, :])[:, :, 0:n],
                                            over(weight[:, c], n), ALU.mult)
                ins.then_inc(stored, 1)

            loop(dve, PT // 2, lambda i, first: [tile(2 * i + u, u, P, first) for u in range(2)])
            tile(PT, 0, NS, False)

        @block.tensor
        def _(pe):
            def tile(t, u, n, first):
                pe.wait_ge(scaled, t + 1)
                if not first:
                    pe.wait_ge(stored, t - 1)
                for c in range(KC):
                    ins = pe.transpose(pt[:, 2 * u + c // 4, c % 4 * P:c % 4 * P + n], h[0:n, u, c * P:c * P + P],
                                       k.c("ident", n)[:, 0:n])
                ins.then_inc(turned, 1)

            loop(pe, PT // 2, lambda i, first: [tile(2 * i + u, u, P, first) for u in range(2)])
            tile(PT, 0, NS, False)


def dense_cols(pe, ps, wb, rhs, kc, done):
    for b in range(NB):
        for c in range(kc):
            ins = pe.matmul(ps[:, b, 0:BW], wb[:, c, :], rhs[:, c, b * BW:(b + 1) * BW], start=(c == 0), stop=(c == kc - 1))
    ins.then_inc(done, 1)


def conv_proj_stage(k):
    nc, d = k.nc, k.d
    R = TA - 1
    RAW = R + SEQ + NSEQ * (R + QN)
    OUT = RAW - R
    NH = NSEQ * R
    LAST = R + NSEQ * R
    with ExitStack() as ctx:
        sem = lambda n: k.sem(f"cv_{n}")
        w_in_sem = [sem(f"w{u}") for u in range(2)]
        proj_done = [sem(f"proj{u}") for u in range(2)]
        evac_done = [sem(f"evac{u}") for u in range(2)]
        hist_set = [sem(f"hist{u}") for u in range(2)]
        conv_done = [sem(f"conv{u}") for u in range(2)]
        act_done = [sem(f"silu{u}") for u in range(2)]
        saved = sem("saved")
        taps_in, taps_turned, taps_sb, zeroed, last_turned, last_sb, last_out, chain, pool_held = (
            sem(n) for n in ("taps_in", "taps_turned", "taps_sb", "zeroed", "last_turned", "last_sb", "last_out", "chain", "pool_held"))
        wb = [k.sb(ctx, f"cv_w{u}", [P, KC, P]) for u in range(2)]
        raw = [k.sb(ctx, f"cv_raw{u}", [P, RAW]) for u in range(2)]
        acc = [k.sb(ctx, f"cv_acc{u}", [P, RAW]) for u in range(2)]
        nat = k.sb(ctx, "cv_nat", [NH + TA, QKV])
        taps = k.sb(ctx, "cv_taps", [P, CA, NH + TA])
        last = k.sb(ctx, "cv_last", [P, CA, LAST])
        lastn = k.sb(ctx, "cv_lastn", [LAST, QKV])
        ps = [k.ps(ctx, f"cv_ps{u}", 3) for u in range(2)]
        pt = k.ps(ctx, "cv_pt", 2)
        samp = [raw[u][:, R + SEQ:RAW].rearrange("p (s c) -> p s c", s=NSEQ) for u in range(2)]
        samp_out = [acc[u][:, R + SEQ:RAW].rearrange("p (s c) -> p s c", s=NSEQ) for u in range(2)]
        w_cols = d["w_in"].rearrange("a (c p) n -> p (a c) n", p=P)
        block = ctx.enter_context(nc.Block())

        @block.sync
        def _(sp):
            sp.dma_start(nat[0:NH, :], d["state_conv_a"].rearrange("a s r n -> (a s r) n")).then_inc(taps_in, 16)
            sp.dma_start(nat[NH:NH + TA, :], d["conv_a"].rearrange("a w n -> (a w) n")).then_inc(taps_in, 16)

            def load(i, first):
                for u in range(2):
                    if not first:
                        sp.wait_ge(proj_done[u], i)
                    sp.dma_start(wb[u][:, :, :], w_cols[:, :, at((2 * i + u) * P, P)]).then_inc(w_in_sem[u], 16)

            loop(sp, (CA + H) // 2, load)
            sp.wait_ge(last_sb, 3)
            sp.dma_start(d["conv_a_prompt"].rearrange("a b r n -> (a b r) n"), lastn[0:R, :]).then_inc(last_out, 16)
            sp.dma_start(d["conv_a_sample"].rearrange("a s r n -> (a s r) n"), lastn[R:LAST, :]).then_inc(last_out, 16)
            sp.wait_ge(last_out, 32)

        @block.tensor
        def _(pe):
            pe.wait_ge(taps_in, 32)
            for c in range(CA):
                if c >= 2:
                    pe.wait_ge(taps_sb, c - 1)
                pe.transpose(pt[:, c % 2, 0:NH + TA], nat[:, c * P:(c + 1) * P], k.c("ident", NH + TA)[:, 0:NH + TA]).then_inc(taps_turned, 1)

            def chunks(i, first):
                for u in range(2):
                    pe.wait_ge(w_in_sem[u], 16 * i + 16)
                    if not first:
                        pe.wait_ge(evac_done[u], i)
                    dense_cols(pe, ps[u], wb[u], k.hT, KC, proj_done[u])

            loop(pe, (CA + H) // 2, chunks)
            pe.wait_ge(saved, 2 * CA)
            for c in range(CA):
                if c >= 8:
                    pe.wait_ge(last_sb, 1)
                ins = pe.transpose(pt[0:LAST, c // 4 % 2, c % 4 * P:c % 4 * P + P], last[:, c, :], k.c("ident"))
                if c % 4 == 3:
                    ins.then_inc(last_turned, 1)

        @block.scalar
        def _(act):
            def conv(i, first):
                for u in range(2):
                    act.wait_ge(proj_done[u], i + 1)
                    if not first:
                        act.wait_ge(conv_done[u], i)
                        act.wait_ge(saved, 2 * (2 * i + u - 1))
                    for b in range(NB):
                        lo, hi = b * BW, min(SEQ, (b + 1) * BW)
                        act.activation(raw[u][:, R + lo:R + hi], ps[u][:, b, 0:hi - lo], ACT.Copy)
                    act.activation(samp[u][:, :, R:R + QN], ps[u][:, NB - 1, BW - NS:BW].rearrange("p (s c) -> p s c", s=NSEQ),
                                   ACT.Copy).then_inc(evac_done[u], 1)
                    act.wait_ge(conv_done[u], i + 1)
                    c = 2 * i + u
                    act.activation(k.qkvT[:, at(c), 0:SEQ].rearrange("p a n -> p (a n)"), acc[u][:, 0:SEQ], ACT.Silu)
                    act.activation(k.qkvT[:, at(c), SEQ:T].rearrange("p a (s c) -> p (a s) c", s=NSEQ),
                                   samp_out[u][:, :, 0:QN], ACT.Silu).then_inc(act_done[u], 1)

            loop(act, CA // 2, conv)

            def z(j):
                for u in range(2):
                    i = j + CA // 2
                    act.wait_ge(proj_done[u], i + 1)
                    for b in range(NB):
                        ins = act.activation(k.zT[:, at(2 * j + u), b * BW:(b + 1) * BW].rearrange("p a n -> p (a n)"),
                                             ps[u][:, b, 0:BW], ACT.Silu)
                    ins.then_inc(evac_done[u], 1)

            with act.Fori(0, H // 2) as j:
                z(j)

        @block.gpsimd
        def _(pool):
            def save(i, first):
                for u in range(2):
                    hold(pool, evac_done[u], i + 1, pool_held)
                    c = 2 * i + u
                    pool.tensor_copy(last[:, at(c), 0:R].rearrange("p a n -> p (a n)"), raw[u][:, SEQ:SEQ + R]).then_inc(saved, 1)
                    pool.tensor_copy(last[:, at(c), R:LAST].rearrange("p a (s c) -> p (a s) c", s=NSEQ),
                                     samp[u][:, :, QN:QN + R]).then_inc(saved, 1)

            loop(pool, CA // 2, save)

        @block.vector
        def _(dve):
            for u in range(2):
                dve.memset(raw[u][:, 0:R], 0.0).then_inc(zeroed, 1)
            for c in range(CA):
                dve.wait_ge(taps_turned, c + 1)
                dve.tensor_copy(taps[:, c, :], pt[:, c % 2, 0:NH + TA]).then_inc(taps_sb, 1)
            dve.wait_ge(taps_sb, CA)
            dve.wait_ge(zeroed, 2)

            def conv(i, first):
                link = Links(dve, chain, 2 * (TA + 1) * i)
                for u in range(2):
                    c = 2 * i + u
                    dve.wait_ge(evac_done[u], i + 1)
                    if not first:
                        dve.wait_ge(act_done[u], i)
                    link(dve.tensor_copy(samp[u][:, :, 0:R], taps[:, at(c), 0:NH].rearrange("p a (s r) -> p (a s) r", s=NSEQ)))
                    link(dve.tensor_scalar(acc[u][:, 0:OUT], raw[u][:, 0:OUT], taps[:, at(c), NH:NH + 1].rearrange("p a n -> p (a n)"), None, ALU.mult))
                    for w in range(1, TA):
                        ins = dve.scalar_tensor_tensor(acc[u][:, 0:OUT], raw[u][:, w:w + OUT],
                                                       taps[:, at(c), NH + w:NH + w + 1].rearrange("p a n -> p (a n)"),
                                                       acc[u][:, 0:OUT], ALU.mult, ALU.add)
                        link(ins)
                    dve.sem_inc(conv_done[u], 1)

            loop(dve, CA // 2, conv)
            for g in range(CA // 4):
                dve.wait_ge(last_turned, g + 1)
                dve.tensor_copy(lastn[:, g * W:(g + 1) * W], pt[0:LAST, g % 2, :]).then_inc(last_sb, 1)


def gates_stage(k):
    nc, d = k.nc, k.d
    with ExitStack() as ctx:
        sem = lambda n: k.sem(f"gt_{n}")
        w_loaded, proj_done, steps, acts = (sem(n) for n in ("w_loaded", "proj", "steps", "acts"))
        wb = k.sb(ctx, "gt_w", [P, KC, 2 * H])
        ba = k.sb(ctx, "gt_ba", [P, PT + 1, 2 * H])
        th = k.sb(ctx, "gt_th", [P, PT + 1, H])
        aa = k.sb(ctx, "gt_aa", [P, PT + 1, H])
        mod = k.sb(ctx, "gt_mod", [P, PT + 1, H])
        ps = k.ps(ctx, "gt_ps")
        psv = ps[:, 0:(PT + 1) * 2 * H].rearrange("p (t n) -> p t n", t=PT + 1)
        block = ctx.enter_context(nc.Block())

        @block.sync
        def _(sp):
            sp.dma_start(wb[:, :, :], d["w_in"].rearrange("a (c p) n -> p (a c) n", p=P)[:, :, C_BA:C_BA + 2 * H]).then_inc(w_loaded, 16)

        @block.tensor
        def _(pe):
            pe.wait_ge(w_loaded, 16)
            for t in range(PT + 1):
                n = P if t < PT else NS
                for c in range(KC):
                    ins = pe.matmul(psv[0:n, t, :], k.hT[:, c, t * P:t * P + n], wb[:, c, :], start=(c == 0), stop=(c == KC - 1))
            ins.then_inc(proj_done, 1)

        @block.scalar
        def _(act):
            act.wait_ge(steps, 3)
            act.activation(th[:, :, :], ba[:, :, 0:H], ACT.Tanh, scale=0.5).then_inc(acts, 1)
            act.activation(k.alog[:, :], k.alog[:, :], ACT.Exp).then_inc(acts, 1)
            act.wait_ge(steps, 6)
            act.activation(mod[:, :, :], mod[:, :, :], ACT.Exp, scale=-1.0).then_inc(acts, 1)
            act.wait_ge(acts, 3)
            act.activation(mod[:, :, :], mod[:, :, :], ACT.Ln, bias=1.0).then_inc(acts, 1)

        @block.vector
        def _(dve):
            link = Links(dve, steps)
            link(dve.memset(ba[:, :, :], 0.0))
            dve.wait_ge(proj_done, 1)
            link(dve.tensor_copy(ba[:, 0:PT, :], psv[:, 0:PT, :]))
            link(dve.tensor_copy(ba[0:NS, PT, :], psv[0:NS, PT, :]))
            link(dve.tensor_tensor(aa[:, :, :], ba[:, :, H:2 * H], repeat(k.dtb[:, :], PT + 1), ALU.add))
            link(dve.tensor_scalar(mod[:, :, :], aa[:, :, :], -1.0, None, ALU.mult))
            link(dve.tensor_tensor(mod[:, :, :], mod[:, :, :], aa[:, :, :], ALU.max))
            dve.wait_ge(acts, 4)
            link(dve.tensor_scalar(k.beta[:, :, :], th[:, :, :], 0.5, 0.5, ALU.mult, ALU.add))
            link(dve.scalar_tensor_tensor(mod[:, :, :], aa[:, :, :], 0.0, mod[:, :, :], ALU.max, ALU.add))
            link(dve.tensor_tensor(mod[:, :, :], mod[:, :, :], repeat(k.alog[:, :], PT + 1), ALU.mult))
            link(dve.tensor_scalar(k.g[:, :, :], mod[:, :, :], -1.0, None, ALU.mult))


def delta_stage(k, sample):
    nc, d = k.nc, k.d
    pre = "ds" if sample else "dp"
    n = NS if sample else P
    levels = SLEVELS if sample else LEVELS
    steps = 1 if sample else PT
    HN = H * n
    tri, neglow = ("s_triu", "s_neglow") if sample else ("triu", "neglow")
    tot = "s_same" if sample else "ones"
    with ExitStack() as ctx:
        sem = lambda s: k.sem(f"{pre}_{s}")
        (staged, gb_staged, identity_set, raw_turned, sums_done, gp_ready, row_done, gc_done, negd_ready, kdx_ready, exps_done,
         masks_done, qk_scaled, kv_scaled, qk_turned, qkT_ready, qg_ready, kk_done, m_ready, a_ready, x_done,
         xs_ready, zu_done, zl_done, level_done, w_done, w_ready, v_done, v_ready, o_done, su_done, s_ready,
         osum_done, o_scaled, o_turned, out_ready, chain, pchain, achain, upd_done, state_in, state_out, held, pool_held) = (sem(s) for s in (
             "staged", "gb_staged", "identity_set", "raw_turned", "sums", "gp", "row", "gc", "negd", "kdx", "exps", "masks",
             "qk_scaled", "kv_scaled", "qk_turned", "qkT", "qg", "kk", "m", "a", "x", "xs", "zu", "zl", "level",
             "w", "w_ready", "v", "v_ready", "o", "su", "s", "osum", "o_scaled", "o_turned", "out", "chain",
             "pchain", "achain", "upd", "state_in", "state_out", "held", "pool_held"))
        sb = lambda s, shape: k.sb(ctx, f"{pre}_{s}", shape)
        stage = sb("stage", [P, CA, n])
        gb = sb("gb", [n, 2 * H])
        gp = sb("gp", [n, HN])
        gcs = sb("gcs", [n, 2 * H])
        kdx, eg, ekd, nbe = (sb(s, [n, H]) for s in ("kdx", "eg", "ekd", "nbe"))
        negd, es, esl, esu = (sb(s, [n, HN]) for s in ("negd", "es", "esl", "esu"))
        er = sb("er", [P, HN])
        ss, r, work = (sb(s, [n, 2 * H]) for s in ("ss", "r", "work"))
        junk = sb("junk", [P, 2, P])
        qn, kn, vb, kbg, kd = (sb(s, [n, W]) for s in ("qn", "kn", "vb", "kbg", "kd"))
        qT, kT, qgT, wT = (sb(s, [P, HN]) for s in ("qT", "kT", "qgT", "wT"))
        m, aT, U, L, xs = (sb(s, [n, HN]) for s in ("m", "aT", "U", "L", "xs"))
        vn = sb("vn", [n, W])
        B = [k.ps(ctx, f"{pre}_b{i}") for i in range(8)]
        S = sb("S", [P, NSEQ * H if sample else H, DH])
        egl = sb("egl", [P, NSEQ * H if sample else H])
        if sample:
            gm = sb("gm", [n, NSEQ, H])
            uT, vnT, oT, sq = (sb(s, [P, HN]) for s in ("uT", "vnT", "oT", "sq"))
            rT, workT = (sb(s, [P, HN]) for s in ("rT", "workT"))
            vm = k.x[0:n, 0:H, :]
        else:
            on = sb("on", [n, W])
            so, ro, worko = (sb(s, [n, H]) for s in ("so", "ro", "worko"))
        ident = k.c("ident")
        block = ctx.enter_context(nc.Block())

        def tiles(eng, body):
            if sample:
                body(PT, 0, True)
            else:
                body(0, 0, True)
                with eng.Fori(1, steps) as t:
                    body(t, t, False)

        def cols(t):
            return at(t * P, n)

        @block.sync
        def _(sp):
            if sample:
                sp.dma_start(S[:, :, :], d["state_delta"].rearrange("a s h p n -> p (a s h) n")).then_inc(state_in, 16)
                sp.wait_ge(s_ready, 1)
                sp.dma_start(d["delta_sample"].rearrange("a s h p n -> p (a s h) n"), S[:, :, :]).then_inc(state_out, 16)
            else:
                sp.wait_ge(s_ready, steps)
                sp.dma_start(d["delta_prompt"].rearrange("a b h p n -> p (a b h) n"), S[:, :, :]).then_inc(state_out, 16)
            sp.wait_ge(state_out, 16)

        @block.gpsimd
        def _(pool):
            def tile(t, i, first):
                if not first:
                    hold(pool, raw_turned, i, pool_held)
                pool.tensor_copy(stage[:, :, :], k.qkvT[:, :, cols(t)]).then_inc(staged, 1)
                if not first:
                    pool.wait_ge(kv_scaled, i)
                    hold(pool, gc_done, i, pool_held)
                pool.tensor_copy(gb[:, 0:H], k.g[0:n, at(t), :].rearrange("p a n -> p (a n)")).then_inc(gb_staged, 1)
                pool.tensor_copy(gb[:, H:2 * H], k.beta[0:n, at(t), :].rearrange("p a n -> p (a n)")).then_inc(gb_staged, 1)
                if not first:
                    hold(pool, v_done, i, pool_held)
                for buf in (U, L):
                    pool.tensor_copy(hd(buf[:, :]), repeat(ident[0:n, 0:n], H)).then_inc(identity_set, 1)
                pool.wait_ge(exps_done, i + 1)
                link = Links(pool, pchain, 3 * i)
                if not first:
                    pool.wait_ge(m_ready, i)
                link(pool.tensor_tensor(hd(esl[:, :]), hd(es[:, :]), repeat(k.c(neglow, n), H), ALU.mult))
                link(pool.tensor_tensor(hd(esl[:, :]), hd(esl[:, :]), over(gb[:, H:2 * H], n), ALU.mult))
                if not first:
                    pool.wait_ge(a_ready, i)
                link(pool.tensor_tensor(hd(esu[:, :]), hd(es[:, :]), repeat(k.c(tri, n), H), ALU.mult))
                pool.sem_inc(masks_done, 1)
                pool.wait_ge(qkT_ready, i + 1)
                if not first:
                    pool.wait_ge(o_done, i)
                pool.tensor_tensor(qgT[:, :], qT[:, :], er[:, :], ALU.mult).then_inc(qg_ready, 1)

            tiles(pool, tile)

        @block.tensor
        def _(pe):
            if sample:
                pe.wait_ge(state_in, 16)

            def tile(t, i, first):
                pe.wait_ge(staged, i + 1)
                if not first:
                    pe.wait_ge(level_done, (2 * levels - 1) * i)
                    pe.wait_ge(v_ready, i)
                    pe.wait_ge(out_ready, i)
                    pe.wait_ge(s_ready, i)
                for c in range(CA):
                    ins = pe.transpose(B[c // H][0:n, c % H * P:c % H * P + P], stage[:, c, :], ident)
                ins.then_inc(raw_turned, 1)
                pe.wait_ge(gp_ready, i + 1)
                pe.matmul(B[3][:, 0:HN], k.c("ones", n), gp[:, :], start=True, stop=True).then_inc(row_done, 1)
                pe.matmul(B[4][0:n, 0:H], k.c(tri, n)[:, 0:n], gb[:, 0:H], start=True, stop=True)
                ins = pe.matmul(B[4][0:n, H:2 * H], k.c(tot, n)[:, 0:n], gb[:, 0:H], start=True, stop=True)
                if sample:
                    ins = pe.matmul(B[4][:, 2 * H:2 * H + NSEQ * H], k.c("ones", n), gm[:, :, :].rearrange("p s h -> p (s h)"), start=True, stop=True)
                ins.then_inc(gc_done, 1)
                pe.wait_ge(qk_scaled, i + 1)
                for h in range(H):
                    pe.transpose(B[5][:, h * n:h * n + n], qn[:, h * P:h * P + P], ident[0:n, 0:n])
                for h in range(H):
                    ins = pe.transpose(B[6][:, h * n:h * n + n], kn[:, h * P:h * P + P], ident[0:n, 0:n])
                ins.then_inc(qk_turned, 1)
                pe.wait_ge(qkT_ready, i + 1)
                for h in range(H):
                    s = slice(h * n, h * n + n)
                    pe.matmul(B[0][0:n, s], kT[:, s], kT[:, s], start=True, stop=True)
                for h in range(H):
                    s = slice(h * n, h * n + n)
                    ins = pe.matmul(B[1][0:n, s], kT[:, s], qT[:, s], start=True, stop=True)
                ins.then_inc(kk_done, 1)
                pe.wait_ge(m_ready, i + 1)
                pe.wait_ge(kv_scaled, i + 1)
                for l in range(levels):
                    if l:
                        pe.wait_ge(level_done, (2 * levels - 1) * i + 2 * l)
                    if l == 1:
                        pe.wait_ge(a_ready, i + 1)
                    for h in range(H):
                        s = slice(h * n, h * n + n)
                        ins = pe.matmul(B[2][0:n, s], m[:, s], U[:, s] if l else ident[0:n, 0:n], start=True, stop=True)
                    ins.then_inc(x_done, 1)
                    if l:
                        pe.wait_ge(xs_ready, (levels - 1) * i + l)
                        for h in range(H):
                            s = slice(h * n, h * n + n)
                            ins = pe.matmul(B[0][0:n, s], L[:, s], xs[:, s], start=True, stop=True)
                        ins.then_inc(zu_done, 1)
                        if l < levels - 1:
                            for h in range(H):
                                s = slice(h * n, h * n + n)
                                ins = pe.matmul(B[1][0:n, s], xs[:, s], L[:, s], start=True, stop=True)
                            ins.then_inc(zl_done, 1)
                pe.wait_ge(level_done, (2 * levels - 1) * (i + 1))
                for h in range(H):
                    ins = pe.matmul(B[3][:, h * n:h * n + n], kbg[:, h * P:h * P + P], U[:, h * n:h * n + n], start=True, stop=True)
                ins.then_inc(w_done, 1)
                if not sample:
                    pe.wait_ge(w_ready, i + 1)
                    if not first:
                        pe.wait_ge(s_ready, i)
                    else:
                        pe.wait_ge(chain, 1)
                    for h in range(H):
                        s = slice(h * P, h * P + P)
                        pe.matmul(B[4][:, s], U[:, s], vb[:, s], start=True, stop=False)
                        ins = pe.matmul(B[4][:, s], wT[:, s], S[:, h, :], start=False, stop=True)
                    ins.then_inc(v_done, 1)
                    pe.wait_ge(v_ready, i + 1)
                    pe.wait_ge(qg_ready, i + 1)
                    for h in range(H):
                        s = slice(h * P, h * P + P)
                        pe.matmul(B[5][:, s], qgT[:, s], S[:, h, :], start=True, stop=False)
                        ins = pe.matmul(B[5][:, s], aT[:, s], vn[:, s], start=False, stop=True)
                    ins.then_inc(o_done, 1)
                    for h in range(H):
                        s = slice(h * P, h * P + P)
                        ins = pe.matmul(B[6][:, s], kd[:, s], vn[:, s], start=True, stop=True)
                    ins.then_inc(su_done, 1)
                    pe.wait_ge(o_scaled, i + 1)
                    for h in range(H):
                        s = slice(h * P, h * P + P)
                        ins = pe.transpose(B[7][:, s], on[:, s], ident)
                    ins.then_inc(o_turned, 1)
                else:
                    for h in range(H):
                        pe.matmul(B[7][:, h * n:h * n + n], vb[:, h * P:h * P + P], U[:, h * n:h * n + n], start=True, stop=True)
                    pe.wait_ge(w_ready, 1)
                    pe.wait_ge(qg_ready, 1)
                    for h in range(H):
                        for s in range(NSEQ):
                            c = h * n + s * QN
                            pe.matmul(B[2][:, c:c + QN], S[:, s * H + h, :], wT[:, c:c + QN], start=True, stop=True)
                            ins = pe.matmul(B[2][:, HN + c:HN + c + QN], S[:, s * H + h, :], qgT[:, c:c + QN], start=True, stop=True)
                    ins.then_inc(v_done, 1)
                    pe.wait_ge(v_ready, 1)
                    for h in range(H):
                        ins = pe.transpose(B[3][0:n, h * P:h * P + P], vnT[:, h * n:h * n + n], ident)
                    ins.then_inc(x_done, 1)
                    pe.wait_ge(v_ready, 2)
                    for h in range(H):
                        ins = pe.matmul(B[7][:, h * n:h * n + n], vn[:, h * P:h * P + P], aT[:, h * n:h * n + n], start=True, stop=True)
                    ins.then_inc(o_done, 1)
                    pe.wait_ge(o_scaled, 1)
                    pe.matmul(B[4][:, 0:HN], k.c("ones"), sq[:, :], start=True, stop=True).then_inc(o_turned, 1)
                    pe.wait_ge(v_ready, 3)
                    for h in range(H):
                        for half in range(2):
                            u = 2 * h + half
                            if u >= 2:
                                pe.wait_ge(upd_done, u - 1)
                            pe.matmul(B[5 + half][:, :], kd[:, h * P:h * P + P], vm[:, h, half * 512:half * 512 + 512],
                                      start=True, stop=True).then_inc(su_done, 1)

            tiles(pe, tile)

        @block.scalar
        def _(act):
            def tile(t, i, first):
                link = Links(act, achain, (2 * H + (0 if sample else H)) * i)
                act.wait_ge(raw_turned, i + 1)
                if not first:
                    act.wait_ge(kv_scaled, i)
                for h in range(2 * H):
                    link(act.activation(junk[0:n, 0, :], B[h // H][0:n, h % H * P:h % H * P + P], ACT.Square, accum_out=ss[:, h:h + 1]))
                act.sem_inc(sums_done, 1)
                act.wait_ge(negd_ready, i + 1)
                if not first:
                    act.wait_ge(s_ready, i)
                act.activation(er[:, :], B[3][:, 0:HN], ACT.Exp)
                act.activation(eg[:, :], B[4][0:n, 0:H], ACT.Exp)
                if sample:
                    act.activation(egl[:, :], B[4][:, 2 * H:2 * H + NSEQ * H], ACT.Exp)
                else:
                    act.activation(egl[:, :], B[4][:, H:2 * H], ACT.Exp)
                if not first:
                    act.wait_ge(masks_done, i)
                act.activation(es[:, :], negd[:, :], ACT.Exp)
                act.wait_ge(kdx_ready, i + 1)
                act.activation(ekd[:, :], kdx[:, :], ACT.Exp).then_inc(exps_done, 1)
                act.wait_ge(qk_turned, i + 1)
                act.activation(qT[:, :], B[5][:, 0:HN], ACT.Copy)
                act.activation(kT[:, :], B[6][:, 0:HN], ACT.Copy).then_inc(qkT_ready, 1)
                for l in range(1, levels):
                    act.wait_ge(x_done, levels * i + l + 1)
                    if l >= 2:
                        act.wait_ge(zl_done, (levels - 2) * i + l - 1)
                    act.activation(xs[:, :], B[2][0:n, 0:HN], ACT.Copy).then_inc(xs_ready, 1)
                act.wait_ge(w_done, i + 1)
                act.activation(wT[:, :], B[3][:, 0:HN], ACT.Copy).then_inc(w_ready, 1)
                if not sample:
                    act.wait_ge(v_done, i + 1)
                    act.activation(vn[:, :], B[4][:, :], ACT.Copy).then_inc(v_ready, 1)
                    act.wait_ge(o_done, i + 1)
                    for h in range(H):
                        link(act.activation(junk[:, 0, :], B[5][:, h * P:h * P + P], ACT.Square, accum_out=so[:, h:h + 1]))
                    act.sem_inc(osum_done, 1)

            tiles(act, tile)

        @block.vector
        def _(dve):
            pr = 0 if sample else 1
            if not sample:
                dve.memset(S[:, :, :], 0.0).then_inc(chain, 1)
            per_tile = [0]

            def tile(t, i, first):
                link = Links(dve, chain, pr + per_tile[0] * i)
                dve.wait_ge(gb_staged, 2 * i + 2)
                dve.tensor_tensor(hd(gp[:, :]), repeat(k.c(tri, n)[:, 0:n], H), over(gb[:, 0:H], n), ALU.mult)
                if sample:
                    dve.tensor_tensor(gm[:, :, :], over(k.c("s_seq", n), H), repeat(gb[:, 0:H], NSEQ), ALU.mult).then_inc(gp_ready, 1)
                else:
                    dve.tensor_scalar(nbe[:, :], gb[:, H:2 * H], -1.0, None, ALU.mult).then_inc(gp_ready, 1)
                dve.wait_ge(gc_done, i + 1)
                link(dve.tensor_copy(gcs[:, :], B[4][0:n, 0:2 * H]))
                link(dve.tensor_tensor(hd(negd[:, :]), hd(B[3][0:n, 0:HN]), over(gcs[:, 0:H], n), ALU.subtract))
                link(dve.scalar_tensor_tensor(negd[:, :], negd[:, :], -1.0, negd[:, :], ALU.mult, ALU.min))
                dve.sem_inc(negd_ready, 1)
                link(dve.tensor_tensor(kdx[:, :], gcs[:, H:2 * H], gcs[:, 0:H], ALU.subtract))
                dve.sem_inc(kdx_ready, 1)
                dve.wait_ge(sums_done, i + 1)
                link(dve.tensor_scalar(ss[:, :], ss[:, :], EPS, None, ALU.add))
                rsqrt(dve, link, r[:, :], ss[:, :], work[:, :])
                link(dve.tensor_scalar(r[:, 0:H], r[:, 0:H], DH ** -0.5, None, ALU.mult))
                link(dve.tensor_tensor(hd(qn[:, :]), hd(B[0][0:n, :]), over(r[:, 0:H], P), ALU.mult))
                link(dve.tensor_tensor(hd(kn[:, :]), hd(B[1][0:n, :]), over(r[:, H:2 * H], P), ALU.mult))
                dve.sem_inc(qk_scaled, 1)
                link(dve.tensor_tensor(hd(vb[:, :]), hd(B[2][0:n, :]), over(gb[:, H:2 * H], P), ALU.mult))
                dve.wait_ge(exps_done, i + 1)
                link(dve.scalar_tensor_tensor(nbe[:, :], gb[:, H:2 * H], -1.0, eg[:, :], ALU.mult, ALU.mult))
                link(dve.tensor_tensor(hd(kbg[:, :]), hd(kn[:, :]), over(nbe[:, :], P), ALU.mult))
                link(dve.tensor_tensor(hd(kd[:, :]), hd(kn[:, :]), over(ekd[:, :], P), ALU.mult))
                dve.sem_inc(kv_scaled, 1)
                dve.wait_ge(kk_done, i + 1)
                dve.wait_ge(masks_done, i + 1)
                dve.tensor_tensor(m[:, :], B[0][0:n, 0:HN], esl[:, :], ALU.mult).then_inc(m_ready, 1)
                dve.tensor_tensor(aT[:, :], B[1][0:n, 0:HN], esu[:, :], ALU.mult).then_inc(a_ready, 1)
                dve.wait_ge(m_ready, i + 1)
                dve.wait_ge(identity_set, 2 * i + 2)
                for l in range(levels):
                    up = repeat(k.c(f"up{l}", n)[:, 0:n].bitcast(I32), H)
                    low = repeat(k.c(f"low{l}", n)[:, 0:n].bitcast(I32), H)
                    if l == 0:
                        hold(dve, x_done, levels * i + 1, held)
                        dve.copy_predicated(hd(U[:, :]), up, hd(B[2][0:n, 0:HN])).then_inc(level_done, 1)
                        dve.copy_predicated(hd(L[:, :]), low, hd(m[:, :])).then_inc(level_done, 1)
                    else:
                        dve.wait_ge(level_done, (2 * levels - 1) * i + 2 * l)
                        hold(dve, zu_done, (levels - 1) * i + l, held)
                        dve.copy_predicated(hd(U[:, :]), up, hd(B[0][0:n, 0:HN])).then_inc(level_done, 1)
                        if l < levels - 1:
                            hold(dve, zl_done, (levels - 2) * i + l, held)
                            dve.copy_predicated(hd(L[:, :]), low, hd(B[1][0:n, 0:HN])).then_inc(level_done, 1)
                if not sample:
                    dve.wait_ge(o_done, i + 1)
                    link(dve.tensor_tensor(S[:, :, :], S[:, :, :], over(egl[:, :], DH), ALU.mult))
                    dve.wait_ge(su_done, i + 1)
                    link(dve.tensor_tensor(S[:, :, :], S[:, :, :], hd(B[6][:, :]), ALU.add))
                    dve.sem_inc(s_ready, 1)
                    dve.wait_ge(osum_done, i + 1)
                    link(dve.tensor_scalar(so[:, :], so[:, :], 1.0 / DH, EPS, ALU.mult, ALU.add))
                    rsqrt(dve, link, ro[:, :], so[:, :], worko[:, :])
                    link(dve.tensor_tensor(hd(on[:, :]), hd(B[5][:, :]), over(ro[:, :], P), ALU.mult))
                    dve.sem_inc(o_scaled, 1)
                    dve.wait_ge(o_turned, i + 1)
                    link(dve.tensor_scalar(on[:, :], B[7][:, :], k.onorm[:, 0:1], None, ALU.mult))
                    z = k.zT[:, :, cols(t)]
                    link(dve.tensor_tensor(z, z, hd(on[:, :]), ALU.mult))
                    dve.sem_inc(out_ready, 1)
                    per_tile[0] = link.n
                    return
                dve.wait_ge(v_done, 1)
                link(dve.tensor_copy(uT[:, :], B[7][:, 0:HN]))
                dve.tensor_tensor(vnT[:, :], uT[:, :], B[2][:, 0:HN], ALU.add).then_inc(v_ready, 1)
                dve.wait_ge(x_done, levels + 1)
                dve.tensor_copy(vn[:, :], B[3][0:n, :]).then_inc(v_ready, 1)
                dve.wait_ge(v_ready, 2)
                for h in range(H):
                    ins = dve.tensor_tensor(hd(vm[:, h, :], NSEQ), repeat(vn[:, h * P:h * P + P], NSEQ), over(k.c("s_seq", n), DH), ALU.mult)
                ins.then_inc(v_ready, 1)
                dve.wait_ge(o_done, 1)
                link(dve.tensor_copy(oT[:, :], B[7][:, 0:HN]))
                link(dve.tensor_tensor(oT[:, :], oT[:, :], B[2][:, HN:2 * HN], ALU.add))
                dve.tensor_tensor(sq[:, :], oT[:, :], oT[:, :], ALU.mult).then_inc(o_scaled, 1)
                dve.wait_ge(o_turned, 1)
                link(dve.tensor_scalar(rT[:, :], B[4][:, 0:HN], 1.0 / DH, EPS, ALU.mult, ALU.add))
                link(dve.tensor_copy(sq[:, :], rT[:, :]))
                rsqrt(dve, link, rT[:, :], sq[:, :], workT[:, :])
                link(dve.tensor_tensor(oT[:, :], oT[:, :], rT[:, :], ALU.mult))
                z = k.zT[:, :, SEQ:T]
                link(dve.scalar_tensor_tensor(z, hd(oT[:, :]), k.onorm[:, 0:1], z, ALU.mult, ALU.mult))
                link(dve.tensor_tensor(S[:, :, :], S[:, :, :], over(egl[:, :], DH), ALU.mult))
                for u in range(2 * H):
                    h, half = u // 2, u % 2
                    st = S[:, 4 * H * half + h:4 * H * (half + 1):H, :]
                    dve.wait_ge(su_done, u + 1)
                    ins = dve.tensor_tensor(st, st, hd(B[5 + half][:, :]), ALU.add)
                    ins.then_inc(upd_done, 1) if u < 2 * H - 1 else ins.then_inc(s_ready, 1)

            tiles(dve, tile)


def qkv_stage(k):
    nc, d = k.nc, k.d
    G = 2 * H
    with ExitStack() as ctx:
        sem = lambda s: k.sem(f"qk_{s}")
        w_loaded = [sem(f"w{u}") for u in range(2)]
        k_out = [sem(f"k_out{u}") for u in range(2)]
        proj_done, copied, steps, normed, turned, stored, v_out, squared, passed = (
            sem(s) for s in ("proj", "copied", "steps", "normed", "turned", "stored", "v_out", "squared", "passed"))
        wb = [k.sb(ctx, f"qk_w{u}", [P, KC, W]) for u in range(2)]
        raw = k.sb(ctx, "qk_raw", [P, 2, W])
        sq = k.sb(ctx, "qk_sq", [P, W])
        ss, r, work = (k.sb(ctx, f"qk_{s}", [P, G]) for s in ("ss", "r", "work"))
        nrm = k.sb(ctx, "qk_nrm", [P, 2, W])
        ps = [k.ps(ctx, f"qk_ps{u}") for u in range(4)]
        pt = [k.ps(ctx, f"qk_pt{u}") for u in range(2)]
        w_cols = d["w_in"].rearrange("a (c p) n -> p (a c) n", p=P)
        kp = d["k_prompt"].rearrange("a b t h n -> (a b t) (h n)")
        vp = d["v_prompt"].rearrange("a b t h n -> (a b t) (h n)")
        ks = d["k_sample"].rearrange("a b t h n -> (a b t) (h n)")
        vs = d["v_sample"].rearrange("a b t h n -> (a b t) (h n)")
        block = ctx.enter_context(nc.Block())
        NT = PT + 1
        n_of = lambda t: P if t < PT else NS

        @block.sync
        def _(sp):
            for g in range(3):
                if g == 2:
                    sp.wait_ge(proj_done, NT)
                sp.dma_start(wb[g % 2][:, :, :], w_cols[:, :, C_Q + g * W:C_Q + (g + 1) * W]).then_inc(w_loaded[g % 2], 16)
            for t in range(NT):
                sp.wait_ge(normed, NT + t + 1)
                src = nrm[0:n_of(t), (NT + t) % 2, :]
                sp.dma_start(kp[t * P:t * P + P, :] if t < PT else ks, src).then_inc(k_out[(NT + t) % 2], 16)
            sp.wait_ge(copied, 3 * NT)
            sp.dma_start(vp.rearrange("(t p) n -> p t n", p=P), k.v[:, 0:PT, :]).then_inc(v_out, 16)
            sp.dma_start(vs, k.v[0:NS, PT, :]).then_inc(v_out, 16)
            sp.wait_ge(v_out, 32)
            for u in range(2):
                sp.wait_ge(k_out[u], 16 * ((NT + u) // 2))

        @block.tensor
        def _(pe):
            def turn(j):
                n = n_of(j % NT)
                pe.wait_ge(normed, j + 1)
                if j >= 2:
                    pe.wait_ge(stored, j - 1)
                for h in range(H):
                    ins = pe.transpose(pt[j % 2][:, h * P:h * P + n], nrm[0:n, j % 2, h * P:h * P + P], k.c("ident", n)[:, 0:n])
                ins.then_inc(turned, 1)

            for g in range(3):
                pe.wait_ge(w_loaded[g % 2], 16 * (g // 2 + 1))
                for t in range(NT):
                    j = g * NT + t
                    n = n_of(t)
                    if j >= 4:
                        pe.wait_ge(copied, j - 3)
                    for c in range(KC):
                        ins = pe.matmul(ps[j % 4][0:n, :], k.hT[:, c, t * P:t * P + n], wb[g % 2][:, c, :], start=(c == 0), stop=(c == KC - 1))
                    ins.then_inc(proj_done, 1)
                    if 2 <= j < 2 * NT + 2:
                        turn(j - 2)

        @block.scalar
        def _(act):
            for j in range(3 * NT):
                n = n_of(j % NT)
                act.wait_ge(proj_done, j + 1)
                if j < 2 * NT:
                    if j >= 2:
                        act.wait_ge(normed, j - 1)
                    act.activation(raw[0:n, j % 2, :], ps[j % 4][0:n, :], ACT.Copy).then_inc(copied, 1)
                    act.wait_ge(copied, j + 1)
                    if j:
                        act.wait_ge(passed, j)
                    act.activation(sq[0:n, :], raw[0:n, j % 2, :], ACT.Square).then_inc(squared, 1)
                else:
                    act.activation(k.v[0:n, j % NT, :], ps[j % 4][0:n, :], ACT.Copy).then_inc(copied, 1)

        @block.vector
        def _(dve):
            def store(j):
                n, t = n_of(j % NT), j % NT
                dst = k.qT if j < NT else k.kT
                dve.wait_ge(turned, j + 1)
                dve.tensor_copy(dst[:, :, t * P:t * P + n], hd(pt[j % 2][:, :])[:, :, 0:n]).then_inc(stored, 1)

            link = Links(dve, steps)
            for j in range(2 * NT):
                n = n_of(j % NT)
                weight = k.qw if j < NT else k.kw
                dve.wait_ge(squared, j + 1)
                dve.tensor_reduce(ss[0:n, :], sq[0:n, :].rearrange("p (g n) -> p g n", g=G), AX.X, ALU.add).then_inc(passed, 1)
                dve.wait_ge(passed, j + 1)
                link(dve.tensor_scalar(ss[0:n, :], ss[0:n, :], 1.0 / 64, EPS, ALU.mult, ALU.add))
                rsqrt(dve, link, r[0:n, :], ss[0:n, :], work[0:n, :])
                if j >= 2:
                    dve.wait_ge(turned, j - 1)
                if j >= NT + 2:
                    dve.wait_ge(k_out[j % 2], 16 * ((j - NT) // 2))
                out = nrm[0:n, j % 2, :].rearrange("p (g n) -> p g n", g=G)
                link(dve.tensor_tensor(out, raw[0:n, j % 2, :].rearrange("p (g n) -> p g n", g=G), over(r[0:n, :], 64), ALU.mult))
                dve.tensor_tensor(out, out, repeat(weight[0:n, :], G), ALU.mult).then_inc(normed, 1)
                if j >= 1:
                    store(j - 1)
            store(2 * NT - 1)


def attention_stage(k):
    nc = k.nc
    with ExitStack() as ctx:
        sem = lambda s: k.sem(f"at_{s}")
        (staged, scored, maxed, exped, weighed, turned, moved, summed, o_saved, squared, o_normed, o_turned,
         ob_stored, chain, pool_held) = (sem(s) for s in (
             "staged", "scored", "maxed", "exped", "weighed", "turned", "moved", "summed", "o_saved", "squared",
             "o_normed", "o_turned", "ob_stored", "chain", "pool_held"))
        qh, kh = (k.sb(ctx, f"at_{s}", [P, SEQ]) for s in ("qh", "kh"))
        E = [k.sb(ctx, f"at_e{m}", [P, SEQ]) for m in range(2)]
        pr = k.sb(ctx, "at_p", [P, 2, SEQ])
        prT = k.sb(ctx, "at_pt", [P, 2, 512])
        mx, nmx, sums, rs = (k.sb(ctx, f"at_{s}", [P, 2]) for s in ("mx", "nmx", "sums", "rs"))
        o, on = (k.sb(ctx, f"at_{s}", [P, PT, DH]) for s in ("o", "on"))
        so, ro, worko = (k.sb(ctx, f"at_{s}", [P, PT]) for s in ("so", "ro", "worko"))
        ps = [k.ps(ctx, f"at_ps{m}", 2) for m in range(2)]
        pt = [k.ps(ctx, f"at_pt{m}") for m in range(2)]
        po = [k.ps(ctx, f"at_po{m}") for m in range(2)]
        flat = [ps[m][:, :, :].rearrange("p a n -> p (a n)") for m in range(2)]
        GROUPS = [(i, g) for i in range(PT) for g in range(0, i + 1, 4)]
        NG = len(GROUPS)
        first_group = [GROUPS.index((i, 0)) for i in range(PT)]
        ngroups = [(i + 4) // 4 for i in range(PT)]
        block = ctx.enter_context(nc.Block())

        def heads(eng, body):
            loop(eng, H, body)

        @block.gpsimd
        def _(pool):
            def head(h, first):
                if not first:
                    hold(pool, scored, 2 * PT * h, pool_held)
                pool.tensor_copy(qh[:, :], k.qT[:, at(h), 0:SEQ].rearrange("p a n -> p (a n)")).then_inc(staged, 1)
                pool.tensor_copy(kh[:, :], k.kT[:, at(h), 0:SEQ].rearrange("p a n -> p (a n)")).then_inc(staged, 1)

            heads(pool, head)

        @block.tensor
        def _(pe):
            def head(h, first):
                def scores(i):
                    for m in range(2):
                        if i or not first:
                            pe.wait_ge(exped, 2 * PT * h + 2 * i - 1 + m)
                        rows = slice(64 * m, 64 * m + 64)
                        nk = (i + 1) * P
                        for b in range(0, nk, 512):
                            e = min(nk, b + 512)
                            near = [c for c in (i - 1, i) if c >= 0 and b <= c * P < e]
                            pe.matmul(flat[m][:, b:e], qh[rows, i * P:i * P + P], kh[rows, b:e], start=True, stop=not near)
                            for c in near:
                                ins = pe.matmul(flat[m][:, c * P:c * P + P], k.c("ident"),
                                                k.bias[:, at(h), (c - i + 1) * P:(c - i + 2) * P].rearrange("p a n -> p (a n)"),
                                                start=False, stop=(c == near[-1]))
                        ins.then_inc(scored, 1)

                def values(i):
                    pe.wait_ge(weighed, PT * h + i + 1)
                    for n in range(ngroups[i]):
                        G = first_group[i] + n
                        g, ge = 4 * n, min(4 * n + 4, i + 1)
                        if not first or G >= 2:
                            pe.wait_ge(moved, NG * h + G - 1)
                        for c in range(g, ge):
                            ins = pe.transpose(pt[G % 2][:, (c - g) * P:(c - g + 1) * P], pr[:, i % 2, c * P:c * P + P], k.c("ident"))
                        ins.then_inc(turned, 1)
                    if not first or i >= 2:
                        pe.wait_ge(o_saved, PT * h + i - 1)
                    for n in range(ngroups[i]):
                        G = first_group[i] + n
                        g, ge = 4 * n, min(4 * n + 4, i + 1)
                        pe.wait_ge(moved, NG * h + G + 1)
                        for c in range(g, ge):
                            ins = pe.matmul(po[i % 2][:, 0:DH], prT[:, G % 2, (c - g) * P:(c - g + 1) * P],
                                            k.v[:, c, at(h * P, P)], start=(c == 0), stop=(c == i))
                    ins.then_inc(summed, 1)

                pe.wait_ge(staged, 2 * h + 2)
                scores(0)
                for i in range(PT):
                    if i + 1 < PT:
                        scores(i + 1)
                    values(i)
                pe.wait_ge(o_normed, h + 1)
                for g in range(2):
                    for i in range(4):
                        ins = pe.transpose(pt[g][:, i * P:i * P + P], on[:, 4 * g + i, :], k.c("ident"))
                    ins.then_inc(o_turned, 1)
                pe.wait_ge(ob_stored, 2 * h + 2)

            heads(pe, head)

        @block.scalar
        def _(act):
            def head(h, first):
                def move(i):
                    for n in range(ngroups[i]):
                        G = first_group[i] + n
                        w = (min(4 * n + 4, i + 1) - 4 * n) * P
                        act.wait_ge(turned, NG * h + G + 1)
                        if not first or G >= 2:
                            act.wait_ge(summed, PT * h + (GROUPS[G - 2][0] + 1 if G >= 2 else 0))
                        act.activation(prT[:, G % 2, 0:w], pt[G % 2][:, 0:w], ACT.Copy).then_inc(moved, 1)

                for i in range(PT):
                    for m in range(2):
                        act.wait_ge(maxed, 2 * PT * h + 2 * i + m + 1)
                        if not first or i:
                            act.wait_ge(weighed, PT * h + i)
                        act.activation(E[m][:, 0:(i + 1) * P], flat[m][:, 0:(i + 1) * P], ACT.Exp, bias=nmx[:, m:m + 1],
                                       scale=0.125, accum_out=sums[:, m:m + 1]).then_inc(exped, 1)
                    if i:
                        move(i - 1)
                move(PT - 1)
                for i in range(PT):
                    act.wait_ge(o_saved, PT * h + i + 1)
                    if not first or i:
                        act.wait_ge(squared, PT * h + i)
                    act.activation(E[1][:, 0:DH], o[:, i, :], ACT.Square, accum_out=so[:, i:i + 1]).then_inc(squared, 1)

            heads(act, head)

        @block.vector
        def _(dve):
            per = [0]

            def head(h, first):
                link = Links(dve, chain, per[0] * h)

                def save(i):
                    dve.wait_ge(summed, PT * h + i + 1)
                    dve.tensor_copy(o[:, i, :], po[i % 2][:, 0:DH]).then_inc(o_saved, 1)

                for i in range(PT):
                    nk = (i + 1) * P
                    for m in range(2):
                        dve.wait_ge(scored, 2 * PT * h + 2 * i + m + 1)
                        if m == 0 and (i or not first):
                            dve.wait_ge(exped, 2 * PT * h + 2 * i)
                        link(dve.tensor_reduce(mx[:, m:m + 1], flat[m][:, 0:nk], AX.X, ALU.max))
                        link(dve.tensor_scalar(nmx[:, m:m + 1], mx[:, m:m + 1], -0.125, None, ALU.mult))
                        dve.sem_inc(maxed, 1)
                    dve.wait_ge(exped, 2 * PT * h + 2 * i + 2)
                    link(dve.reciprocal(rs[:, :], sums[:, :]))
                    link(dve.scalar_tensor_tensor(rs[:, 1:2], rs[:, 1:2], -1.0, k.lam[:, :], ALU.mult, ALU.mult))
                    if not first or i >= 2:
                        dve.wait_ge(turned, NG * h + (first_group[i - 2] + ngroups[i - 2] if i >= 2 else (first_group[PT + i - 2] + ngroups[PT + i - 2] - NG)))
                    link(dve.tensor_scalar(pr[:, i % 2, 0:nk], E[0][:, 0:nk], rs[:, 0:1], None, ALU.mult))
                    link(dve.scalar_tensor_tensor(pr[:, i % 2, 0:nk], E[1][:, 0:nk], rs[:, 1:2], pr[:, i % 2, 0:nk], ALU.mult, ALU.add))
                    dve.sem_inc(weighed, 1)
                    if i:
                        save(i - 1)
                save(PT - 1)
                dve.wait_ge(squared, PT * h + PT)
                link(dve.tensor_scalar(so[:, :], so[:, :], 1.0 / DH, EPS, ALU.mult, ALU.add))
                rsqrt(dve, link, ro[:, :], so[:, :], worko[:, :])
                if not first:
                    dve.wait_ge(o_turned, 2 * h)
                link(dve.tensor_tensor(on[:, :, :], o[:, :, :], over(ro[:, :], DH), ALU.mult))
                dve.sem_inc(o_normed, 1)
                for g in range(2):
                    dve.wait_ge(o_turned, 2 * h + g + 1)
                    dve.tensor_scalar(k.obT[:, at(h), g * 512:(g + 1) * 512].rearrange("p a n -> p (a n)"), pt[g][:, :],
                                      k.subln[:, 0:1], None, ALU.mult).then_inc(ob_stored, 1)
                per[0] = link.n

            heads(dve, head)


def decode_stage(k):
    nc, d = k.nc, k.d
    NK = PAST + NS
    RG = 2
    with ExitStack() as ctx:
        sem = lambda s: k.sem(f"de_{s}")
        (table_in, v_in, q_set, k_turned, k_moved, scored, new_scored, sc_moved, row_turned, biased, exped, weighed, steps,
         back, back_moved, pt_ready, summed, sq_ready, norm_done, bias_set) = (sem(s) for s in (
             "table_in", "v_in", "q_set", "k_turned", "k_moved", "scored", "new_scored", "sc_moved", "row_turned", "biased", "exped",
             "weighed", "steps", "back", "back_moved", "pt_ready", "summed", "sq_ready", "norm_done", "bias_set"))
        k_in = [sem(f"k_in{u}") for u in range(4)]
        table = k.sb(ctx, "de_table", [1, NSEQ * PAGES], I32)
        kpg = k.sb(ctx, "de_kpg", [P, 4, W])
        vpg = k.sb(ctx, "de_vpg", [P, NSEQ * PAGES, W])
        kpT = k.sb(ctx, "de_kpT", [P, 2, W])
        Q = k.sb(ctx, "de_q", [P, NSEQ, H, 2, QN])
        sc = k.sb(ctx, "de_sc", [P, PAGES, 256])
        scn = k.sb(ctx, "de_scn", [NS, 256])
        bnew = k.sb(ctx, "de_bnew", [P, RG, NSEQ, QN])
        X = k.sb(ctx, "de_x", [P, RG, NK])
        mx, nmx, sums, rs = (k.sb(ctx, f"de_{s}", [P, RG]) for s in ("mx", "nmx", "sums", "rs"))
        sgn = k.sb(ctx, "de_sgn", [P, 1])
        pb = k.sb(ctx, "de_pb", [P, PAGES, 256])
        pbn = k.sb(ctx, "de_pbn", [NS, 256])
        prT = k.sb(ctx, "de_prT", [P, PAGES, NSEQ * H, QN])
        prTn = k.sb(ctx, "de_prTn", [NS, NSEQ * H, QN])
        oT, sq, ro, work = (k.sb(ctx, f"de_{s}", [P, P]) for s in ("oT", "sq", "ro", "work"))
        pk = [k.ps(ctx, f"de_pk{u}") for u in range(2)]
        psc, psn, po, pss = (k.ps(ctx, f"de_{s}") for s in ("psc", "psn", "po", "pss"))
        prow = [k.ps(ctx, f"de_prow{u}") for u in range(RG)]
        block = ctx.enter_context(nc.Block())
        ck = d["cache_k"].rearrange("a g p h n -> p (a g) (h n)")
        cv = d["cache_v"].rearrange("a g p h n -> p (a g) (h n)")
        pool_pages = ck.shape[1]
        NPG = NSEQ * PAGES

        @block.sync
        def _(sp):
            sp.dma_start(table[:, :], d["page_table"].rearrange("(a s) g -> a (s g)", a=1)).then_inc(table_in, 16)
            sp.wait_ge(table_in, 16)
            for j in range(NPG):
                page = sp.value_load(table[0:1, j:j + 1], min_val=0, max_val=pool_pages - 1)
                if j >= 4:
                    sp.wait_ge(k_turned, j - 3)
                sp.dma_start(kpg[:, j % 4, :], ck[:, at(page), :].rearrange("p a n -> p (a n)")).then_inc(k_in[j % 4], 16)
                sp.dma_start(vpg[:, j, :], cv[:, at(page), :].rearrange("p a n -> p (a n)")).then_inc(v_in, 16)

        @block.tensor
        def _(pe):
            ident = k.c("ident")

            def turn(j):
                pe.wait_ge(k_in[j % 4], 16 * (j // 4 + 1))
                if j >= 2:
                    pe.wait_ge(k_moved, j - 1)
                for h in range(H):
                    ins = pe.transpose(pk[j % 2][:, h * P:h * P + P], kpg[:, j % 4, h * P:h * P + P], ident)
                ins.then_inc(k_turned, 1)

            def score(j):
                s, g = j // PAGES, j % PAGES
                pe.wait_ge(k_moved, j + 1)
                for h in range(H):
                    c = g * 256 + (s * H + h) * 8
                    ins = pe.matmul(psc[:, c:c + 8], kpT[:, j % 2, h * P:h * P + P], Q[:, s, h, :, :].rearrange("p m q -> p (m q)"),
                                    start=True, stop=True)
                ins.then_inc(scored, 1)

            turn(0)
            pe.wait_ge(q_set, 9)
            for h in range(H):
                ins = pe.matmul(psn[0:NS, 0:256].rearrange("p (s h n) -> p s h n", s=NSEQ, h=H)[:, :, h, :],
                                k.kT[:, h, SEQ:T], Q[:, :, h, :, :].rearrange("p s m q -> p s (m q)"), start=True, stop=True)
            ins.then_inc(new_scored, 1)
            for j in range(NPG):
                if j + 1 < NPG:
                    turn(j + 1)
                score(j)
            pe.wait_ge(sc_moved, 2)
            for r in range(RG):
                for g in range(PAGES):
                    pe.transpose(prow[r][:, g * P:g * P + P], sc[:, g, r * P:r * P + P], ident)
                pe.transpose(prow[r][:, PAST:NK], scn[:, r * P:r * P + P], ident[0:NS, 0:NS]).then_inc(row_turned, 1)
            pe.wait_ge(weighed, 1)
            for r in range(RG):
                for g in range(PAGES):
                    pe.transpose(psc[:, g * 256 + r * P:g * 256 + r * P + P], X[:, r, g * P:g * P + P], ident)
                ins = pe.transpose(psn[0:NS, r * P:r * P + P], X[:, r, PAST:NK], ident)
            ins.then_inc(back, 1)
            pe.wait_ge(pt_ready, 2)
            pe.wait_ge(v_in, 16 * NPG)
            for h in range(H):
                for s in range(NSEQ):
                    out = po[:, (h * NSEQ + s) * QN:(h * NSEQ + s + 1) * QN]
                    for g in range(PAGES):
                        pe.matmul(out, vpg[:, s * PAGES + g, h * P:h * P + P], prT[:, g, s * H + h, :], start=(g == 0), stop=False)
                    ins = pe.matmul(out, k.v[0:NS, PT, h * P:h * P + P], prTn[:, s * H + h, :], start=False, stop=True)
            ins.then_inc(summed, 1)
            pe.wait_ge(sq_ready, 1)
            pe.matmul(pss[:, 0:P], k.c("ones"), sq[:, :], start=True, stop=True).then_inc(norm_done, 1)

        @block.scalar
        def _(act):
            for j in range(NPG):
                act.wait_ge(k_turned, j + 1)
                if j >= 2:
                    act.wait_ge(scored, j - 1)
                act.activation(kpT[:, j % 2, :], pk[j % 2][:, :], ACT.Copy).then_inc(k_moved, 1)
            act.wait_ge(biased, 1)
            for r in range(RG):
                act.activation(X[:, r, :], X[:, r, :], ACT.Exp, bias=nmx[:, r:r + 1], scale=0.125,
                               accum_out=sums[:, r:r + 1]).then_inc(exped, 1)

        @block.vector
        def _(dve):
            link = Links(dve, steps)
            dve.memset(Q[:, :, :, :, :], 0.0).then_inc(q_set, 1)
            dve.wait_ge(q_set, 1)
            for m in range(2):
                rows = slice(64 * m, 64 * m + 64)
                for h in range(H):
                    dve.tensor_copy(Q[rows, :, h, m, :], k.qT[rows, h, SEQ:T].rearrange("p (s q) -> p s q", s=NSEQ)).then_inc(q_set, 1)
            link(dve.scalar_tensor_tensor(sgn[:, :], k.c("m1"), -1.0, k.lam[:, :], ALU.mult, ALU.mult))
            link(dve.tensor_tensor(sgn[:, :], sgn[:, :], k.c("m0"), ALU.add))
            for r in range(RG):
                cross = k.c("s_cross")[:, r * NSEQ:(r + 1) * NSEQ]
                link(dve.tensor_tensor(bnew[:, r, :, :], repeat(k.sbias[:, PAST:PAST + QN], NSEQ), over(cross, QN), ALU.add))
            dve.wait_ge(new_scored, 1)
            dve.tensor_copy(scn[:, :], psn[0:NS, 0:256]).then_inc(sc_moved, 1)
            dve.wait_ge(scored, NPG)
            dve.tensor_copy(sc[:, :, :], psc[:, :].rearrange("p (g n) -> p g n", g=PAGES)).then_inc(sc_moved, 1)
            for r in range(RG):
                dve.wait_ge(row_turned, r + 1)
                link(dve.tensor_tensor(X[:, r, 0:PAST], prow[r][:, 0:PAST], k.sbias[:, 0:PAST], ALU.add))
                link(dve.tensor_tensor(X[:, r, PAST:NK], prow[r][:, PAST:NK], bnew[:, r, :, :].rearrange("p s q -> p (s q)"), ALU.add))
            link(dve.tensor_reduce(mx[:, :], X[:, :, :], AX.X, ALU.max))
            dve.tensor_scalar(nmx[:, :], mx[:, :], -0.125, None, ALU.mult).then_inc(biased, 1)
            dve.wait_ge(exped, RG)
            link(dve.reciprocal(rs[:, :], sums[:, :]))
            link(dve.tensor_scalar(rs[:, :], rs[:, :], sgn[:, 0:1], None, ALU.mult))
            dve.tensor_tensor(X[:, :, :], X[:, :, :], over(rs[:, :], NK), ALU.mult).then_inc(weighed, 1)
            dve.wait_ge(back, 1)
            link(dve.tensor_copy(pb[:, :, :], psc[:, :].rearrange("p (g n) -> p g n", g=PAGES)))
            link(dve.tensor_copy(pbn[:, :], psn[0:NS, 0:256]))
            pv = pb[:, :, :].rearrange("p g (s m q) -> p (g s) m q", m=2, q=QN)
            dve.tensor_tensor(prT[:, :, :, :].rearrange("p g s q -> p (g s) q"), pv[:, :, 0, :], pv[:, :, 1, :], ALU.add).then_inc(pt_ready, 1)
            pn = pbn[:, :].rearrange("p (s m q) -> p s m q", m=2, q=QN)
            dve.tensor_tensor(prTn[:, :, :], pn[:, :, 0, :], pn[:, :, 1, :], ALU.add).then_inc(pt_ready, 1)
            dve.wait_ge(summed, 1)
            link(dve.tensor_copy(oT[:, :], po[:, 0:P]))
            dve.tensor_tensor(sq[:, :], oT[:, :], oT[:, :], ALU.mult).then_inc(sq_ready, 1)
            dve.wait_ge(norm_done, 1)
            link(dve.tensor_scalar(sq[:, :], pss[:, 0:P], 1.0 / DH, EPS, ALU.mult, ALU.add))
            rsqrt(dve, link, ro[:, :], sq[:, :], work[:, :])
            link(dve.tensor_tensor(oT[:, :], oT[:, :], ro[:, :], ALU.mult))
            link(dve.tensor_scalar(k.obT[:, :, SEQ:T], hd(oT[:, :]), k.subln[:, 0:1], None, ALU.mult))


def mix_stage(k):
    nc, d = k.nc, k.d
    with ExitStack() as ctx:
        sem = lambda s: k.sem(f"mx_{s}")
        gate_done, gate_ready, branch_done, mixed_done, chain, sp_held = (sem(s) for s in ("gate", "gate_ready", "branch", "mixed", "chain", "sp_held"))
        g_in, b_in = ([sem(f"{s}{u}") for u in range(2)] for s in ("g_in", "b_in"))
        wg = k.sb(ctx, "mx_wg", [P, 2, KC, P])
        wbr = k.sb(ctx, "mx_wb", [P, 2, H, P])
        sg = k.sb(ctx, "mx_sg", [P, 2, T])
        ps = [k.ps(ctx, f"mx_ps{u}", 3) for u in range(2)]
        w_cols = d["w_in"].rearrange("a (c p) n -> p (a c) n", p=P)
        b_cols = d["w_branch"].rearrange("a b (c p) n -> p (a b) c n", p=P)
        block = ctx.enter_context(nc.Block())

        @block.sync
        def _(sp):
            def step(i, first):
                for u in range(2):
                    if not first:
                        hold(sp, gate_done, 2 * i - 1 + u, sp_held)
                    sp.dma_start(wg[:, u, :, :], w_cols[:, :, at(i * P + (C_GB if u else C_GA), P)]).then_inc(g_in[u], 16)
                    if not first:
                        hold(sp, branch_done, 2 * i - 1 + u, sp_held)
                    sp.dma_start(wbr[:, u, :, :], b_cols[:, u, :, at(i * P, P)]).then_inc(b_in[u], 16)

            loop(sp, KC, step)

        @block.tensor
        def _(pe):
            def step(i, first):
                for u in range(2):
                    pe.wait_ge(g_in[u], 16 * i + 16)
                    if u or not first:
                        pe.wait_ge(gate_ready, 2 * i + u)
                    dense_cols(pe, ps[0], wg[:, u, :, :], k.hT, KC, gate_done)
                    pe.wait_ge(b_in[u], 16 * i + 16)
                    if u or not first:
                        pe.wait_ge(mixed_done, 2 * i + u)
                    dense_cols(pe, ps[1], wbr[:, u, :, :], k.obT if u else k.zT, H, branch_done)

            loop(pe, KC, step)

        @block.scalar
        def _(act):
            def step(i, first):
                for u in range(2):
                    act.wait_ge(gate_done, 2 * i + u + 1)
                    if not first:
                        act.wait_ge(mixed_done, 2 * i - 1 + u)
                    for b in range(NB):
                        ins = act.activation(sg[:, u, b * BW:(b + 1) * BW], ps[0][:, b, 0:BW], ACT.Sigmoid)
                    ins.then_inc(gate_ready, 1)

            loop(act, KC, step)

        @block.vector
        def _(dve):
            def step(i, first):
                for u in range(2):
                    dve.wait_ge(branch_done, 2 * i + u + 1)
                    dve.wait_ge(gate_ready, 2 * i + u + 1)
                    g = sg[:, u, :].rearrange("p (b n) -> p b n", b=NB)
                    out = k.mixedT[:, at(i), :].rearrange("p a (b n) -> p (a b) n", b=NB)
                    if u == 0:
                        dve.tensor_tensor(out, g, ps[1][:, :, 0:BW], ALU.mult).then_inc(mixed_done, 1)
                    else:
                        dve.tensor_tensor(g, g, ps[1][:, :, 0:BW], ALU.mult).then_inc(chain, 1)
                        dve.wait_ge(chain, i + 1)
                        dve.wait_ge(mixed_done, 2 * i + 1)
                        dve.tensor_tensor(out, out, g, ALU.add).then_inc(mixed_done, 1)

            loop(dve, KC, step)


def out_proj_stage(k):
    nc, d = k.nc, k.d
    with ExitStack() as ctx:
        sem = lambda s: k.sem(f"wo_{s}")
        x_in, done, added = (sem(s) for s in ("x_in", "done", "added"))
        w_loaded = [sem(f"w{half}") for half in range(2)]
        wb = k.sb(ctx, "wo_w", [P, 2, KC, 512])
        ps = [k.ps(ctx, f"wo_ps{u}") for u in range(4)]
        block = ctx.enter_context(nc.Block())
        NT = PT + 1

        @block.sync
        def _(sp):
            wv = d["w_o"].rearrange("a (c p) n -> p (a c) n", p=P)
            for half in range(2):
                sp.dma_start(wb[:, half, :, :], wv[:, :, half * 512:(half + 1) * 512]).then_inc(w_loaded[half], 16)
                if half == 0:
                    sp.dma_start(k.x[:, 0:PT, :], d["x_prompt"].rearrange("b (t p) n -> p (b t) n", p=P)).then_inc(x_in, 16)
                    sp.dma_start(k.x[0:NS, PT, :], d["x_sample"].rearrange("b q n -> (b q) n")).then_inc(x_in, 16)

        @block.tensor
        def _(pe):
            for half in range(2):
                pe.wait_ge(w_loaded[half], 16)
                for t in range(NT):
                    j, n = half * NT + t, P if t < PT else NS
                    if j >= 4:
                        pe.wait_ge(added, j - 3)
                    for c in range(KC):
                        ins = pe.matmul(ps[j % 4][0:n, :], k.mixedT[:, c, t * P:t * P + n], wb[:, half, c, :], start=(c == 0), stop=(c == KC - 1))
                    ins.then_inc(done, 1)

        @block.vector
        def _(dve):
            dve.wait_ge(x_in, 32)
            for half in range(2):
                for t in range(NT):
                    j, n = half * NT + t, P if t < PT else NS
                    x = k.x[0:n, t, half * 512:(half + 1) * 512]
                    dve.wait_ge(done, j + 1)
                    dve.tensor_tensor(x, x, ps[j % 4][0:n, :], ALU.add).then_inc(added, 1)


def ffn_up_stage(k):
    nc, d = k.nc, k.d
    R = TF - 1
    RAW = R + SEQ + NSEQ * (R + QN)
    OUT = RAW - R
    NH = NSEQ * R
    NR = NH + TF + 1
    LAST = R + NSEQ * R
    NC = 2 * CF
    with ExitStack() as ctx:
        sem = lambda n: k.sem(f"up_{n}")
        w_loaded = [sem(f"w{u}") for u in range(2)]
        proj_done = [sem(f"proj{u}") for u in range(2)]
        evac_done = [sem(f"evac{u}") for u in range(2)]
        conv_done = [sem(f"conv{u}") for u in range(2)]
        tap_done = [sem(f"tap{u}") for u in range(2)]
        taps_in = [sem(f"taps_in{u}") for u in range(2)]
        last_out = [sem(f"last_out{u}") for u in range(2)]
        saved, taps_turned, taps_sb, last_turned, last_sb, chain, silu_done, u_done, sp_held, pool_held = (
            sem(n) for n in ("saved", "taps_turned", "taps_sb", "last_turned", "last_sb", "chain", "silu", "u", "sp_held", "pool_held"))
        wb = [k.sb(ctx, f"up_w{u}", [P, KC, P]) for u in range(2)]
        raw = [k.sb(ctx, f"up_raw{u}", [P, RAW]) for u in range(2)]
        acc = [k.sb(ctx, f"up_acc{u}", [P, RAW]) for u in range(2)]
        nat = k.sb(ctx, "up_nat", [NR, 2, 4 * P])
        taps = k.sb(ctx, "up_taps", [P, NC, NR])
        last = k.sb(ctx, "up_last", [P, NC, LAST])
        ps = [k.ps(ctx, f"up_ps{u}", 3) for u in range(2)]
        pt = k.ps(ctx, "up_pt", 2)
        samp = [raw[u][:, R + SEQ:RAW].rearrange("p (s c) -> p s c", s=NSEQ) for u in range(2)]
        samp_out = [acc[u][:, R + SEQ:RAW].rearrange("p (s c) -> p s c", s=NSEQ) for u in range(2)]
        w_cols = d["w_up"].rearrange("a (c p) n -> p (a c) n", p=P)
        NQ = NC // 4
        hist = d["state_conv_ffn"].rearrange("a s r n -> (a s r) n")
        cf = d["conv_f"].rearrange("a w n -> (a w) n")
        block = ctx.enter_context(nc.Block())

        @block.sync
        def _(sp):
            for q in range(NQ):
                if q >= 2:
                    sp.wait_ge(taps_turned, q - 1)
                c = slice(q * 512, (q + 1) * 512)
                sp.dma_start(nat[0:NH, q % 2, :], hist[:, c]).then_inc(taps_in[q % 2], 16)
                sp.dma_start(nat[NH:NH + TF, q % 2, :], cf[:, c]).then_inc(taps_in[q % 2], 16)
                sp.dma_start(nat[NH + TF:NR, q % 2, :], d["conv_f_b"][:, c]).then_inc(taps_in[q % 2], 16)
                if q == 0:
                    for u in range(2):
                        sp.dma_start(wb[u][:, :, :], w_cols[:, :, u * DFF:u * DFF + P]).then_inc(w_loaded[u], 16)

            with sp.Fori(1, CF) as i:
                for u in range(2):
                    hold(sp, proj_done[u], i, sp_held)
                    sp.dma_start(wb[u][:, :, :], w_cols[:, :, at(i * P + u * DFF, P)]).then_inc(w_loaded[u], 16)
            for q in range(NQ):
                sp.wait_ge(last_sb, q + 1)
                c = slice(q * 512, (q + 1) * 512)
                sp.dma_start(d["conv_ffn_prompt"].rearrange("a b r n -> (a b r) n")[:, c], nat[0:R, q % 2, :]).then_inc(last_out[q % 2], 16)
                sp.dma_start(d["conv_ffn_sample"].rearrange("a s r n -> (a s r) n")[:, c], nat[R:LAST, q % 2, :]).then_inc(last_out[q % 2], 16)
            for u in range(2):
                sp.wait_ge(last_out[u], 32 * ((NQ + 1 - u) // 2))

        @block.tensor
        def _(pe):
            for q in range(NQ):
                pe.wait_ge(taps_in[q % 2], 48 * (q // 2 + 1))
                if q >= 2:
                    pe.wait_ge(taps_sb, q - 1)
                for c in range(4):
                    ins = pe.transpose(pt[:, q % 2, c * P:c * P + NR], nat[:, q % 2, c * P:(c + 1) * P], k.c("ident", NR)[:, 0:NR])
                ins.then_inc(taps_turned, 1)

            def chunks(i, first):
                for u in range(2):
                    pe.wait_ge(w_loaded[u], 16 * i + 16)
                    if not first:
                        pe.wait_ge(evac_done[u], i)
                    dense_cols(pe, ps[u], wb[u], k.hT, KC, proj_done[u])

            loop(pe, CF, chunks)
            pe.wait_ge(saved, 4 * CF)
            for q in range(NQ):
                if q >= 2:
                    pe.wait_ge(last_sb, q - 1)
                for c in range(4):
                    ins = pe.transpose(pt[0:LAST, q % 2, c * P:c * P + P], last[:, 4 * q + c, :], k.c("ident"))
                ins.then_inc(last_turned, 1)

        @block.scalar
        def _(act):
            def chunk(i, first):
                for u in range(2):
                    act.wait_ge(proj_done[u], i + 1)
                    if not first:
                        act.wait_ge(conv_done[u], i)
                        act.wait_ge(saved, 4 * i - 2 + 2 * u)
                    for b in range(NB):
                        lo, hi = b * BW, min(SEQ, (b + 1) * BW)
                        act.activation(raw[u][:, R + lo:R + hi], ps[u][:, b, 0:hi - lo], ACT.Copy)
                    act.activation(samp[u][:, :, R:R + QN], ps[u][:, NB - 1, BW - NS:BW].rearrange("p (s c) -> p s c", s=NSEQ),
                                   ACT.Copy).then_inc(evac_done[u], 1)
                act.wait_ge(conv_done[0], i + 1)
                act.activation(acc[0][:, 0:OUT], acc[0][:, 0:OUT], ACT.Silu).then_inc(silu_done, 1)

            loop(act, CF, chunk)

        @block.gpsimd
        def _(pool):
            def save(i, first):
                for u in range(2):
                    hold(pool, evac_done[u], i + 1, pool_held)
                    pool.tensor_copy(last[:, at(i + u * CF), 0:R].rearrange("p a n -> p (a n)"), raw[u][:, SEQ:SEQ + R]).then_inc(saved, 1)
                    pool.tensor_copy(last[:, at(i + u * CF), R:LAST].rearrange("p a (s c) -> p (a s) c", s=NSEQ),
                                     samp[u][:, :, QN:QN + R]).then_inc(saved, 1)

            loop(pool, CF, save)

        @block.vector
        def _(dve):
            for u in range(2):
                dve.memset(raw[u][:, 0:R], 0.0).then_inc(chain, 1)
            for q in range(NQ):
                dve.wait_ge(taps_turned, q + 1)
                dve.tensor_copy(taps[:, 4 * q:4 * q + 4, :], hd(pt[:, q % 2, :])[:, :, 0:NR]).then_inc(taps_sb, 1)
            dve.wait_ge(taps_sb, NQ)
            dve.wait_ge(chain, 2)
            per = [0]

            def tap(c, w):
                return taps[:, at(c), NH + w:NH + w + 1].rearrange("p a n -> p (a n)")

            def chunk(i, first):
                link = Links(dve, chain, 2 + per[0] * i)
                for u in range(2):
                    c = i + u * CF
                    dve.wait_ge(evac_done[u], i + 1)
                    if not first:
                        dve.wait_ge(u_done, 2 * i)
                    link(dve.tensor_copy(samp[u][:, :, 0:R], taps[:, at(c), 0:NH].rearrange("p a (s r) -> p (a s) r", s=NSEQ)))
                    link(dve.tensor_scalar(acc[u][:, 0:OUT], raw[u][:, 0:OUT], tap(c, 0), tap(c, TF), ALU.mult, ALU.add))
                    for w in range(1, TF):
                        link(dve.scalar_tensor_tensor(acc[u][:, 0:OUT], raw[u][:, w:w + OUT], tap(c, w), acc[u][:, 0:OUT], ALU.mult, ALU.add))
                    dve.sem_inc(conv_done[u], 1)
                dve.wait_ge(silu_done, i + 1)
                dve.tensor_tensor(k.uT[:, at(i), 0:SEQ].rearrange("p a n -> p (a n)"), acc[0][:, 0:SEQ], acc[1][:, 0:SEQ], ALU.mult).then_inc(u_done, 1)
                dve.tensor_tensor(k.uT[:, at(i), SEQ:T].rearrange("p a (s c) -> p (a s) c", s=NSEQ), samp_out[0][:, :, 0:QN],
                                  samp_out[1][:, :, 0:QN], ALU.mult).then_inc(u_done, 1)
                per[0] = link.n

            loop(dve, CF, chunk)
            for q in range(NQ):
                dve.wait_ge(last_turned, q + 1)
                if q >= 2:
                    dve.wait_ge(last_out[q % 2], 32 * (q // 2))
                dve.tensor_copy(nat[0:LAST, q % 2, :], pt[0:LAST, q % 2, :]).then_inc(last_sb, 1)


def ffn_down_stage(k):
    nc, d = k.nc, k.d
    NQ, QW = 4, D // 4
    NT = PT + 1
    with ExitStack() as ctx:
        sem = lambda s: k.sem(f"dn_{s}")
        w_loaded = [sem(f"w{u}") for u in range(2)]
        done, added, y_out = (sem(s) for s in ("done", "added", "y_out"))
        wb = [k.hT[:, :, :].rearrange("p c n -> p (c n)")[:, 0:CF * QW].rearrange("p (c n) -> p c n", c=CF),
              k.sb(ctx, "dn_w", [P, CF, QW])[:, :, :]]
        ps = [k.ps(ctx, f"dn_ps{u}") for u in range(4)]
        block = ctx.enter_context(nc.Block())

        @block.sync
        def _(sp):
            wv = d["w_down"].rearrange("a (c p) n -> p (a c) n", p=P)
            yp = d["y_prompt"].rearrange("b (t p) n -> p (b t) n", p=P)
            ys = d["y_sample"].rearrange("b q n -> (b q) n")
            for q in range(NQ + 1):
                if q < NQ:
                    if q >= 2:
                        sp.wait_ge(done, NT * (q - 1))
                    for c in range(0, CF, CF // 2):
                        sp.dma_start(wb[q % 2][:, c:c + CF // 2, :], wv[:, c:c + CF // 2, q * QW:(q + 1) * QW]).then_inc(w_loaded[q % 2], 16)
                if q:
                    cs = slice((q - 1) * QW, q * QW)
                    for t0 in (0, PT // 2):
                        sp.wait_ge(added, NT * (q - 1) + t0 + PT // 2)
                        sp.dma_start(yp[:, t0:t0 + PT // 2, cs], k.x[:, t0:t0 + PT // 2, cs]).then_inc(y_out, 16)
                    sp.wait_ge(added, NT * q)
                    sp.dma_start(ys[:, cs], k.x[0:NS, PT, cs]).then_inc(y_out, 16)
            sp.wait_ge(y_out, 16 * 3 * NQ)

        @block.tensor
        def _(pe):
            for q in range(NQ):
                pe.wait_ge(w_loaded[q % 2], 32 * (q // 2 + 1))
                for t in range(NT):
                    j, n = q * NT + t, P if t < PT else NS
                    if j >= 4:
                        pe.wait_ge(added, j - 3)
                    for c in range(CF):
                        ins = pe.matmul(ps[j % 4][0:n, 0:QW], k.uT[:, c, t * P:t * P + n], wb[q % 2][:, c, :], start=(c == 0), stop=(c == CF - 1))
                    ins.then_inc(done, 1)

        @block.vector
        def _(dve):
            for q in range(NQ):
                for t in range(NT):
                    j, n = q * NT + t, P if t < PT else NS
                    x = k.x[0:n, t, q * QW:(q + 1) * QW]
                    dve.wait_ge(done, j + 1)
                    dve.tensor_tensor(x, x, ps[j % 4][0:n, 0:QW], ALU.add).then_inc(added, 1)


def layer(nc, d, only=None):
    k = Core(nc, d)
    with ExitStack() as ctx:
        k.const = k.sb(ctx, "const", [P, CONSTS.shape[1]])
        k.qw, k.kw = (k.sb(ctx, n, [P, 64]) for n in ("qw", "kw"))
        k.alog, k.dtb = (k.sb(ctx, n, [P, H]) for n in ("alog", "dtb"))
        k.wmix, k.wffn = (k.sb(ctx, n, [P, KC]) for n in ("wmix", "wffn"))
        k.onorm, k.subln, k.lam = (k.sb(ctx, n, [P, 1]) for n in ("onorm", "subln", "lam"))
        k.hT = k.sb(ctx, "hT", [P, KC, T])
        k.x = k.sb(ctx, "x", [P, PT + 1, D])
        with ExitStack() as mix:
            k.bias = k.sb(mix, "bias", [P, H, 2 * P])
            k.sbias = k.sb(mix, "sbias", [P, PAST + QN])
            k.zT = k.sb(mix, "zT", [P, H, T])
            k.g, k.beta = (k.sb(mix, n, [P, PT + 1, H]) for n in ("g", "beta"))
            load_stage(k)
            norm_stage(k, "mix", k.wmix)
            with ExitStack() as gdn:
                k.qkvT = k.sb(gdn, "qkvT", [P, CA, T])
                conv_proj_stage(k)
                gates_stage(k)
                delta_stage(k, False)
                k.clear()
                delta_stage(k, True)
                k.clear()
            spare = k.x[:, :, :].rearrange("p t n -> p (t n)")
            k.v = spare[:, 0:(PT + 1) * W].rearrange("p (t n) -> p t n", n=W)
            k.obT = spare[:, (PT + 1) * W:(PT + 1) * W + H * T].rearrange("p (h n) -> p h n", h=H)
            with ExitStack() as att:
                k.qT, k.kT = (k.sb(att, n, [P, H, T]) for n in ("qT", "kT"))
                qkv_stage(k)
                attention_stage(k)
                decode_stage(k)
                k.clear()
            k.mixedT = k.sb(mix, "mixedT", [P, KC, T])
            mix_stage(k)
            out_proj_stage(k)
        norm_stage(k, "ffn", k.wffn)
        k.uT = k.sb(ctx, "uT", [P, CF, T])
        ffn_up_stage(k)
        ffn_down_stage(k)


_INS = ["x_prompt", "x_sample", "cache_k", "cache_v", "state_delta", "state_conv_a", "state_conv_ffn", "page_table",
        "rel_bias", "norm_mix", "w_in", "conv_a", "a_log", "dt_bias", "onorm_a", "qnorm_b", "knorm_b", "lam_q1",
        "lam_k1", "lam_q2", "lam_k2", "subln_b", "w_branch", "w_o", "norm_ffn", "w_up", "conv_f", "conv_f_b", "w_down"]
_OUTS = [("y_prompt", (1, SEQ, D)), ("y_sample", (NSEQ, QN, D)), ("k_prompt", (1, 1, SEQ, H, DH)),
         ("v_prompt", (1, 1, SEQ, H, DH)), ("delta_prompt", (1, 1, H, DH, DH)), ("conv_a_prompt", (1, 1, TA - 1, QKV)),
         ("conv_ffn_prompt", (1, 1, TF - 1, 2 * DFF)), ("k_sample", (1, NSEQ, QN, H, DH)),
         ("v_sample", (1, NSEQ, QN, H, DH)), ("delta_sample", (1, NSEQ, H, DH, DH)),
         ("conv_a_sample", (1, NSEQ, TA - 1, QKV)), ("conv_ffn_sample", (1, NSEQ, TF - 1, 2 * DFF))]


def kernel(**inputs):
    import concourse.bacc as _bacc
    from concourse.bass_utils import run_bass_kernel_spmd as _run

    nc = _bacc.Bacc("TRN2", target_bir_lowering=False, num_devices=1)
    arrays, d = {"in_consts": CONSTS}, {}
    for name in _INS:
        arrays[f"in_{name}"] = np.ascontiguousarray(inputs[name])
    for name, a in arrays.items():
        d[name[3:]] = nc.dram_tensor(name, a.shape, mybir.dt.from_np(a.dtype), kind="ExternalInput").ap()
    for name, shape in _OUTS:
        d[name] = nc.dram_tensor(f"out_{name}", shape, F32, kind="ExternalOutput").ap()
    layer(nc, d)
    r = _run(nc, [arrays], core_ids=[0])
    return tuple(r.results[0][f"out_{name}"] for name, _ in _OUTS)
```

```python
import math
from contextlib import ExitStack

import numpy as np

import concourse.bass as bass
from concourse import mybir

F32 = mybir.dt.float32
F32R = mybir.dt.float32r
I32 = mybir.dt.int32
ALU = mybir.AluOpType
ACT = mybir.ActivationFunctionType
AX = mybir.AxisListType

P = 128
D = 1024
KC = D // P
SEQ = 1024
NSEQ, QN = 8, 4
NS = NSEQ * QN
T = SEQ + NS
TPAD = SEQ + 128
PT = SEQ // P
NB, BW = 3, T // 3
H = 4
DH = 128
W = H * DH
QKV = 3 * W
CA = QKV // P
TA = 4
DFF = 2816
CF = DFF // P
TF = 3
PAST, PAGE = 256, 128
PAGES = PAST // PAGE
BUCKETS, MAXD = 32, 128
EPS = 1e-6
LAM0 = 0.8 - 0.6 * math.exp(-0.3 * 0)
NEG = -1e30
C_BA = QKV + W
C_Q = C_BA + 2 * H
C_K, C_V = C_Q + W, C_Q + 2 * W
C_GA = C_Q + 3 * W
C_GB = C_GA + D
LEVELS = 7
SLEVELS = 2
MLO, ML = -(PAST + QN - 1), 388
RSQRT_MAGIC = float(0x5F3759DF)
RSQRT_LINKS = 11


def rel_buckets():
    rel = -(MLO + np.arange(ML))
    n = np.maximum(rel, 0)
    half = BUCKETS // 2
    nf = np.maximum(n, 1).astype(np.float32)
    large = half + (np.log(nf / np.float32(half)) / np.float32(math.log(MAXD / half)) * (BUCKETS - half)).astype(np.int32)
    return rel, np.where(n < half, n, np.minimum(large, BUCKETS - 1))


def constants():
    i = np.arange(P)[:, None]
    j = np.arange(P)[None, :]
    blk = (i // QN == j // QN) & (i < NS) & (j < NS)
    parts = {"ident": i == j, "ones": i >= 0 * j, "triu": i <= j, "neglow": -1.0 * (j < i)}
    for b in range(LEVELS):
        low = (i >> (b + 1) == j >> (b + 1)) & (i >> b & 1 == 1) & (j >> b & 1 == 0)
        parts[f"low{b}"], parts[f"up{b}"] = low, low.T
    parts["s_triu"] = (blk & (i <= j))[:, :NS]
    parts["s_same"] = blk[:, :NS]
    parts["s_neglow"] = (-1.0 * (blk & (j < i)))[:, :NS]
    parts["s_seq"] = (i // QN == np.arange(NSEQ)[None, :]) & (i < NS)
    rel, bucket = rel_buckets()
    hot = np.zeros((P, ML), np.float32)
    seen = np.nonzero(rel >= 0)[0]
    hot[bucket[seen], seen] = 8.0
    hot[BUCKETS - 1, seen] -= 8.0
    hot[BUCKETS, rel < 0] = 8.0
    parts["hot"] = hot
    h, m, q = i // 8 % 4, i // 4 % 2, i % 4
    parts["m0"], parts["m1"] = m == 0, m == 1
    parts["spread"] = (j // 8 % 4 == i // QN) & (j % 4 == i % QN) & (i < 4 * QN)
    parts["s_cross"] = np.concatenate(
        [np.where(i // 32 + 4 * g == np.arange(NSEQ)[None, :], 0.0, 8 * NEG) for g in range(2)], 1)
    at, cols, n = {}, [], 0
    for name, a in parts.items():
        a = np.broadcast_to(a, (P, a.shape[1])).astype(np.float32)
        at[name] = (n, n + a.shape[1])
        cols.append(a)
        n += a.shape[1]
    return np.ascontiguousarray(np.concatenate(cols, 1)), at


CONSTS, CONST_AT = constants()


class Links:

    def __init__(self, eng, sem, base=0):
        self.eng, self.sem, self.base, self.n = eng, sem, base, 0

    def __call__(self, ins):
        self.n += 1
        ins.then_inc(self.sem, 1)
        self.eng.wait_ge(self.sem, self.base + self.n)


def loop(eng, n, body):
    body(0, True)
    with eng.Fori(1, n) as i:
        body(i, False)


def at(i, n=1):
    return bass.ds(i, n)


def over(ap, n):
    return ap.unsqueeze(2).to_broadcast([ap.shape[0], ap.shape[1], n])


def repeat(ap, n):
    return ap.unsqueeze(1).to_broadcast([ap.shape[0], n, ap.shape[1]])


def hd(ap, h=H):
    return ap.rearrange("p (h n) -> p h n", h=h)


def rsqrt(dve, link, out, x, work):
    link(dve.tensor_scalar(work.bitcast(I32), x.bitcast(I32), 1, None, ALU.logical_shift_right))
    link(dve.tensor_scalar(out.bitcast(I32), work.bitcast(I32), -1.0, RSQRT_MAGIC, ALU.mult, ALU.add))
    for _ in range(3):
        link(dve.scalar_tensor_tensor(work, out, -0.5, out, ALU.mult, ALU.mult))
        link(dve.tensor_tensor(work, work, x, ALU.mult))
        link(dve.scalar_tensor_tensor(out, work, 1.5, out, ALU.add, ALU.mult))


def hold(eng, sem, value, held):
    eng.wait_ge(sem, value)
    eng.sem_inc(held, 1)


SBUF = 16512
M_END = 212800
ROW = T * 4
M_CONST = 0
M_SMALL = 11776
M_H = 12800
M_QKV = M_H + 2 * KC * TPAD * 4
M_Z = M_QKV + 2 * H * ROW + (PT + 1) * W * 4
M_OA = M_Z + H * ROW
M_OB = M_OA + 2 * H * ROW
M_BIAS = M_END - 5536
M_MIX = M_H
M_U = M_MIX + 2 * KC * ROW
UPART = (6, 6, 5, 5)
M_X1 = M_U + 2 * max(UPART) * ROW
M_FFN = M_X1 + KC * ROW


class Core:

    def __init__(self, nc, dram):
        self.nc, self.d, self.sems = nc, dram, []

    def put(self, name, shape, offset, dt=F32):
        return self.nc.alloc_sbuf_tensor_at(name, shape, dt, offset=SBUF + offset)

    def area(self, pre, offset, end):
        at = [offset]

        def sb(name, shape, dt=F32):
            t = self.put(f"{pre}_{name}", shape, at[0], dt)
            at[0] += -(-int(np.prod(shape[1:])) * 4 // 32) * 32
            assert at[0] <= end, (pre, name, at[0], end)
            return t

        return sb

    def ps(self, ctx, name, banks=1):
        shape = [P, 512] if banks == 1 else [P, banks, 512]
        return ctx.enter_context(self.nc.psum_tensor(name, shape, F32))

    def sem(self, name):
        self.sems.append(self.nc.alloc_semaphore(name=name))
        return self.sems[-1]

    def clear(self):
        self.nc.clear_and_free_semaphores(self.sems)
        self.sems = []
        self.nc.all_engine_barrier()

    def c(self, name, n=P):
        a, b = CONST_AT[name]
        return self.const[0:n, a:b]


def load_stage(k):
    nc, d = k.nc, k.d
    sb = k.area("ld", M_H, M_BIAS)
    with ExitStack() as ctx:
        sem = lambda n: k.sem(n)
        const_in, small_in, bias_rows_out, bias_in = (
            sem(n) for n in ("const_in", "small_in", "bias_rows_out", "bias_in"))
        table_ready, rows_done, rows_sb, steps, lam_e, b16_done, b16_sb = (
            sem(n) for n in ("table_ready", "rows_done", "rows_sb", "ld_steps", "lam_e", "b16_done", "b16_sb"))
        rel = sb("rel", [BUCKETS + 1, H])
        relb = sb("relb", [BUCKETS + 1, H, P])
        lams = sb("lams", [P, 4, 64])
        prod = sb("prod", [P, 2, 64])
        dots = sb("dots", [P, 2])
        rows = sb("rows", [P, H, ML])
        b16 = sb("b16", [4 * QN, PAST + QN])
        prow = [k.ps(ctx, f"prow{h}") for h in range(H)]
        p16 = k.ps(ctx, "p16")
        scratch = nc.dram_tensor("bias_rows", (H, P, ML), F32, kind="Internal").ap()
        block = ctx.enter_context(nc.Block())

        @block.sync
        def _(sp):
            sp.dma_start(k.const[:, :], d["consts"]).then_inc(const_in, 16)

        @block.scalar
        def _(act):
            act.dma_start(rel[0:BUCKETS, :], d["rel_bias"]).then_inc(small_in, 16)
            for n, name in enumerate(("lam_q1", "lam_k1", "lam_q2", "lam_k2")):
                act.dma_start(lams[:, n, :], d[name].partition_broadcast(P).rearrange("p a n -> p (a n)")).then_inc(small_in, 16)
            for buf, name in ((k.qw, "qnorm_b"), (k.kw, "knorm_b"), (k.alog, "a_log"), (k.dtb, "dt_bias")):
                act.dma_start(buf[:, :], d[name].partition_broadcast(P).rearrange("p a n -> p (a n)")).then_inc(small_in, 16)
            with nc.allow_non_contiguous_dma(reason="a few columns"):
                act.dma_start(k.wmix[:, :], d["norm_mix"].rearrange("a (c p) -> p (a c)", p=P)).then_inc(small_in, 16)
                act.dma_start(k.wffn[:, :], d["norm_ffn"].rearrange("a (c p) -> p (a c)", p=P)).then_inc(small_in, 16)
                act.dma_start(k.onorm[:, :], d["onorm_a"].rearrange("a (c p) -> p (a c)", p=P)).then_inc(small_in, 16)
                act.dma_start(k.subln[:, :], d["subln_b"].rearrange("a (c p) -> p (a c)", p=P)).then_inc(small_in, 16)
            act.wait_ge(small_in, 16 * 13)
            act.wait_ge(steps, 4)
            act.activation(dots[:, :], dots[:, :], ACT.Exp).then_inc(lam_e, 1)
            for h in range(H):
                act.wait_ge(rows_done, h + 1)
                act.activation(rows[:, h, :], prow[h][:, 0:ML], ACT.Copy).then_inc(rows_sb, 1)
            for h in range(H):
                act.wait_ge(rows_sb, H)
                act.dma_start(scratch[h], rows[:, h, :]).then_inc(bias_rows_out, 16)
            act.wait_ge(bias_rows_out, 16 * H)
            with nc.allow_non_contiguous_dma(reason="a skewed read"):
                for h in range(H):
                    skew = bass.AP(scratch.tensor, h * P * ML + (-P - MLO), [[ML - 1, P], [1, 2 * P]])
                    act.dma_start(k.bias[:, h, :], skew).then_inc(bias_in, 16)
                for h in range(H):
                    skew = bass.AP(scratch.tensor, h * P * ML + (-PAST - MLO), [[ML - 1, QN], [1, PAST + QN]])
                    act.dma_start(b16[QN * h:QN * h + QN, :], skew).then_inc(bias_in, 16)
            act.wait_ge(bias_in, 16 * 2 * H)
            act.wait_ge(b16_done, 1)
            act.activation(k.sbias[:, :], p16[:, 0:PAST + QN], ACT.Copy).then_inc(b16_sb, 1)

        @block.vector
        def _(dve):
            link = Links(dve, steps)
            link(dve.memset(rel[BUCKETS:BUCKETS + 1, :], NEG))
            dve.wait_ge(small_in, 16 * 13)
            link(dve.tensor_tensor(prod[:, :, :], lams[:, 0:4:2, :], lams[:, 1:4:2, :], ALU.mult))
            link(dve.tensor_reduce(dots[:, :], prod[:, :, :], AX.X, ALU.add))
            link(dve.tensor_copy(relb[:, :, :], over(rel[:, :], P)))
            dve.wait_ge(lam_e, 1)
            link(dve.scalar_tensor_tensor(k.lam[:, :], dots[:, 1:2], -1.0, dots[:, 0:1], ALU.mult, ALU.add))
            link(dve.tensor_scalar(k.lam[:, :], k.lam[:, :], LAM0, None, ALU.add))
            link(dve.tensor_scalar(k.subln[:, :], k.subln[:, :], 1.0 - LAM0, None, ALU.mult))

        @block.tensor
        def _(pe):
            pe.wait_ge(const_in, 16)
            pe.wait_ge(steps, 4)
            for h in range(H):
                pe.matmul(prow[h][:, 0:ML], relb[:, h, :], k.c("hot", BUCKETS + 1), start=True, stop=True).then_inc(rows_done, 1)
            pe.wait_ge(bias_in, 16 * 2 * H)
            pe.matmul(p16[:, 0:PAST + QN], k.c("spread", 4 * QN), b16[:, :], start=True, stop=True).then_inc(b16_done, 1)


def loop3(eng, n, body):
    body(0, True, n == 1)
    if n > 2:
        with eng.Fori(1, n - 1) as i:
            body(i, False, False)
    if n > 1:
        body(n - 1, False, True)


def flat(ap):
    return ap.rearrange("p a n -> p (a n)")


class Stream:

    def __init__(self, k, pre, sb, used):
        self.raw, self.hi, self.lo = ([sb(f"{s}{u}", [P, KC, P], dt) for u in range(2)]
                                      for s, dt in (("raw", F32), ("hi", F32R), ("lo", F32R)))
        self.raw_in, self.hi_ready, self.lo_ready = ([k.sem(f"{pre}_{s}{u}") for u in range(2)]
                                                     for s in ("raw_in", "hi_ready", "lo_ready"))
        self.sp_held = k.sem(f"{pre}_sp_held")
        self.used = used

    def load(self, sp, u, i, src, first):
        if not first:
            hold(sp, self.lo_ready[u], i, self.sp_held)
        sp.dma_start(self.raw[u][:, 0:src.shape[1], :], src).then_inc(self.raw_in[u], 16)

    def high(self, act, u, i, kc, first):
        act.wait_ge(self.raw_in[u], 16 * i + 16)
        if not first:
            act.wait_ge(self.used[u], i)
        act.activation(self.hi[u][:, 0:kc, :], self.raw[u][:, 0:kc, :], ACT.Copy).then_inc(self.hi_ready[u], 1)

    def low(self, dve, u, i, kc):
        dve.wait_ge(self.hi_ready[u], i + 1)
        dve.tensor_tensor(self.lo[u][:, 0:kc, :], self.raw[u][:, 0:kc, :], self.hi[u][:, 0:kc, :].bitcast(F32),
                          ALU.subtract).then_inc(self.lo_ready[u], 1)

    def multiply(self, pe, u, i, ps, actH, actL, kc):
        pe.wait_ge(self.lo_ready[u], i + 1)
        for b in range(NB):
            cols = slice(b * BW, (b + 1) * BW)
            for c in range(kc):
                three(pe, ps[:, b, 0:BW], (self.hi[u][:, c, :], self.lo[u][:, c, :]), (actH[:, c, cols], actL[:, c, cols]),
                      c == 0, c == kc - 1, self.used[u] if b == NB - 1 else None)


def three(pe, out, w, a, start, stop, done=None):
    pe.matmul(out, w[0], a[0], start=start, stop=False)
    pe.matmul(out, w[0], a[1], start=False, stop=False)
    ins = pe.matmul(out, w[1], a[0], start=False, stop=stop)
    if stop and done is not None:
        ins.then_inc(done, 1)


def turn_stage(k):
    nc, d = k.nc, k.d
    with ExitStack() as ctx:
        sem = lambda n: k.sem(f"tx_{n}")
        x_in = [sem(f"x_in{u}") for u in range(2)]
        turned, stored, spilled = (sem(s) for s in ("turned", "stored", "spilled"))
        x = k.put("tx_x", [P, 2, D], M_QKV + KC * ROW)
        pt = k.ps(ctx, "tx_pt", 4)
        block = ctx.enter_context(nc.Block())
        n_of = lambda t: P if t < PT else NS

        @block.sync
        def _(sp):
            for t in range(PT + 1):
                if t >= 2:
                    sp.wait_ge(turned, t - 1)
                src = d["x_prompt"][0, t * P:t * P + P, :] if t < PT else d["x_sample"].rearrange("b q n -> (b q) n")
                sp.dma_start(x[0:n_of(t), t % 2, :], src).then_inc(x_in[t % 2], 16)
            sp.wait_ge(stored, 2 * (PT + 1))
            sp.dma_start(k.xT_dram.rearrange("c p n -> p c n"), k.xT[:, :, :]).then_inc(spilled, 16)
            sp.wait_ge(spilled, 16)

        @block.tensor
        def _(pe):
            for t in range(PT + 1):
                n = n_of(t)
                pe.wait_ge(x_in[t % 2], 16 * (t // 2 + 1))
                if t >= 2:
                    pe.wait_ge(stored, 2 * (t - 1))
                for c in range(KC):
                    ins = pe.transpose(pt[:, 2 * (t % 2) + c // 4, c % 4 * P:c % 4 * P + n], x[0:n, t % 2, c * P:c * P + P], k.c("ident", n)[:, 0:n])
                ins.then_inc(turned, 1)

        def store(eng, copy, half):
            for t in range(PT + 1):
                n = n_of(t)
                eng.wait_ge(turned, t + 1)
                if t:
                    eng.wait_ge(stored, 2 * t)
                copy(k.xT[:, 4 * half:4 * half + 4, t * P:t * P + n], hd(pt[:, 2 * (t % 2) + half, :])[:, :, 0:n]).then_inc(stored, 1)

        @block.scalar
        def _(act):
            store(act, lambda o, i: act.activation(o, i, ACT.Copy), 0)

        @block.vector
        def _(dve):
            store(dve, lambda o, i: dve.tensor_copy(o, i), 1)


def norm_stage(k, pre, xT, weight, hH, hL, sb, pad):
    nc = k.nc
    with ExitStack() as ctx:
        sem = lambda n: k.sem(f"{pre}_{n}")
        squared, summed, steps, rooted, scaled, high, low, low_pool, padded = (
            sem(n) for n in ("squared", "summed", "steps", "rooted", "scaled", "high", "low", "low_pool", "padded"))
        sq = sb("sq", [P, 2, T])
        rb = sb("rb", [P, T])
        ps = k.ps(ctx, f"{pre}_ps", 3)
        block = ctx.enter_context(nc.Block())
        banks = lambda ap: ap.rearrange("p (b n) -> p b n", b=NB)

        @block.scalar
        def _(act):
            for c in range(KC):
                if c >= 2:
                    act.wait_ge(summed, c - 1)
                act.activation(sq[:, c % 2, :], xT[:, c, :], ACT.Square).then_inc(squared, 1)
            act.wait_ge(steps, 1)
            act.activation(rb[:, :], rb[:, :], ACT.Sqrt).then_inc(rooted, 1)
            for c in range(KC):
                act.wait_ge(scaled, c + 1)
                act.activation(hH[:, c, 0:T], sq[:, c % 2, :], ACT.Copy).then_inc(high, 1)

        @block.tensor
        def _(pe):
            for c in range(KC):
                pe.wait_ge(squared, c + 1)
                for b in range(NB):
                    ins = pe.matmul(ps[:, b, 0:BW], k.c("ones"), sq[:, c % 2, b * BW:(b + 1) * BW], start=(c == 0), stop=(c == KC - 1))
                ins.then_inc(summed, 1)

        @block.gpsimd
        def _(pool):
            if pad:
                for buf in (hH, hL):
                    pool.memset(buf[:, :, T:TPAD].bitcast(F32), 0.0).then_inc(padded, 1)
            for c in range(1, KC, 2):
                pool.wait_ge(high, c + 1)
                pool.tensor_tensor(hL[:, c, 0:T], sq[:, 1, :], hH[:, c, 0:T].bitcast(F32), ALU.subtract).then_inc(low_pool, 1)

        @block.vector
        def _(dve):
            link = Links(dve, steps)
            dve.wait_ge(summed, KC)
            link(dve.tensor_scalar(banks(rb[:, :]), ps[:, :, 0:BW], 1.0 / D, EPS, ALU.mult, ALU.add))
            dve.wait_ge(rooted, 1)
            link(dve.reciprocal(rb[:, :], rb[:, :]))

            def lower(c):
                dve.wait_ge(high, c + 1)
                dve.tensor_tensor(hL[:, c, 0:T], sq[:, 0, :], hH[:, c, 0:T].bitcast(F32), ALU.subtract).then_inc(low, 1)

            for c in range(KC):
                if c >= 2:
                    dve.wait_ge(*((low_pool, c // 2) if c % 2 else (low, c // 2)))
                dve.scalar_tensor_tensor(sq[:, c % 2, :], xT[:, c, :], weight[:, c:c + 1], rb[:, :], ALU.mult, ALU.mult).then_inc(scaled, 1)
                if c % 2:
                    lower(c - 1)


def conv_proj_stage(k):
    nc, d = k.nc, k.d
    R = TA - 1
    RAW = R + SEQ + NSEQ * (R + QN)
    OUT = RAW - R
    NH = NSEQ * R
    LAST = R + NSEQ * R
    with ExitStack() as ctx:
        sem = lambda n: k.sem(f"cv_{n}")
        proj_done = [sem(f"proj{u}") for u in range(2)]
        evac_done = [sem(f"evac{u}") for u in range(2)]
        conv_done = [sem(f"conv{u}") for u in range(2)]
        act_done = [sem(f"silu{u}") for u in range(2)]
        rows_out = [sem(f"rows_out{u}") for u in range(2)]
        saved, taps_in, taps_turned, taps_sb, zeroed, last_turned, last_sb, last_out, chain, pool_held = (
            sem(n) for n in ("saved", "taps_in", "taps_turned", "taps_sb", "zeroed", "last_turned", "last_sb", "last_out", "chain", "pool_held"))
        sb = k.area("cv", M_OA, M_BIAS)
        w = Stream(k, "cv", sb, proj_done)
        raw = [sb(f"conv_in{u}", [P, RAW]) for u in range(2)]
        acc = [sb(f"acc{u}", [P, RAW]) for u in range(2)]
        nat = sb("nat", [NH + TA, QKV])
        taps = sb("taps", [P, CA, NH + TA])
        last = sb("last", [P, CA, LAST])
        ps = [k.ps(ctx, f"cv_ps{u}", 3) for u in range(2)]
        pt = k.ps(ctx, "cv_pt", 2)
        samp = [raw[u][:, R + SEQ:RAW].rearrange("p (s c) -> p s c", s=NSEQ) for u in range(2)]
        samp_out = [acc[u][:, R + SEQ:RAW].rearrange("p (s c) -> p s c", s=NSEQ) for u in range(2)]
        w_cols = d["w_in"].rearrange("a (c p) n -> p (a c) n", p=P)
        rows = k.qkvT_dram.rearrange("c p n -> p c n")
        NPAIR = (CA + H) // 2
        CPAIR = CA // 2
        block = ctx.enter_context(nc.Block())

        @block.sync
        def _(sp):
            sp.dma_start(nat[0:NH, :], d["state_conv_a"].rearrange("a s r n -> (a s r) n")).then_inc(taps_in, 16)
            sp.dma_start(nat[NH:NH + TA, :], d["conv_a"].rearrange("a w n -> (a w) n")).then_inc(taps_in, 16)
            for u in range(2):
                w.load(sp, u, 0, w_cols[:, :, u * P:u * P + P], True)

            def step(i, first, last_step):
                for u in range(2):
                    if not last_step:
                        w.load(sp, u, i + 1, w_cols[:, :, at((2 * i + 2 + u) * P, P)], False)

            def out(i):
                for u in range(2):
                    hold(sp, act_done[u], i + 1, w.sp_held)
                    c = 2 * i + u
                    sp.dma_start(flat(rows[:, at(c), 0:SEQ]), acc[u][:, 0:SEQ]).then_inc(rows_out[u], 16)
                    sp.dma_start(rows[:, at(c), SEQ:T].rearrange("p a (s c) -> p (a s) c", s=NSEQ),
                                 samp_out[u][:, :, 0:QN]).then_inc(rows_out[u], 16)

            def both(i, first):
                step(i, first, False)
                out(i)

            loop(sp, CPAIR, both)
            step(CPAIR, False, False)
            for u in range(2):
                sp.wait_ge(rows_out[u], 32 * CPAIR)
            sp.wait_ge(last_sb, 3)
            sp.dma_start(d["conv_a_prompt"].rearrange("a b r n -> (a b r) n"), nat[0:R, :]).then_inc(last_out, 16)
            sp.dma_start(d["conv_a_sample"].rearrange("a s r n -> (a s r) n"), nat[R:LAST, :]).then_inc(last_out, 16)
            sp.wait_ge(last_out, 32)

        @block.tensor
        def _(pe):
            pe.wait_ge(taps_in, 32)
            for c in range(CA):
                if c >= 2:
                    pe.wait_ge(taps_sb, c - 1)
                pe.transpose(pt[:, c % 2, 0:NH + TA], nat[:, c * P:(c + 1) * P], k.c("ident", NH + TA)[:, 0:NH + TA]).then_inc(taps_turned, 1)

            def chunks(i, first):
                for u in range(2):
                    if not first:
                        pe.wait_ge(evac_done[u], i)
                    w.multiply(pe, u, i, ps[u], k.hH, k.hL, KC)

            loop(pe, NPAIR, chunks)
            pe.wait_ge(saved, 2 * CA)
            for c in range(CA):
                if c >= 8:
                    pe.wait_ge(last_sb, 1)
                ins = pe.transpose(pt[0:LAST, c // 4 % 2, c % 4 * P:c % 4 * P + P], last[:, c, :], k.c("ident"))
                if c % 4 == 3:
                    ins.then_inc(last_turned, 1)

        @block.scalar
        def _(act):
            for u in range(2):
                w.high(act, u, 0, KC, True)

            def conv(i, first, final):
                for u in range(2):
                    act.wait_ge(proj_done[u], i + 1)
                    w.high(act, u, i + 1, KC, False)
                    if not first:
                        act.wait_ge(conv_done[u], i)
                        act.wait_ge(saved, 2 * (2 * i + u - 1))
                    for b in range(NB):
                        lo, hi = b * BW, min(SEQ, (b + 1) * BW)
                        act.activation(raw[u][:, R + lo:R + hi], ps[u][:, b, 0:hi - lo], ACT.Copy)
                    act.activation(samp[u][:, :, R:R + QN], ps[u][:, NB - 1, BW - NS:BW].rearrange("p (s c) -> p s c", s=NSEQ),
                                   ACT.Copy).then_inc(evac_done[u], 1)
                for u in range(2):
                    act.wait_ge(conv_done[u], i + 1)
                    act.activation(acc[u][:, 0:OUT], acc[u][:, 0:OUT], ACT.Silu).then_inc(act_done[u], 1)

            loop3(act, CPAIR, conv)
            for j in range(H // 2):
                i = j + CPAIR
                for u in range(2):
                    act.wait_ge(proj_done[u], i + 1)
                    if i + 1 < NPAIR:
                        w.high(act, u, i + 1, KC, False)
                    for b in range(NB):
                        ins = act.activation(k.zT[:, 2 * j + u, b * BW:(b + 1) * BW], ps[u][:, b, 0:BW], ACT.Silu)
                    ins.then_inc(evac_done[u], 1)

        @block.gpsimd
        def _(pool):
            def save(i, first):
                for u in range(2):
                    hold(pool, evac_done[u], i + 1, pool_held)
                    c = 2 * i + u
                    pool.tensor_copy(flat(last[:, at(c), 0:R]), raw[u][:, SEQ:SEQ + R]).then_inc(saved, 1)
                    pool.tensor_copy(last[:, at(c), R:LAST].rearrange("p a (s c) -> p (a s) c", s=NSEQ),
                                     samp[u][:, :, QN:QN + R]).then_inc(saved, 1)

            loop(pool, CPAIR, save)

        @block.vector
        def _(dve):
            for u in range(2):
                dve.memset(raw[u][:, 0:R], 0.0).then_inc(zeroed, 1)
                w.low(dve, u, 0, KC)
            for c in range(CA):
                dve.wait_ge(taps_turned, c + 1)
                dve.tensor_copy(taps[:, c, :], pt[:, c % 2, 0:NH + TA]).then_inc(taps_sb, 1)
            dve.wait_ge(taps_sb, CA)
            dve.wait_ge(zeroed, 2)

            def conv(i, first):
                link = Links(dve, chain, 2 * (TA + 1) * i)
                for u in range(2):
                    c = 2 * i + u
                    w.low(dve, u, i + 1, KC)
                    dve.wait_ge(evac_done[u], i + 1)
                    if not first:
                        dve.wait_ge(rows_out[u], 32 * i)
                    link(dve.tensor_copy(samp[u][:, :, 0:R], taps[:, at(c), 0:NH].rearrange("p a (s r) -> p (a s) r", s=NSEQ)))
                    link(dve.tensor_scalar(acc[u][:, 0:OUT], raw[u][:, 0:OUT], flat(taps[:, at(c), NH:NH + 1]), None, ALU.mult))
                    for t in range(1, TA):
                        link(dve.scalar_tensor_tensor(acc[u][:, 0:OUT], raw[u][:, t:t + OUT], flat(taps[:, at(c), NH + t:NH + t + 1]),
                                                      acc[u][:, 0:OUT], ALU.mult, ALU.add))
                    dve.sem_inc(conv_done[u], 1)

            loop(dve, CPAIR, conv)
            for u in range(2):
                w.low(dve, u, CPAIR + 1, KC)
            for g in range(CA // 4):
                dve.wait_ge(last_turned, g + 1)
                dve.tensor_copy(nat[0:LAST, g * W:(g + 1) * W], pt[0:LAST, g % 2, :]).then_inc(last_sb, 1)


def gate_proj_stage(k):
    nc, d = k.nc, k.d
    with ExitStack() as ctx:
        sem = lambda n: k.sem(f"gp_{n}")
        proj_done = [sem(f"proj{u}") for u in range(2)]
        evac_done = [sem(f"evac{u}") for u in range(2)]
        rows_out = [sem(f"rows_out{u}") for u in range(2)]
        sb = k.area("gp", M_OA, M_BIAS)
        w = Stream(k, "gp", sb, proj_done)
        sig = [sb(f"sig{u}", [P, T]) for u in range(2)]
        ps = [k.ps(ctx, f"gp_ps{u}", 3) for u in range(2)]
        w_cols = d["w_in"].rearrange("a (c p) n -> p (a c) n", p=P)
        rows = k.gate_dram.rearrange("c p n -> p c n")
        block = ctx.enter_context(nc.Block())

        @block.sync
        def _(sp):
            for u in range(2):
                w.load(sp, u, 0, w_cols[:, :, C_GA + u * D:C_GA + u * D + P], True)

            def step(i, first, final):
                if not final:
                    for u in range(2):
                        w.load(sp, u, i + 1, w_cols[:, :, at(i * P + (C_GA + u * D + P), P)], False)
                for u in range(2):
                    hold(sp, evac_done[u], i + 1, w.sp_held)
                    sp.dma_start(flat(rows[:, at(i + u * KC), :]), sig[u][:, :]).then_inc(rows_out[u], 16)

            loop3(sp, KC, step)
            for u in range(2):
                sp.wait_ge(rows_out[u], 16 * KC)

        @block.tensor
        def _(pe):
            def step(i, first):
                for u in range(2):
                    if not first:
                        pe.wait_ge(evac_done[u], i)
                    w.multiply(pe, u, i, ps[u], k.hH, k.hL, KC)

            loop(pe, KC, step)

        @block.scalar
        def _(act):
            for u in range(2):
                w.high(act, u, 0, KC, True)

            def step(i, first, final):
                for u in range(2):
                    act.wait_ge(proj_done[u], i + 1)
                    if not final:
                        w.high(act, u, i + 1, KC, False)
                    if not first:
                        act.wait_ge(rows_out[u], 16 * i)
                    for b in range(NB):
                        ins = act.activation(sig[u][:, b * BW:(b + 1) * BW], ps[u][:, b, 0:BW], ACT.Sigmoid)
                    ins.then_inc(evac_done[u], 1)

            loop3(act, KC, step)

        @block.vector
        def _(dve):
            for u in range(2):
                w.low(dve, u, 0, KC)

            def step(i):
                for u in range(2):
                    w.low(dve, u, i, KC)

            with dve.Fori(1, KC) as i:
                step(i)


def gates_stage(k):
    nc, d = k.nc, k.d
    with ExitStack() as ctx:
        sem = lambda n: k.sem(f"gt_{n}")
        w_loaded, proj_done, steps, acts = (sem(n) for n in ("w_loaded", "proj", "steps", "acts"))
        sb = k.area("gt", M_OA, M_BIAS)
        wb = sb("w", [P, KC, 2 * H])
        wH, wL = (sb(s, [P, KC, 2 * H], F32R) for s in ("wH", "wL"))
        split = sem("split")
        ba = sb("ba", [P, PT + 1, 2 * H])
        th, aa, mod = (sb(s, [P, PT + 1, H]) for s in ("th", "aa", "mod"))
        ps = k.ps(ctx, "gt_ps")
        psv = ps[:, 0:(PT + 1) * 2 * H].rearrange("p (t n) -> p t n", t=PT + 1)
        block = ctx.enter_context(nc.Block())

        @block.sync
        def _(sp):
            sp.dma_start(wb[:, :, :], d["w_in"].rearrange("a (c p) n -> p (a c) n", p=P)[:, :, C_BA:C_BA + 2 * H]).then_inc(w_loaded, 16)

        @block.tensor
        def _(pe):
            pe.wait_ge(split, 2)
            for t in range(PT + 1):
                cols = slice(t * P, t * P + P)
                for c in range(KC):
                    three(pe, psv[:, t, :], (k.hH[:, c, cols], k.hL[:, c, cols]), (wH[:, c, :], wL[:, c, :]), c == 0, c == KC - 1,
                          proj_done if t == PT else None)

        @block.scalar
        def _(act):
            act.wait_ge(steps, 1)
            act.activation(th[:, :, :], ba[:, :, 0:H], ACT.Tanh, scale=0.5).then_inc(acts, 1)
            act.activation(k.alog[:, :], k.alog[:, :], ACT.Exp).then_inc(acts, 1)
            act.wait_ge(steps, 4)
            act.activation(mod[:, :, :], mod[:, :, :], ACT.Exp, scale=-1.0).then_inc(acts, 1)
            act.wait_ge(acts, 3)
            act.activation(mod[:, :, :], mod[:, :, :], ACT.Ln, bias=1.0).then_inc(acts, 1)

        @block.vector
        def _(dve):
            link = Links(dve, steps)
            dve.wait_ge(w_loaded, 16)
            dve.tensor_copy(wH[:, :, :], wb[:, :, :]).then_inc(split, 1)
            dve.wait_ge(split, 1)
            dve.tensor_tensor(wL[:, :, :], wb[:, :, :], wH[:, :, :].bitcast(F32), ALU.subtract).then_inc(split, 1)
            dve.wait_ge(proj_done, 1)
            link(dve.tensor_copy(ba[:, :, :], psv[:, :, :]))
            link(dve.tensor_tensor(aa[:, :, :], ba[:, :, H:2 * H], repeat(k.dtb[:, :], PT + 1), ALU.add))
            link(dve.tensor_scalar(mod[:, :, :], aa[:, :, :], -1.0, None, ALU.mult))
            link(dve.tensor_tensor(mod[:, :, :], mod[:, :, :], aa[:, :, :], ALU.max))
            dve.wait_ge(acts, 4)
            link(dve.tensor_scalar(k.beta[:, :, :], th[:, :, :], 0.5, 0.5, ALU.mult, ALU.add))
            link(dve.scalar_tensor_tensor(mod[:, :, :], aa[:, :, :], 0.0, mod[:, :, :], ALU.max, ALU.add))
            link(dve.tensor_tensor(mod[:, :, :], mod[:, :, :], repeat(k.alog[:, :], PT + 1), ALU.mult))
            link(dve.tensor_scalar(k.g[:, :, :], mod[:, :, :], -1.0, None, ALU.mult))


def delta_stage(k, sample):
    nc, d = k.nc, k.d
    pre = "ds" if sample else "dp"
    n = NS if sample else P
    levels = SLEVELS if sample else LEVELS
    steps = 1 if sample else PT
    HN = H * n
    tri, neglow = ("s_triu", "s_neglow") if sample else ("triu", "neglow")
    tot = "s_same" if sample else "ones"
    with ExitStack() as ctx:
        sem = lambda s: k.sem(f"{pre}_{s}")
        (staged, gb_staged, identity_set, raw_turned, sums_done, gp_ready, row_done, gc_done, negd_ready, kdx_ready, exps_done,
         masks_done, qk_scaled, kv_scaled, qk_turned, qkT_ready, qg_ready, kk_done, m_ready, a_ready, x_done,
         xs_ready, zu_done, zl_done, level_done, w_done, w_ready, v_done, v_ready, o_done, su_done, s_ready,
         osum_done, o_scaled, o_turned, out_ready, chain, pchain, achain, upd_done, state_in, state_out, held, pool_held) = (sem(s) for s in (
             "staged", "gb_staged", "identity_set", "raw_turned", "sums", "gp", "row", "gc", "negd", "kdx", "exps", "masks",
             "qk_scaled", "kv_scaled", "qk_turned", "qkT", "qg", "kk", "m", "a", "x", "xs", "zu", "zl", "level",
             "w", "w_ready", "v", "v_ready", "o", "su", "s", "osum", "o_scaled", "o_turned", "out", "chain",
             "pchain", "achain", "upd", "state_in", "state_out", "held", "pool_held"))
        sb = k.area(pre, M_H, M_QKV)
        stage_in = sem("stage_in")
        on_split = sem("on_split")
        stage = sb("stage", [P, CA, n])
        gb = sb("gb", [n, 2 * H])
        gp = sb("gp", [n, HN])
        gcs = sb("gcs", [n, 2 * H])
        kdx, eg, ekd, nbe = (sb(s, [n, H]) for s in ("kdx", "eg", "ekd", "nbe"))
        negd, es, esl, esu = (sb(s, [n, HN]) for s in ("negd", "es", "esl", "esu"))
        er = sb("er", [P, HN])
        ss, r, work = (sb(s, [n, 2 * H]) for s in ("ss", "r", "work"))
        junk = sb("junk", [P, 2, P])
        qn, kn, vb, kbg, kd = (sb(s, [n, W]) for s in ("qn", "kn", "vb", "kbg", "kd"))
        qT, kT, qgT, wT = (sb(s, [P, HN]) for s in ("qT", "kT", "qgT", "wT"))
        m, aT, U, L, xs = (sb(s, [n, HN]) for s in ("m", "aT", "U", "L", "xs"))
        vn = sb("vn", [n, W])
        B = [k.ps(ctx, f"{pre}_b{i}") for i in range(8)]
        S = sb("S", [P, NSEQ * H if sample else H, DH])
        egl = sb("egl", [P, NSEQ * H if sample else H])
        if sample:
            gm = sb("gm", [n, NSEQ, H])
            uT, vnT, oT, sq = (sb(s, [P, HN]) for s in ("uT", "vnT", "oT", "sq"))
            rT, workT = (sb(s, [P, HN]) for s in ("rT", "workT"))
            vm = sb("vm", [n, H, NSEQ * DH])
        else:
            on = sb("on", [n, W])
            so, ro, worko = (sb(s, [n, H]) for s in ("so", "ro", "worko"))
        ident = k.c("ident")
        block = ctx.enter_context(nc.Block())

        def tiles(eng, body):
            if sample:
                body(PT, 0, True)
            else:
                body(0, 0, True)
                with eng.Fori(1, steps) as t:
                    body(t, t, False)

        def cols(t):
            return at(t * P, n)

        @block.sync
        def _(sp):
            rows = k.qkvT_dram.rearrange("c p n -> p c n")

            def stage_load(t, i, first):
                if not first:
                    hold(sp, raw_turned, i, staged)
                sp.dma_start(stage[:, :, :], rows[:, :, cols(t)]).then_inc(stage_in, 16)

            tiles(sp, stage_load)
            if sample:
                sp.dma_start(S[:, :, :], d["state_delta"].rearrange("a s h p n -> p (a s h) n")).then_inc(state_in, 16)
                sp.wait_ge(s_ready, 1)
                sp.dma_start(d["delta_sample"].rearrange("a s h p n -> p (a s h) n"), S[:, :, :]).then_inc(state_out, 16)
            else:
                sp.wait_ge(s_ready, steps)
                sp.dma_start(d["delta_prompt"].rearrange("a b h p n -> p (a b h) n"), S[:, :, :]).then_inc(state_out, 16)
            sp.wait_ge(state_out, 16)

        @block.gpsimd
        def _(pool):
            def tile(t, i, first):
                if not first:
                    pool.wait_ge(kv_scaled, i)
                    hold(pool, gc_done, i, pool_held)
                pool.tensor_copy(gb[:, 0:H], k.g[0:n, at(t), :].rearrange("p a n -> p (a n)")).then_inc(gb_staged, 1)
                pool.tensor_copy(gb[:, H:2 * H], k.beta[0:n, at(t), :].rearrange("p a n -> p (a n)")).then_inc(gb_staged, 1)
                if not first:
                    hold(pool, v_done, i, pool_held)
                for buf in (U, L):
                    pool.tensor_copy(hd(buf[:, :]), repeat(ident[0:n, 0:n], H)).then_inc(identity_set, 1)
                pool.wait_ge(exps_done, i + 1)
                link = Links(pool, pchain, 3 * i)
                if not first:
                    pool.wait_ge(m_ready, i)
                link(pool.tensor_tensor(hd(esl[:, :]), hd(es[:, :]), repeat(k.c(neglow, n), H), ALU.mult))
                link(pool.tensor_tensor(hd(esl[:, :]), hd(esl[:, :]), over(gb[:, H:2 * H], n), ALU.mult))
                if not first:
                    pool.wait_ge(a_ready, i)
                link(pool.tensor_tensor(hd(esu[:, :]), hd(es[:, :]), repeat(k.c(tri, n), H), ALU.mult))
                pool.sem_inc(masks_done, 1)
                pool.wait_ge(qkT_ready, i + 1)
                if not first:
                    pool.wait_ge(o_done, i)
                pool.tensor_tensor(qgT[:, :], qT[:, :], er[:, :], ALU.mult).then_inc(qg_ready, 1)

            tiles(pool, tile)

        @block.tensor
        def _(pe):
            if sample:
                pe.wait_ge(state_in, 16)

            def tile(t, i, first):
                pe.wait_ge(stage_in, 16 * i + 16)
                pe.wait_ge(gb_staged, 2 * i + 2)
                if not first:
                    pe.wait_ge(level_done, (2 * levels - 1) * i)
                    pe.wait_ge(v_ready, i)
                    pe.wait_ge(out_ready, i)
                    pe.wait_ge(s_ready, i)
                for c in range(CA):
                    ins = pe.transpose(B[c // H][0:n, c % H * P:c % H * P + P], stage[:, c, :], ident)
                ins.then_inc(raw_turned, 1)
                pe.wait_ge(gp_ready, i + 1)
                pe.matmul(B[3][:, 0:HN], k.c("ones", n), gp[:, :], start=True, stop=True).then_inc(row_done, 1)
                pe.matmul(B[4][0:n, 0:H], k.c(tri, n)[:, 0:n], gb[:, 0:H], start=True, stop=True)
                ins = pe.matmul(B[4][0:n, H:2 * H], k.c(tot, n)[:, 0:n], gb[:, 0:H], start=True, stop=True)
                if sample:
                    ins = pe.matmul(B[4][:, 2 * H:2 * H + NSEQ * H], k.c("ones", n), gm[:, :, :].rearrange("p s h -> p (s h)"), start=True, stop=True)
                ins.then_inc(gc_done, 1)
                pe.wait_ge(qk_scaled, i + 1)
                for h in range(H):
                    pe.transpose(B[5][:, h * n:h * n + n], qn[:, h * P:h * P + P], ident[0:n, 0:n])
                for h in range(H):
                    ins = pe.transpose(B[6][:, h * n:h * n + n], kn[:, h * P:h * P + P], ident[0:n, 0:n])
                ins.then_inc(qk_turned, 1)
                pe.wait_ge(qkT_ready, i + 1)
                for h in range(H):
                    s = slice(h * n, h * n + n)
                    pe.matmul(B[0][0:n, s], kT[:, s], kT[:, s], start=True, stop=True)
                for h in range(H):
                    s = slice(h * n, h * n + n)
                    ins = pe.matmul(B[1][0:n, s], kT[:, s], qT[:, s], start=True, stop=True)
                ins.then_inc(kk_done, 1)
                pe.wait_ge(m_ready, i + 1)
                pe.wait_ge(kv_scaled, i + 1)
                for l in range(levels):
                    if l:
                        pe.wait_ge(level_done, (2 * levels - 1) * i + 2 * l)
                    if l == 1:
                        pe.wait_ge(a_ready, i + 1)
                    for h in range(H):
                        s = slice(h * n, h * n + n)
                        ins = pe.matmul(B[2][0:n, s], m[:, s], U[:, s] if l else ident[0:n, 0:n], start=True, stop=True)
                    ins.then_inc(x_done, 1)
                    if l:
                        pe.wait_ge(xs_ready, (levels - 1) * i + l)
                        for h in range(H):
                            s = slice(h * n, h * n + n)
                            ins = pe.matmul(B[0][0:n, s], L[:, s], xs[:, s], start=True, stop=True)
                        ins.then_inc(zu_done, 1)
                        if l < levels - 1:
                            for h in range(H):
                                s = slice(h * n, h * n + n)
                                ins = pe.matmul(B[1][0:n, s], xs[:, s], L[:, s], start=True, stop=True)
                            ins.then_inc(zl_done, 1)
                pe.wait_ge(level_done, (2 * levels - 1) * (i + 1))
                for h in range(H):
                    ins = pe.matmul(B[3][:, h * n:h * n + n], kbg[:, h * P:h * P + P], U[:, h * n:h * n + n], start=True, stop=True)
                ins.then_inc(w_done, 1)
                if not sample:
                    pe.wait_ge(w_ready, i + 1)
                    if not first:
                        pe.wait_ge(s_ready, i)
                    else:
                        pe.wait_ge(chain, 1)
                    for h in range(H):
                        s = slice(h * P, h * P + P)
                        pe.matmul(B[4][:, s], U[:, s], vb[:, s], start=True, stop=False)
                        ins = pe.matmul(B[4][:, s], wT[:, s], S[:, h, :], start=False, stop=True)
                    ins.then_inc(v_done, 1)
                    pe.wait_ge(v_ready, i + 1)
                    pe.wait_ge(qg_ready, i + 1)
                    for h in range(H):
                        s = slice(h * P, h * P + P)
                        pe.matmul(B[5][:, s], qgT[:, s], S[:, h, :], start=True, stop=False)
                        ins = pe.matmul(B[5][:, s], aT[:, s], vn[:, s], start=False, stop=True)
                    ins.then_inc(o_done, 1)
                    for h in range(H):
                        s = slice(h * P, h * P + P)
                        ins = pe.matmul(B[6][:, s], kd[:, s], vn[:, s], start=True, stop=True)
                    ins.then_inc(su_done, 1)
                    pe.wait_ge(o_scaled, i + 1)
                    for h in range(H):
                        s = slice(h * P, h * P + P)
                        ins = pe.transpose(B[7][:, s], on[:, s], ident)
                    ins.then_inc(o_turned, 1)
                else:
                    for h in range(H):
                        pe.matmul(B[7][:, h * n:h * n + n], vb[:, h * P:h * P + P], U[:, h * n:h * n + n], start=True, stop=True)
                    pe.wait_ge(w_ready, 1)
                    pe.wait_ge(qg_ready, 1)
                    for h in range(H):
                        for s in range(NSEQ):
                            c = h * n + s * QN
                            pe.matmul(B[2][:, c:c + QN], S[:, s * H + h, :], wT[:, c:c + QN], start=True, stop=True)
                            ins = pe.matmul(B[2][:, HN + c:HN + c + QN], S[:, s * H + h, :], qgT[:, c:c + QN], start=True, stop=True)
                    ins.then_inc(v_done, 1)
                    pe.wait_ge(v_ready, 1)
                    for h in range(H):
                        ins = pe.transpose(B[3][0:n, h * P:h * P + P], vnT[:, h * n:h * n + n], ident)
                    ins.then_inc(x_done, 1)
                    pe.wait_ge(v_ready, 2)
                    for h in range(H):
                        ins = pe.matmul(B[7][:, h * n:h * n + n], vn[:, h * P:h * P + P], aT[:, h * n:h * n + n], start=True, stop=True)
                    ins.then_inc(o_done, 1)
                    pe.wait_ge(o_scaled, 1)
                    pe.matmul(B[4][:, 0:HN], k.c("ones"), sq[:, :], start=True, stop=True).then_inc(o_turned, 1)
                    pe.wait_ge(v_ready, 3)
                    for h in range(H):
                        for half in range(2):
                            u = 2 * h + half
                            if u >= 2:
                                pe.wait_ge(upd_done, u - 1)
                            pe.matmul(B[5 + half][:, :], kd[:, h * P:h * P + P], vm[:, h, half * 512:half * 512 + 512],
                                      start=True, stop=True).then_inc(su_done, 1)

            tiles(pe, tile)

        @block.scalar
        def _(act):
            def tile(t, i, first):
                link = Links(act, achain, (2 * H + (0 if sample else H)) * i)
                act.wait_ge(raw_turned, i + 1)
                if not first:
                    act.wait_ge(kv_scaled, i)
                for h in range(2 * H):
                    link(act.activation(junk[0:n, 0, :], B[h // H][0:n, h % H * P:h % H * P + P], ACT.Square, accum_out=ss[:, h:h + 1]))
                act.sem_inc(sums_done, 1)
                act.wait_ge(negd_ready, i + 1)
                if not first:
                    act.wait_ge(s_ready, i)
                act.activation(er[:, :], B[3][:, 0:HN], ACT.Exp)
                act.activation(eg[:, :], B[4][0:n, 0:H], ACT.Exp)
                if sample:
                    act.activation(egl[:, :], B[4][:, 2 * H:2 * H + NSEQ * H], ACT.Exp)
                else:
                    act.activation(egl[:, :], B[4][:, H:2 * H], ACT.Exp)
                if not first:
                    act.wait_ge(masks_done, i)
                act.activation(es[:, :], negd[:, :], ACT.Exp)
                act.wait_ge(kdx_ready, i + 1)
                act.activation(ekd[:, :], kdx[:, :], ACT.Exp).then_inc(exps_done, 1)
                act.wait_ge(qk_turned, i + 1)
                act.activation(qT[:, :], B[5][:, 0:HN], ACT.Copy)
                act.activation(kT[:, :], B[6][:, 0:HN], ACT.Copy).then_inc(qkT_ready, 1)
                for l in range(1, levels):
                    act.wait_ge(x_done, levels * i + l + 1)
                    if l >= 2:
                        act.wait_ge(zl_done, (levels - 2) * i + l - 1)
                    act.activation(xs[:, :], B[2][0:n, 0:HN], ACT.Copy).then_inc(xs_ready, 1)
                act.wait_ge(w_done, i + 1)
                act.activation(wT[:, :], B[3][:, 0:HN], ACT.Copy).then_inc(w_ready, 1)
                if not sample:
                    act.wait_ge(v_done, i + 1)
                    act.activation(vn[:, :], B[4][:, :], ACT.Copy).then_inc(v_ready, 1)
                    act.wait_ge(o_done, i + 1)
                    for h in range(H):
                        link(act.activation(junk[:, 0, :], B[5][:, h * P:h * P + P], ACT.Square, accum_out=so[:, h:h + 1]))
                    act.sem_inc(osum_done, 1)

            tiles(act, tile)

        @block.vector
        def _(dve):
            pr = 0 if sample else 1
            if not sample:
                dve.memset(S[:, :, :], 0.0).then_inc(chain, 1)
            per_tile = [0]

            def tile(t, i, first):
                link = Links(dve, chain, pr + per_tile[0] * i)
                dve.wait_ge(gb_staged, 2 * i + 2)
                dve.tensor_tensor(hd(gp[:, :]), repeat(k.c(tri, n)[:, 0:n], H), over(gb[:, 0:H], n), ALU.mult)
                if sample:
                    dve.tensor_tensor(gm[:, :, :], over(k.c("s_seq", n), H), repeat(gb[:, 0:H], NSEQ), ALU.mult).then_inc(gp_ready, 1)
                else:
                    dve.tensor_scalar(nbe[:, :], gb[:, H:2 * H], -1.0, None, ALU.mult).then_inc(gp_ready, 1)
                dve.wait_ge(gc_done, i + 1)
                link(dve.tensor_copy(gcs[:, :], B[4][0:n, 0:2 * H]))
                link(dve.tensor_tensor(hd(negd[:, :]), hd(B[3][0:n, 0:HN]), over(gcs[:, 0:H], n), ALU.subtract))
                link(dve.scalar_tensor_tensor(negd[:, :], negd[:, :], -1.0, negd[:, :], ALU.mult, ALU.min))
                dve.sem_inc(negd_ready, 1)
                link(dve.tensor_tensor(kdx[:, :], gcs[:, H:2 * H], gcs[:, 0:H], ALU.subtract))
                dve.sem_inc(kdx_ready, 1)
                dve.wait_ge(sums_done, i + 1)
                link(dve.tensor_scalar(ss[:, :], ss[:, :], EPS, None, ALU.add))
                rsqrt(dve, link, r[:, :], ss[:, :], work[:, :])
                link(dve.tensor_scalar(r[:, 0:H], r[:, 0:H], DH ** -0.5, None, ALU.mult))
                link(dve.tensor_tensor(hd(qn[:, :]), hd(B[0][0:n, :]), over(r[:, 0:H], P), ALU.mult))
                link(dve.tensor_tensor(hd(kn[:, :]), hd(B[1][0:n, :]), over(r[:, H:2 * H], P), ALU.mult))
                dve.sem_inc(qk_scaled, 1)
                link(dve.tensor_tensor(hd(vb[:, :]), hd(B[2][0:n, :]), over(gb[:, H:2 * H], P), ALU.mult))
                dve.wait_ge(exps_done, i + 1)
                link(dve.scalar_tensor_tensor(nbe[:, :], gb[:, H:2 * H], -1.0, eg[:, :], ALU.mult, ALU.mult))
                link(dve.tensor_tensor(hd(kbg[:, :]), hd(kn[:, :]), over(nbe[:, :], P), ALU.mult))
                link(dve.tensor_tensor(hd(kd[:, :]), hd(kn[:, :]), over(ekd[:, :], P), ALU.mult))
                dve.sem_inc(kv_scaled, 1)
                dve.wait_ge(kk_done, i + 1)
                dve.wait_ge(masks_done, i + 1)
                dve.tensor_tensor(m[:, :], B[0][0:n, 0:HN], esl[:, :], ALU.mult).then_inc(m_ready, 1)
                dve.tensor_tensor(aT[:, :], B[1][0:n, 0:HN], esu[:, :], ALU.mult).then_inc(a_ready, 1)
                dve.wait_ge(m_ready, i + 1)
                dve.wait_ge(identity_set, 2 * i + 2)
                for l in range(levels):
                    up = repeat(k.c(f"up{l}", n)[:, 0:n].bitcast(I32), H)
                    low = repeat(k.c(f"low{l}", n)[:, 0:n].bitcast(I32), H)
                    if l == 0:
                        hold(dve, x_done, levels * i + 1, held)
                        dve.copy_predicated(hd(U[:, :]), up, hd(B[2][0:n, 0:HN])).then_inc(level_done, 1)
                        dve.copy_predicated(hd(L[:, :]), low, hd(m[:, :])).then_inc(level_done, 1)
                    else:
                        dve.wait_ge(level_done, (2 * levels - 1) * i + 2 * l)
                        hold(dve, zu_done, (levels - 1) * i + l, held)
                        dve.copy_predicated(hd(U[:, :]), up, hd(B[0][0:n, 0:HN])).then_inc(level_done, 1)
                        if l < levels - 1:
                            hold(dve, zl_done, (levels - 2) * i + l, held)
                            dve.copy_predicated(hd(L[:, :]), low, hd(B[1][0:n, 0:HN])).then_inc(level_done, 1)
                if not sample:
                    dve.wait_ge(o_done, i + 1)
                    link(dve.tensor_tensor(S[:, :, :], S[:, :, :], over(egl[:, :], DH), ALU.mult))
                    dve.wait_ge(su_done, i + 1)
                    link(dve.tensor_tensor(S[:, :, :], S[:, :, :], hd(B[6][:, :]), ALU.add))
                    dve.sem_inc(s_ready, 1)
                    dve.wait_ge(osum_done, i + 1)
                    link(dve.tensor_scalar(so[:, :], so[:, :], 1.0 / DH, EPS, ALU.mult, ALU.add))
                    rsqrt(dve, link, ro[:, :], so[:, :], worko[:, :])
                    link(dve.tensor_tensor(hd(on[:, :]), hd(B[5][:, :]), over(ro[:, :], P), ALU.mult))
                    dve.sem_inc(o_scaled, 1)
                    dve.wait_ge(o_turned, i + 1)
                    link(dve.tensor_scalar(on[:, :], B[7][:, :], k.onorm[:, 0:1], None, ALU.mult))
                    link(dve.tensor_tensor(hd(on[:, :]), hd(on[:, :]), k.zT[:, :, cols(t)], ALU.mult))
                    link(dve.tensor_copy(k.oaH[:, :, cols(t)], hd(on[:, :])))
                    link(dve.tensor_tensor(k.oaL[:, :, cols(t)], hd(on[:, :]), k.oaH[:, :, cols(t)].bitcast(F32), ALU.subtract))
                    dve.sem_inc(out_ready, 1)
                    per_tile[0] = link.n
                    return
                dve.wait_ge(v_done, 1)
                link(dve.tensor_copy(uT[:, :], B[7][:, 0:HN]))
                dve.tensor_tensor(vnT[:, :], uT[:, :], B[2][:, 0:HN], ALU.add).then_inc(v_ready, 1)
                dve.wait_ge(x_done, levels + 1)
                dve.tensor_copy(vn[:, :], B[3][0:n, :]).then_inc(v_ready, 1)
                dve.wait_ge(v_ready, 2)
                for h in range(H):
                    ins = dve.tensor_tensor(hd(vm[:, h, :], NSEQ), repeat(vn[:, h * P:h * P + P], NSEQ), over(k.c("s_seq", n), DH), ALU.mult)
                ins.then_inc(v_ready, 1)
                dve.wait_ge(o_done, 1)
                link(dve.tensor_copy(oT[:, :], B[7][:, 0:HN]))
                link(dve.tensor_tensor(oT[:, :], oT[:, :], B[2][:, HN:2 * HN], ALU.add))
                dve.tensor_tensor(sq[:, :], oT[:, :], oT[:, :], ALU.mult).then_inc(o_scaled, 1)
                dve.wait_ge(o_turned, 1)
                link(dve.tensor_scalar(rT[:, :], B[4][:, 0:HN], 1.0 / DH, EPS, ALU.mult, ALU.add))
                link(dve.tensor_copy(sq[:, :], rT[:, :]))
                rsqrt(dve, link, rT[:, :], sq[:, :], workT[:, :])
                link(dve.tensor_tensor(oT[:, :], oT[:, :], rT[:, :], ALU.mult))
                link(dve.scalar_tensor_tensor(hd(oT[:, :]), hd(oT[:, :]), k.onorm[:, 0:1], k.zT[:, :, SEQ:T], ALU.mult, ALU.mult))
                link(dve.tensor_copy(k.oaH[:, :, SEQ:T], hd(oT[:, :])))
                link(dve.tensor_tensor(k.oaL[:, :, SEQ:T], hd(oT[:, :]), k.oaH[:, :, SEQ:T].bitcast(F32), ALU.subtract))
                link(dve.tensor_tensor(S[:, :, :], S[:, :, :], over(egl[:, :], DH), ALU.mult))
                for u in range(2 * H):
                    h, half = u // 2, u % 2
                    st = S[:, 4 * H * half + h:4 * H * (half + 1):H, :]
                    dve.wait_ge(su_done, u + 1)
                    ins = dve.tensor_tensor(st, st, hd(B[5 + half][:, :]), ALU.add)
                    ins.then_inc(upd_done, 1) if u < 2 * H - 1 else ins.then_inc(s_ready, 1)

            tiles(dve, tile)


def qkv_stage(k):
    nc, d = k.nc, k.d
    G = 2 * H
    with ExitStack() as ctx:
        sem = lambda s: k.sem(f"qk_{s}")
        w_loaded, w_high, w_low = (sem(s) for s in ("w", "w_high", "w_low"))
        k_out = [sem(f"k_out{u}") for u in range(2)]
        proj_done, copied, steps, normed, turned, stored, v_out, squared, passed = (
            sem(s) for s in ("proj", "copied", "steps", "normed", "turned", "stored", "v_out", "squared", "passed"))
        sb = k.area("qk", M_Z, M_BIAS)
        wb = sb("w", [P, KC, W])
        wH, wL = (sb(s, [P, KC, W], F32R) for s in ("wH", "wL"))
        raw = sb("raw", [P, 2, W])
        sq = sb("sq", [P, W])
        ss, r, work = (sb(s, [P, G]) for s in ("ss", "r", "work"))
        nrm = sb("nrm", [P, 2, W])
        ps = [k.ps(ctx, f"qk_ps{u}") for u in range(4)]
        pt = [k.ps(ctx, f"qk_pt{u}") for u in range(2)]
        w_cols = d["w_in"].rearrange("a (c p) n -> p (a c) n", p=P)
        kp = d["k_prompt"].rearrange("a b t h n -> (a b t) (h n)")
        vp = d["v_prompt"].rearrange("a b t h n -> (a b t) (h n)")
        ks = d["k_sample"].rearrange("a b t h n -> (a b t) (h n)")
        vs = d["v_sample"].rearrange("a b t h n -> (a b t) (h n)")
        block = ctx.enter_context(nc.Block())
        NT = PT + 1
        n_of = lambda t: P if t < PT else NS

        @block.sync
        def _(sp):
            for g in range(3):
                if g:
                    sp.wait_ge(w_low, KC * g)
                sp.dma_start(wb[:, :, :], w_cols[:, :, C_Q + g * W:C_Q + (g + 1) * W]).then_inc(w_loaded, 16)
            for t in range(NT):
                sp.wait_ge(normed, NT + t + 1)
                src = nrm[0:n_of(t), (NT + t) % 2, :]
                sp.dma_start(kp[t * P:t * P + P, :] if t < PT else ks, src).then_inc(k_out[(NT + t) % 2], 16)
            sp.wait_ge(copied, 3 * NT)
            sp.dma_start(vp.rearrange("(t p) n -> p t n", p=P), k.v[:, 0:PT, :]).then_inc(v_out, 16)
            sp.dma_start(vs, k.v[0:NS, PT, :]).then_inc(v_out, 16)
            sp.wait_ge(v_out, 32)
            for u in range(2):
                sp.wait_ge(k_out[u], 16 * ((NT + u) // 2))

        @block.tensor
        def _(pe):
            def turn(j):
                n = n_of(j % NT)
                pe.wait_ge(normed, j + 1)
                if j >= 2:
                    pe.wait_ge(stored, j - 1)
                for h in range(H):
                    ins = pe.transpose(pt[j % 2][:, h * P:h * P + n], nrm[0:n, j % 2, h * P:h * P + P], k.c("ident", n)[:, 0:n])
                ins.then_inc(turned, 1)

            for g in range(3):
                for t in range(NT):
                    j = g * NT + t
                    n = n_of(t)
                    if j >= 4:
                        pe.wait_ge(copied, j - 3)
                    cols = slice(t * P, t * P + P)
                    for c in range(KC):
                        if t == 0:
                            pe.wait_ge(w_low, KC * g + c + 1)
                        three(pe, ps[j % 4][:, :], (k.hH[:, c, cols], k.hL[:, c, cols]), (wH[:, c, :], wL[:, c, :]),
                              c == 0, c == KC - 1, proj_done)
                    if 2 <= j < 2 * NT + 2:
                        turn(j - 2)

        @block.scalar
        def _(act):
            def high(g):
                act.wait_ge(w_loaded, 16 * g + 16)
                if g:
                    act.wait_ge(proj_done, NT * g)
                for c in range(KC):
                    act.activation(wH[:, c, :], wb[:, c, :], ACT.Copy).then_inc(w_high, 1)

            high(0)
            for j in range(3 * NT):
                n = n_of(j % NT)
                act.wait_ge(proj_done, j + 1)
                if j % NT == NT - 1 and j < 2 * NT:
                    high(j // NT + 1)
                if j < 2 * NT:
                    if j >= 2:
                        act.wait_ge(normed, j - 1)
                    act.activation(raw[0:n, j % 2, :], ps[j % 4][0:n, :], ACT.Copy).then_inc(copied, 1)
                    act.wait_ge(copied, j + 1)
                    if j:
                        act.wait_ge(passed, j)
                    act.activation(sq[0:n, :], raw[0:n, j % 2, :], ACT.Square).then_inc(squared, 1)
                else:
                    act.activation(k.v[0:n, j % NT, :], ps[j % 4][0:n, :], ACT.Copy).then_inc(copied, 1)

        @block.vector
        def _(dve):
            def store(j):
                n, t = n_of(j % NT), j % NT
                dst = k.qT if j < NT else k.kT
                dve.wait_ge(turned, j + 1)
                dve.tensor_copy(dst[:, :, t * P:t * P + n], hd(pt[j % 2][:, :])[:, :, 0:n]).then_inc(stored, 1)

            def low(g):
                for c in range(KC):
                    dve.wait_ge(w_high, KC * g + c + 1)
                    dve.tensor_tensor(wL[:, c, :], wb[:, c, :], wH[:, c, :].bitcast(F32), ALU.subtract).then_inc(w_low, 1)

            link = Links(dve, steps)
            low(0)
            for j in range(2 * NT):
                n = n_of(j % NT)
                if j % NT == NT - 1:
                    low(j // NT + 1)
                weight = k.qw if j < NT else k.kw
                dve.wait_ge(squared, j + 1)
                dve.tensor_reduce(ss[0:n, :], sq[0:n, :].rearrange("p (g n) -> p g n", g=G), AX.X, ALU.add).then_inc(passed, 1)
                dve.wait_ge(passed, j + 1)
                link(dve.tensor_scalar(ss[0:n, :], ss[0:n, :], 1.0 / 64, EPS, ALU.mult, ALU.add))
                rsqrt(dve, link, r[0:n, :], ss[0:n, :], work[0:n, :])
                if j >= 2:
                    dve.wait_ge(turned, j - 1)
                if j >= NT + 2:
                    dve.wait_ge(k_out[j % 2], 16 * ((j - NT) // 2))
                out = nrm[0:n, j % 2, :].rearrange("p (g n) -> p g n", g=G)
                link(dve.tensor_tensor(out, raw[0:n, j % 2, :].rearrange("p (g n) -> p g n", g=G), over(r[0:n, :], 64), ALU.mult))
                dve.tensor_tensor(out, out, repeat(weight[0:n, :], G), ALU.mult).then_inc(normed, 1)
                if j >= 1:
                    store(j - 1)
            store(2 * NT - 1)


def attention_stage(k):
    nc = k.nc
    with ExitStack() as ctx:
        sem = lambda s: k.sem(f"at_{s}")
        (staged, scored, maxed, exped, weighed, turned, moved, summed, o_saved, squared, o_normed, o_turned,
         ob_stored, chain, pool_held) = (sem(s) for s in (
             "staged", "scored", "maxed", "exped", "weighed", "turned", "moved", "summed", "o_saved", "squared",
             "o_normed", "o_turned", "ob_stored", "chain", "pool_held"))
        sb = k.area("at", M_H, M_QKV)
        qh, kh = (sb(s, [P, SEQ]) for s in ("qh", "kh"))
        E = [sb(f"e{m}", [P, SEQ]) for m in range(2)]
        pr = sb("p", [P, 2, SEQ])
        prT = sb("pt", [P, 2, 512])
        mx, nmx, sums, rs = (sb(s, [P, 2]) for s in ("mx", "nmx", "sums", "rs"))
        o, on = (sb(s, [P, PT, DH]) for s in ("o", "on"))
        so, ro, worko = (sb(s, [P, PT]) for s in ("so", "ro", "worko"))
        ps = [k.ps(ctx, f"at_ps{m}", 2) for m in range(2)]
        pt = [k.ps(ctx, f"at_pt{m}") for m in range(2)]
        po = [k.ps(ctx, f"at_po{m}") for m in range(2)]
        srows = [ps[m][:, :, :].rearrange("p a n -> p (a n)") for m in range(2)]
        GROUPS = [(i, g) for i in range(PT) for g in range(0, i + 1, 4)]
        NG = len(GROUPS)
        first_group = [GROUPS.index((i, 0)) for i in range(PT)]
        ngroups = [(i + 4) // 4 for i in range(PT)]
        block = ctx.enter_context(nc.Block())

        def heads(eng, body):
            loop(eng, H, body)

        @block.gpsimd
        def _(pool):
            def head(h, first):
                if not first:
                    hold(pool, scored, 2 * PT * h, pool_held)
                pool.tensor_copy(qh[:, :], k.qT[:, at(h), 0:SEQ].rearrange("p a n -> p (a n)")).then_inc(staged, 1)
                pool.tensor_copy(kh[:, :], k.kT[:, at(h), 0:SEQ].rearrange("p a n -> p (a n)")).then_inc(staged, 1)

            heads(pool, head)

        @block.tensor
        def _(pe):
            def head(h, first):
                def scores(i):
                    for m in range(2):
                        if i or not first:
                            pe.wait_ge(exped, 2 * PT * h + 2 * i - 1 + m)
                        rows = slice(64 * m, 64 * m + 64)
                        nk = (i + 1) * P
                        for b in range(0, nk, 512):
                            e = min(nk, b + 512)
                            near = [c for c in (i - 1, i) if c >= 0 and b <= c * P < e]
                            pe.matmul(srows[m][:, b:e], qh[rows, i * P:i * P + P], kh[rows, b:e], start=True, stop=not near)
                            for c in near:
                                ins = pe.matmul(srows[m][:, c * P:c * P + P], k.c("ident"),
                                                k.bias[:, at(h), (c - i + 1) * P:(c - i + 2) * P].rearrange("p a n -> p (a n)"),
                                                start=False, stop=(c == near[-1]))
                        ins.then_inc(scored, 1)

                def values(i):
                    pe.wait_ge(weighed, PT * h + i + 1)
                    for n in range(ngroups[i]):
                        G = first_group[i] + n
                        g, ge = 4 * n, min(4 * n + 4, i + 1)
                        if not first or G >= 2:
                            pe.wait_ge(moved, NG * h + G - 1)
                        for c in range(g, ge):
                            ins = pe.transpose(pt[G % 2][:, (c - g) * P:(c - g + 1) * P], pr[:, i % 2, c * P:c * P + P], k.c("ident"))
                        ins.then_inc(turned, 1)
                    if not first or i >= 2:
                        pe.wait_ge(o_saved, PT * h + i - 1)
                    for n in range(ngroups[i]):
                        G = first_group[i] + n
                        g, ge = 4 * n, min(4 * n + 4, i + 1)
                        pe.wait_ge(moved, NG * h + G + 1)
                        for c in range(g, ge):
                            ins = pe.matmul(po[i % 2][:, 0:DH], prT[:, G % 2, (c - g) * P:(c - g + 1) * P],
                                            k.v[:, c, at(h * P, P)], start=(c == 0), stop=(c == i))
                    ins.then_inc(summed, 1)

                pe.wait_ge(staged, 2 * h + 2)
                scores(0)
                for i in range(PT):
                    if i + 1 < PT:
                        scores(i + 1)
                    values(i)
                pe.wait_ge(o_normed, h + 1)
                for g in range(2):
                    for i in range(4):
                        ins = pe.transpose(pt[g][:, i * P:i * P + P], on[:, 4 * g + i, :], k.c("ident"))
                    ins.then_inc(o_turned, 1)
                pe.wait_ge(ob_stored, 2 * h + 2)

            heads(pe, head)

        @block.scalar
        def _(act):
            def head(h, first):
                def move(i):
                    for n in range(ngroups[i]):
                        G = first_group[i] + n
                        w = (min(4 * n + 4, i + 1) - 4 * n) * P
                        act.wait_ge(turned, NG * h + G + 1)
                        if not first or G >= 2:
                            act.wait_ge(summed, PT * h + (GROUPS[G - 2][0] + 1 if G >= 2 else 0))
                        act.activation(prT[:, G % 2, 0:w], pt[G % 2][:, 0:w], ACT.Copy).then_inc(moved, 1)

                for i in range(PT):
                    for m in range(2):
                        act.wait_ge(maxed, 2 * PT * h + 2 * i + m + 1)
                        if not first or i:
                            act.wait_ge(weighed, PT * h + i)
                        act.activation(E[m][:, 0:(i + 1) * P], srows[m][:, 0:(i + 1) * P], ACT.Exp, bias=nmx[:, m:m + 1],
                                       scale=0.125, accum_out=sums[:, m:m + 1]).then_inc(exped, 1)
                    if i:
                        move(i - 1)
                move(PT - 1)
                for i in range(PT):
                    act.wait_ge(o_saved, PT * h + i + 1)
                    if not first or i:
                        act.wait_ge(squared, PT * h + i)
                    act.activation(E[1][:, 0:DH], o[:, i, :], ACT.Square, accum_out=so[:, i:i + 1]).then_inc(squared, 1)

            heads(act, head)

        @block.vector
        def _(dve):
            per = [0]

            def head(h, first):
                link = Links(dve, chain, per[0] * h)

                def save(i):
                    dve.wait_ge(summed, PT * h + i + 1)
                    dve.tensor_copy(o[:, i, :], po[i % 2][:, 0:DH]).then_inc(o_saved, 1)

                for i in range(PT):
                    nk = (i + 1) * P
                    for m in range(2):
                        dve.wait_ge(scored, 2 * PT * h + 2 * i + m + 1)
                        if m == 0 and (i or not first):
                            dve.wait_ge(exped, 2 * PT * h + 2 * i)
                        link(dve.tensor_reduce(mx[:, m:m + 1], srows[m][:, 0:nk], AX.X, ALU.max))
                        link(dve.tensor_scalar(nmx[:, m:m + 1], mx[:, m:m + 1], -0.125, None, ALU.mult))
                        dve.sem_inc(maxed, 1)
                    dve.wait_ge(exped, 2 * PT * h + 2 * i + 2)
                    link(dve.reciprocal(rs[:, :], sums[:, :]))
                    link(dve.scalar_tensor_tensor(rs[:, 1:2], rs[:, 1:2], -1.0, k.lam[:, :], ALU.mult, ALU.mult))
                    if not first or i >= 2:
                        dve.wait_ge(turned, NG * h + (first_group[i - 2] + ngroups[i - 2] if i >= 2 else (first_group[PT + i - 2] + ngroups[PT + i - 2] - NG)))
                    link(dve.tensor_scalar(pr[:, i % 2, 0:nk], E[0][:, 0:nk], rs[:, 0:1], None, ALU.mult))
                    link(dve.scalar_tensor_tensor(pr[:, i % 2, 0:nk], E[1][:, 0:nk], rs[:, 1:2], pr[:, i % 2, 0:nk], ALU.mult, ALU.add))
                    dve.sem_inc(weighed, 1)
                    if i:
                        save(i - 1)
                save(PT - 1)
                dve.wait_ge(squared, PT * h + PT)
                link(dve.tensor_scalar(so[:, :], so[:, :], 1.0 / DH, EPS, ALU.mult, ALU.add))
                rsqrt(dve, link, ro[:, :], so[:, :], worko[:, :])
                if not first:
                    dve.wait_ge(o_turned, 2 * h)
                link(dve.tensor_tensor(on[:, :, :], o[:, :, :], over(ro[:, :], DH), ALU.mult))
                dve.sem_inc(o_normed, 1)
                for g in range(2):
                    dve.wait_ge(o_turned, 2 * h + g + 1)
                    cs = slice(g * 512, (g + 1) * 512)
                    ob = flat(o[:, 4 * g:4 * g + 4, :])
                    link(dve.tensor_scalar(ob, pt[g][:, :], k.subln[:, 0:1], None, ALU.mult))
                    dve.sem_inc(ob_stored, 1)
                    link(dve.tensor_copy(flat(k.obH[:, at(h), cs]), ob))
                    link(dve.tensor_tensor(flat(k.obL[:, at(h), cs]), ob, flat(k.obH[:, at(h), cs]).bitcast(F32), ALU.subtract))
                per[0] = link.n

            heads(dve, head)


def decode_stage(k):
    nc, d = k.nc, k.d
    NK = PAST + NS
    RG = 2
    with ExitStack() as ctx:
        sem = lambda s: k.sem(f"de_{s}")
        (table_in, v_in, q_set, k_turned, k_moved, scored, new_scored, sc_moved, row_turned, biased, exped, weighed, steps,
         back, back_moved, pt_ready, summed, sq_ready, norm_done, bias_set) = (sem(s) for s in (
             "table_in", "v_in", "q_set", "k_turned", "k_moved", "scored", "new_scored", "sc_moved", "row_turned", "biased", "exped",
             "weighed", "steps", "back", "back_moved", "pt_ready", "summed", "sq_ready", "norm_done", "bias_set"))
        k_in = [sem(f"k_in{u}") for u in range(4)]
        sb = k.area("de", M_H, M_QKV)
        table = sb("table", [1, NSEQ * PAGES], I32)
        kpg = sb("kpg", [P, 4, W])
        vpg = sb("vpg", [P, NSEQ * PAGES, W])
        kpT = sb("kpT", [P, 2, W])
        Q = sb("q", [P, NSEQ, H, 2, QN])
        sc = sb("sc", [P, PAGES, 256])
        scn = sb("scn", [NS, 256])
        bnew = sb("bnew", [P, RG, NSEQ, QN])
        X = sb("x", [P, RG, NK])
        mx, nmx, sums, rs = (sb(s, [P, RG]) for s in ("mx", "nmx", "sums", "rs"))
        sgn = sb("sgn", [P, 1])
        pb = sb("pb", [P, PAGES, 256])
        pbn = sb("pbn", [NS, 256])
        prT = sb("prT", [P, PAGES, NSEQ * H, QN])
        prTn = sb("prTn", [NS, NSEQ * H, QN])
        oT, sq, ro, work = (sb(s, [P, P]) for s in ("oT", "sq", "ro", "work"))
        pk = [k.ps(ctx, f"de_pk{u}") for u in range(2)]
        psc, psn, po, pss = (k.ps(ctx, f"de_{s}") for s in ("psc", "psn", "po", "pss"))
        prow = [k.ps(ctx, f"de_prow{u}") for u in range(RG)]
        block = ctx.enter_context(nc.Block())
        ck = d["cache_k"].rearrange("a g p h n -> p (a g) (h n)")
        cv = d["cache_v"].rearrange("a g p h n -> p (a g) (h n)")
        pool_pages = ck.shape[1]
        NPG = NSEQ * PAGES

        @block.sync
        def _(sp):
            sp.dma_start(table[:, :], d["page_table"].rearrange("(a s) g -> a (s g)", a=1)).then_inc(table_in, 16)
            sp.wait_ge(table_in, 16)
            for j in range(NPG):
                page = sp.value_load(table[0:1, j:j + 1], min_val=0, max_val=pool_pages - 1)
                if j >= 4:
                    sp.wait_ge(k_turned, j - 3)
                sp.dma_start(kpg[:, j % 4, :], ck[:, at(page), :].rearrange("p a n -> p (a n)")).then_inc(k_in[j % 4], 16)
                sp.dma_start(vpg[:, j, :], cv[:, at(page), :].rearrange("p a n -> p (a n)")).then_inc(v_in, 16)

        @block.tensor
        def _(pe):
            ident = k.c("ident")

            def turn(j):
                pe.wait_ge(k_in[j % 4], 16 * (j // 4 + 1))
                if j >= 2:
                    pe.wait_ge(k_moved, j - 1)
                for h in range(H):
                    ins = pe.transpose(pk[j % 2][:, h * P:h * P + P], kpg[:, j % 4, h * P:h * P + P], ident)
                ins.then_inc(k_turned, 1)

            def score(j):
                s, g = j // PAGES, j % PAGES
                pe.wait_ge(k_moved, j + 1)
                for h in range(H):
                    c = g * 256 + (s * H + h) * 8
                    ins = pe.matmul(psc[:, c:c + 8], kpT[:, j % 2, h * P:h * P + P], Q[:, s, h, :, :].rearrange("p m q -> p (m q)"),
                                    start=True, stop=True)
                ins.then_inc(scored, 1)

            turn(0)
            pe.wait_ge(q_set, 9)
            for h in range(H):
                ins = pe.matmul(psn[0:NS, 0:256].rearrange("p (s h n) -> p s h n", s=NSEQ, h=H)[:, :, h, :],
                                k.kT[:, h, SEQ:T], Q[:, :, h, :, :].rearrange("p s m q -> p s (m q)"), start=True, stop=True)
            ins.then_inc(new_scored, 1)
            for j in range(NPG):
                if j + 1 < NPG:
                    turn(j + 1)
                score(j)
            pe.wait_ge(sc_moved, 2)
            for r in range(RG):
                for g in range(PAGES):
                    pe.transpose(prow[r][:, g * P:g * P + P], sc[:, g, r * P:r * P + P], ident)
                pe.transpose(prow[r][:, PAST:NK], scn[:, r * P:r * P + P], ident[0:NS, 0:NS]).then_inc(row_turned, 1)
            pe.wait_ge(weighed, 1)
            for r in range(RG):
                for g in range(PAGES):
                    pe.transpose(psc[:, g * 256 + r * P:g * 256 + r * P + P], X[:, r, g * P:g * P + P], ident)
                ins = pe.transpose(psn[0:NS, r * P:r * P + P], X[:, r, PAST:NK], ident)
            ins.then_inc(back, 1)
            pe.wait_ge(pt_ready, 2)
            pe.wait_ge(v_in, 16 * NPG)
            for h in range(H):
                for s in range(NSEQ):
                    out = po[:, (h * NSEQ + s) * QN:(h * NSEQ + s + 1) * QN]
                    for g in range(PAGES):
                        pe.matmul(out, vpg[:, s * PAGES + g, h * P:h * P + P], prT[:, g, s * H + h, :], start=(g == 0), stop=False)
                    ins = pe.matmul(out, k.v[0:NS, PT, h * P:h * P + P], prTn[:, s * H + h, :], start=False, stop=True)
            ins.then_inc(summed, 1)
            pe.wait_ge(sq_ready, 1)
            pe.matmul(pss[:, 0:P], k.c("ones"), sq[:, :], start=True, stop=True).then_inc(norm_done, 1)

        @block.scalar
        def _(act):
            for j in range(NPG):
                act.wait_ge(k_turned, j + 1)
                if j >= 2:
                    act.wait_ge(scored, j - 1)
                act.activation(kpT[:, j % 2, :], pk[j % 2][:, :], ACT.Copy).then_inc(k_moved, 1)
            act.wait_ge(biased, 1)
            for r in range(RG):
                act.activation(X[:, r, :], X[:, r, :], ACT.Exp, bias=nmx[:, r:r + 1], scale=0.125,
                               accum_out=sums[:, r:r + 1]).then_inc(exped, 1)

        @block.vector
        def _(dve):
            link = Links(dve, steps)
            dve.memset(Q[:, :, :, :, :], 0.0).then_inc(q_set, 1)
            dve.wait_ge(q_set, 1)
            for m in range(2):
                rows = slice(64 * m, 64 * m + 64)
                for h in range(H):
                    dve.tensor_copy(Q[rows, :, h, m, :], k.qT[rows, h, SEQ:T].rearrange("p (s q) -> p s q", s=NSEQ)).then_inc(q_set, 1)
            link(dve.scalar_tensor_tensor(sgn[:, :], k.c("m1"), -1.0, k.lam[:, :], ALU.mult, ALU.mult))
            link(dve.tensor_tensor(sgn[:, :], sgn[:, :], k.c("m0"), ALU.add))
            for r in range(RG):
                cross = k.c("s_cross")[:, r * NSEQ:(r + 1) * NSEQ]
                link(dve.tensor_tensor(bnew[:, r, :, :], repeat(k.sbias[:, PAST:PAST + QN], NSEQ), over(cross, QN), ALU.add))
            dve.wait_ge(new_scored, 1)
            dve.tensor_copy(scn[:, :], psn[0:NS, 0:256]).then_inc(sc_moved, 1)
            dve.wait_ge(scored, NPG)
            dve.tensor_copy(sc[:, :, :], psc[:, :].rearrange("p (g n) -> p g n", g=PAGES)).then_inc(sc_moved, 1)
            for r in range(RG):
                dve.wait_ge(row_turned, r + 1)
                link(dve.tensor_tensor(X[:, r, 0:PAST], prow[r][:, 0:PAST], k.sbias[:, 0:PAST], ALU.add))
                link(dve.tensor_tensor(X[:, r, PAST:NK], prow[r][:, PAST:NK], bnew[:, r, :, :].rearrange("p s q -> p (s q)"), ALU.add))
            link(dve.tensor_reduce(mx[:, :], X[:, :, :], AX.X, ALU.max))
            dve.tensor_scalar(nmx[:, :], mx[:, :], -0.125, None, ALU.mult).then_inc(biased, 1)
            dve.wait_ge(exped, RG)
            link(dve.reciprocal(rs[:, :], sums[:, :]))
            link(dve.tensor_scalar(rs[:, :], rs[:, :], sgn[:, 0:1], None, ALU.mult))
            dve.tensor_tensor(X[:, :, :], X[:, :, :], over(rs[:, :], NK), ALU.mult).then_inc(weighed, 1)
            dve.wait_ge(back, 1)
            link(dve.tensor_copy(pb[:, :, :], psc[:, :].rearrange("p (g n) -> p g n", g=PAGES)))
            link(dve.tensor_copy(pbn[:, :], psn[0:NS, 0:256]))
            pv = pb[:, :, :].rearrange("p g (s m q) -> p (g s) m q", m=2, q=QN)
            dve.tensor_tensor(prT[:, :, :, :].rearrange("p g s q -> p (g s) q"), pv[:, :, 0, :], pv[:, :, 1, :], ALU.add).then_inc(pt_ready, 1)
            pn = pbn[:, :].rearrange("p (s m q) -> p s m q", m=2, q=QN)
            dve.tensor_tensor(prTn[:, :, :], pn[:, :, 0, :], pn[:, :, 1, :], ALU.add).then_inc(pt_ready, 1)
            dve.wait_ge(summed, 1)
            link(dve.tensor_copy(oT[:, :], po[:, 0:P]))
            dve.tensor_tensor(sq[:, :], oT[:, :], oT[:, :], ALU.mult).then_inc(sq_ready, 1)
            dve.wait_ge(norm_done, 1)
            link(dve.tensor_scalar(sq[:, :], pss[:, 0:P], 1.0 / DH, EPS, ALU.mult, ALU.add))
            rsqrt(dve, link, ro[:, :], sq[:, :], work[:, :])
            link(dve.tensor_tensor(oT[:, :], oT[:, :], ro[:, :], ALU.mult))
            link(dve.tensor_scalar(oT[:, :], oT[:, :], k.subln[:, 0:1], None, ALU.mult))
            link(dve.tensor_copy(k.obH[:, :, SEQ:T], hd(oT[:, :])))
            link(dve.tensor_tensor(k.obL[:, :, SEQ:T], hd(oT[:, :]), k.obH[:, :, SEQ:T].bitcast(F32), ALU.subtract))


def mix_stage(k):
    nc, d = k.nc, k.d
    with ExitStack() as ctx:
        sem = lambda s: k.sem(f"mx_{s}")
        proj_done = [sem(f"proj{u}") for u in range(2)]
        gate_in = [sem(f"gate_in{u}") for u in range(2)]
        gated = [sem(f"gated{u}") for u in range(2)]
        added, high, low = (sem(s) for s in ("added", "high", "low"))
        sb = k.area("mx", M_U, M_Z)
        w = Stream(k, "mx", sb, proj_done)
        sg = [sb(f"sg{u}", [P, T]) for u in range(2)]
        mixed = [sb(f"mixed{u}", [P, T]) for u in range(2)]
        ps = [k.ps(ctx, f"mx_ps{u}", 3) for u in range(2)]
        b_cols = d["w_branch"].rearrange("a b (c p) n -> p (a b) c n", p=P)
        gates = k.gate_dram.rearrange("c p n -> p c n")
        block = ctx.enter_context(nc.Block())
        act_in = ((k.oaH, k.oaL), (k.obH, k.obL))

        @block.sync
        def _(sp):
            for u in range(2):
                w.load(sp, u, 0, b_cols[:, u, :, 0:P], True)

            def step(i, first, final):
                for u in range(2):
                    if not first:
                        hold(sp, gated[u], i, w.sp_held)
                    sp.dma_start(sg[u][:, :], flat(gates[:, at(i + u * KC), :])).then_inc(gate_in[u], 16)
                if not final:
                    for u in range(2):
                        w.load(sp, u, i + 1, b_cols[:, u, :, at(i * P + P, P)], False)

            loop3(sp, KC, step)

        @block.tensor
        def _(pe):
            def step(i, first):
                for u in range(2):
                    if not first:
                        pe.wait_ge(gated[u], i)
                    w.multiply(pe, u, i, ps[u], *act_in[u], H)

            loop(pe, KC, step)

        @block.scalar
        def _(act):
            for u in range(2):
                w.high(act, u, 0, H, True)

            def step(i, first, final):
                if not final:
                    for u in range(2):
                        w.high(act, u, i + 1, H, False)
                act.wait_ge(added, i + 1)
                act.activation(flat(k.mH[:, at(i), :]), mixed[0][:, :], ACT.Copy).then_inc(high, 1)

            loop3(act, KC, step)

        @block.vector
        def _(dve):
            for u in range(2):
                w.low(dve, u, 0, H)
            banks = lambda ap: ap.rearrange("p (b n) -> p b n", b=NB)

            def step(i, first, final):
                for u in range(2):
                    dve.wait_ge(proj_done[u], i + 1)
                    dve.wait_ge(gate_in[u], 16 * i + 16)
                    if u == 0 and not first:
                        dve.wait_ge(low, i)
                    if u and not first:
                        dve.wait_ge(added, i)
                    dve.tensor_tensor(banks(mixed[u][:, :]), banks(sg[u][:, :]), ps[u][:, :, 0:BW], ALU.mult).then_inc(gated[u], 1)
                    if not final:
                        w.low(dve, u, i + 1, H)
                for u in range(2):
                    dve.wait_ge(gated[u], i + 1)
                dve.tensor_tensor(mixed[0][:, :], mixed[0][:, :], mixed[1][:, :], ALU.add).then_inc(added, 1)
                dve.wait_ge(high, i + 1)
                dve.tensor_tensor(flat(k.mL[:, at(i), :]), mixed[0][:, :], flat(k.mH[:, at(i), :]).bitcast(F32), ALU.subtract).then_inc(low, 1)

            loop3(dve, KC, step)


def out_proj_stage(k):
    nc, d = k.nc, k.d
    with ExitStack() as ctx:
        sem = lambda s: k.sem(f"wo_{s}")
        proj_done = [sem(f"proj{u}") for u in range(2)]
        added = [sem(f"added{u}") for u in range(2)]
        x_in = sem("x_in")
        w = Stream(k, "wo", k.area("wo", M_FFN, M_END), proj_done)
        ps = [k.ps(ctx, f"wo_ps{u}", 3) for u in range(2)]
        w_cols = d["w_o"].rearrange("a (c p) n -> p (a c) n", p=P)
        block = ctx.enter_context(nc.Block())
        NP = KC // 2

        @block.sync
        def _(sp):
            for u in range(2):
                w.load(sp, u, 0, w_cols[:, :, u * P:u * P + P], True)
            sp.dma_start(k.x1T[:, :, :], k.xT_dram.rearrange("c p n -> p c n")).then_inc(x_in, 16)
            with sp.Fori(1, NP) as i:
                for u in range(2):
                    w.load(sp, u, i, w_cols[:, :, at((2 * i + u) * P, P)], False)

        @block.tensor
        def _(pe):
            def step(i, first):
                for u in range(2):
                    if not first:
                        pe.wait_ge(added[u], i)
                    w.multiply(pe, u, i, ps[u], k.mH, k.mL, KC)

            loop(pe, NP, step)

        @block.scalar
        def _(act):
            def step(i, first):
                for u in range(2):
                    w.high(act, u, i, KC, first)

            loop(act, NP, step)

        @block.vector
        def _(dve):
            for u in range(2):
                w.low(dve, u, 0, KC)
            dve.wait_ge(x_in, 16)

            def step(i, first, final):
                for u in range(2):
                    dve.wait_ge(proj_done[u], i + 1)
                    if not final:
                        w.low(dve, u, i + 1, KC)
                    x = k.x1T[:, at(2 * i + u), :].rearrange("p a (b n) -> p (a b) n", b=NB)
                    dve.tensor_tensor(x, x, ps[u][:, :, 0:BW], ALU.add).then_inc(added[u], 1)

            loop3(dve, NP, step)


def ffn_stage(k):
    nc, d = k.nc, k.d
    R = TF - 1
    RAW = R + SEQ + NSEQ * (R + QN)
    OUT = RAW - R
    NH = NSEQ * R
    NR = NH + TF + 1
    LAST = R + NSEQ * R
    NC = 2 * CF
    ND = KC // 2
    with ExitStack() as ctx:
        sem = lambda n: k.sem(f"ff_{n}")
        proj_done = [sem(f"proj{u}") for u in range(2)]
        evac_done = [sem(f"evac{u}") for u in range(2)]
        conv_done = [sem(f"conv{u}") for u in range(2)]
        taps_in = [sem(f"taps_in{u}") for u in range(2)]
        last_out = [sem(f"last_out{u}") for u in range(2)]
        saved, taps_turned, taps_sb, last_turned, last_sb, zeroed, chain, silu_done, made, high, u_done, pool_held, dve_held = (
            sem(n) for n in ("saved", "taps_turned", "taps_sb", "last_turned", "last_sb", "zeroed", "chain", "silu", "made", "high",
                             "u", "pool_held", "dve_held"))
        UMAX = max(UPART)
        uH, uL = (k.put(f"ff_u{s}", [P, UMAX, T], M_U + i * UMAX * ROW, F32R) for i, s in enumerate("HL"))
        sb = k.area("ff", M_FFN, M_END)
        w = Stream(k, "ff", sb, proj_done)
        raw = [sb(f"conv_in{u}", [P, RAW]) for u in range(2)]
        acc = [sb(f"acc{u}", [P, RAW]) for u in range(2)]
        last = sb("last", [P, NC, LAST])
        sb = k.area("ff", M_CONST + 1024, M_SMALL)
        nat = sb("nat", [NR, 2, 4 * P])
        taps = sb("taps", [P, NC, NR])
        ps = [k.ps(ctx, f"ff_ps{u}", 3) for u in range(2)]
        pt = k.ps(ctx, "ff_pt", 2)
        samp = [raw[u][:, R + SEQ:RAW].rearrange("p (s c) -> p s c", s=NSEQ) for u in range(2)]
        samp_out = [acc[u][:, R + SEQ:RAW].rearrange("p (s c) -> p s c", s=NSEQ) for u in range(2)]
        w_up = d["w_up"].rearrange("a (c p) n -> p (a c) n", p=P)
        w_down = d["w_down"].rearrange("a (c p) n -> p (a c) n", p=P)
        NQ = NC // 4
        hist = d["state_conv_ffn"].rearrange("a s r n -> (a s r) n")
        cf = d["conv_f"].rearrange("a w n -> (a w) n")
        block = ctx.enter_context(nc.Block())
        parts, c0, i0 = [], 0, 0
        for n in UPART:
            parts.append((c0, n, i0))
            c0, i0 = c0 + n, i0 + n + ND
        pairs = i0

        def rest(eng, part, up, body):
            c, n, i = part
            steps, base = (n, i) if up else (ND, i + n)
            body(0, base, base == 0, steps == 1)
            if steps > 2:
                with eng.Fori(1, steps - 1) as j:
                    body(j, j + base, False, False)
            body(steps - 1, base + steps - 1, False, True)

        def kc_next(part, up, final):
            if not final:
                return KC if up else part[1]
            return part[1] if up else KC

        @block.sync
        def _(sp):
            for q in range(NQ):
                if q >= 2:
                    sp.wait_ge(taps_turned, q - 1)
                c = slice(q * 512, (q + 1) * 512)
                sp.dma_start(nat[0:NH, q % 2, :], hist[:, c]).then_inc(taps_in[q % 2], 16)
                sp.dma_start(nat[NH:NH + TF, q % 2, :], cf[:, c]).then_inc(taps_in[q % 2], 16)
                sp.dma_start(nat[NH + TF:NR, q % 2, :], d["conv_f_b"][:, c]).then_inc(taps_in[q % 2], 16)
                if q == 0:
                    for u in range(2):
                        w.load(sp, u, 0, w_up[:, :, u * DFF:u * DFF + P], True)
            for p, (c0, n, i0) in enumerate(parts):
                if p:
                    for u in range(2):
                        w.load(sp, u, i0, w_up[:, :, u * DFF + c0 * P:u * DFF + (c0 + 1) * P], False)
                with sp.Fori(1, n) as j:
                    for u in range(2):
                        w.load(sp, u, j + i0, w_up[:, :, at(j * P + (u * DFF + c0 * P), P)], False)
                for u in range(2):
                    w.load(sp, u, i0 + n, w_down[:, c0:c0 + n, u * P:u * P + P], False)
                with sp.Fori(1, ND) as j:
                    for u in range(2):
                        w.load(sp, u, j + (i0 + n), w_down[:, c0:c0 + n, at(j * 2 * P + u * P, P)], False)
            for q in range(NQ):
                sp.wait_ge(last_sb, q + 1)
                c = slice(q * 512, (q + 1) * 512)
                sp.dma_start(d["conv_ffn_prompt"].rearrange("a b r n -> (a b r) n")[:, c], nat[0:R, q % 2, :]).then_inc(last_out[q % 2], 16)
                sp.dma_start(d["conv_ffn_sample"].rearrange("a s r n -> (a s r) n")[:, c], nat[R:LAST, q % 2, :]).then_inc(last_out[q % 2], 16)
            for u in range(2):
                sp.wait_ge(last_out[u], 32 * ((NQ + 1 - u) // 2))

        @block.tensor
        def _(pe):
            for q in range(NQ):
                pe.wait_ge(taps_in[q % 2], 48 * (q // 2 + 1))
                if q >= 2:
                    pe.wait_ge(taps_sb, q - 1)
                for c in range(4):
                    ins = pe.transpose(pt[:, q % 2, c * P:c * P + NR], nat[:, q % 2, c * P:(c + 1) * P], k.c("ident", NR)[:, 0:NR])
                ins.then_inc(taps_turned, 1)

            for part in parts:
                c0, n, i0 = part

                def up(j, i, first, final):
                    for u in range(2):
                        if not first:
                            pe.wait_ge(evac_done[u], i)
                        w.multiply(pe, u, i, ps[u], k.fH, k.fL, KC)

                def down(j, i, first, final):
                    for u in range(2):
                        pe.wait_ge(evac_done[u], i)
                        w.multiply(pe, u, i, ps[u], uH, uL, n)

                rest(pe, part, True, up)
                pe.wait_ge(u_done, 4 * (c0 + n))
                rest(pe, part, False, down)
            for q in range(NQ):
                if q == 0:
                    pe.wait_ge(saved, 4 * CF)
                if q >= 2:
                    pe.wait_ge(last_sb, q - 1)
                for c in range(4):
                    ins = pe.transpose(pt[0:LAST, q % 2, c * P:c * P + P], last[:, 4 * q + c, :], k.c("ident"))
                ins.then_inc(last_turned, 1)

        @block.scalar
        def _(act):
            for u in range(2):
                w.high(act, u, 0, KC, True)
            for part in parts:
                c0, n, i0 = part

                def up(j, i, first, final):
                    for u in range(2):
                        act.wait_ge(proj_done[u], i + 1)
                        w.high(act, u, i + 1, kc_next(part, True, final), False)
                        if not first:
                            act.wait_ge(conv_done[u], j + c0)
                            act.wait_ge(saved, (j + c0) * 4 - 2 + 2 * u)
                        for b in range(NB):
                            lo, hi = b * BW, min(SEQ, (b + 1) * BW)
                            act.activation(raw[u][:, R + lo:R + hi], ps[u][:, b, 0:hi - lo], ACT.Copy)
                        act.activation(samp[u][:, :, R:R + QN], ps[u][:, NB - 1, BW - NS:BW].rearrange("p (s c) -> p s c", s=NSEQ),
                                       ACT.Copy).then_inc(evac_done[u], 1)
                    act.wait_ge(conv_done[0], j + (c0 + 1))
                    act.activation(acc[0][:, 0:OUT], acc[0][:, 0:OUT], ACT.Silu).then_inc(silu_done, 1)
                    act.wait_ge(made, j + (c0 + 1))
                    act.activation(flat(uH[:, at(j), 0:SEQ]), acc[0][:, 0:SEQ], ACT.Copy)
                    act.activation(uH[:, at(j), SEQ:T].rearrange("p a (s c) -> p (a s) c", s=NSEQ), samp_out[0][:, :, 0:QN],
                                   ACT.Copy).then_inc(high, 1)

                def down(j, i, first, final):
                    for u in range(2):
                        act.wait_ge(proj_done[u], i + 1)
                        if not final or part is not parts[-1]:
                            w.high(act, u, i + 1, kc_next(part, False, final), False)

                rest(act, part, True, up)
                rest(act, part, False, down)

        @block.gpsimd
        def _(pool):
            for part in parts:
                c0, n, i0 = part

                def save(j, i, first, final):
                    for u in range(2):
                        hold(pool, evac_done[u], i + 1, pool_held)
                        c = j + (c0 + u * CF)
                        pool.tensor_copy(flat(last[:, at(c), 0:R]), raw[u][:, SEQ:SEQ + R]).then_inc(saved, 1)
                        pool.tensor_copy(last[:, at(c), R:LAST].rearrange("p a (s c) -> p (a s) c", s=NSEQ),
                                         samp[u][:, :, QN:QN + R]).then_inc(saved, 1)

                rest(pool, part, True, save)

        @block.vector
        def _(dve):
            for u in range(2):
                dve.memset(raw[u][:, 0:R], 0.0).then_inc(zeroed, 1)
                w.low(dve, u, 0, KC)
            for q in range(NQ):
                dve.wait_ge(taps_turned, q + 1)
                dve.tensor_copy(taps[:, 4 * q:4 * q + 4, :], hd(pt[:, q % 2, :])[:, :, 0:NR]).then_inc(taps_sb, 1)
            dve.wait_ge(taps_sb, NQ)
            dve.wait_ge(zeroed, 2)
            per = [0]

            def tap(c, t):
                return flat(taps[:, at(c), NH + t:NH + t + 1])

            for part in parts:
                c0, n, i0 = part

                def up(j, i, first, final):
                    link = Links(dve, chain, (j + c0) * per[0])
                    for u in range(2):
                        c = j + (c0 + u * CF)
                        w.low(dve, u, i + 1, kc_next(part, True, final))
                        dve.wait_ge(evac_done[u], i + 1)
                        if not first:
                            dve.wait_ge(u_done, (j + c0) * 4)
                        link(dve.tensor_copy(samp[u][:, :, 0:R], taps[:, at(c), 0:NH].rearrange("p a (s r) -> p (a s) r", s=NSEQ)))
                        link(dve.tensor_scalar(acc[u][:, 0:OUT], raw[u][:, 0:OUT], tap(c, 0), tap(c, TF), ALU.mult, ALU.add))
                        for t in range(1, TF):
                            link(dve.scalar_tensor_tensor(acc[u][:, 0:OUT], raw[u][:, t:t + OUT], tap(c, t), acc[u][:, 0:OUT], ALU.mult, ALU.add))
                        dve.sem_inc(conv_done[u], 1)
                    dve.wait_ge(silu_done, j + (c0 + 1))
                    if type(j) is int and j == 0 and c0:
                        for u in range(2):
                            dve.wait_ge(proj_done[u], i)
                    link(dve.tensor_tensor(acc[0][:, 0:OUT], acc[0][:, 0:OUT], acc[1][:, 0:OUT], ALU.mult))
                    dve.sem_inc(made, 1)
                    dve.wait_ge(high, j + (c0 + 1))
                    low = lambda o, a, b: dve.tensor_tensor(o, a, b.bitcast(F32), ALU.subtract).then_inc(u_done, 2)
                    low(flat(uL[:, at(j), 0:SEQ]), acc[0][:, 0:SEQ], flat(uH[:, at(j), 0:SEQ]))
                    tail = lambda buf: buf[:, at(j), SEQ:T].rearrange("p a (s c) -> p (a s) c", s=NSEQ)
                    low(tail(uL), samp_out[0][:, :, 0:QN], tail(uH))
                    per[0] = link.n

                def down(j, i, first, final):
                    for u in range(2):
                        if not final or part is not parts[-1]:
                            w.low(dve, u, i + 1, kc_next(part, False, final))
                        dve.wait_ge(proj_done[u], i + 1)
                        x = k.x1T[:, at(j * 2 + u), :].rearrange("p a (b n) -> p (a b) n", b=NB)
                        dve.tensor_tensor(x, x, ps[u][:, :, 0:BW], ALU.add).then_inc(evac_done[u], 1)

                rest(dve, part, True, up)
                rest(dve, part, False, down)
            for q in range(NQ):
                dve.wait_ge(last_turned, q + 1)
                if q >= 2:
                    dve.wait_ge(last_out[q % 2], 32 * (q // 2))
                dve.tensor_copy(nat[0:LAST, q % 2, :], pt[0:LAST, q % 2, :]).then_inc(last_sb, 1)


def out_stage(k):
    nc, d = k.nc, k.d
    with ExitStack() as ctx:
        turned, copied = k.sem("y_turned"), k.sem("y_copied")
        y_out = [k.sem(f"y_out{u}") for u in range(2)]
        y = k.put("y", [P, 2, D], M_U)
        pt = k.ps(ctx, "y_pt", 4)
        block = ctx.enter_context(nc.Block())
        n_of = lambda t: P if t < PT else NS

        @block.sync
        def _(sp):
            for t in range(PT + 1):
                sp.wait_ge(copied, 2 * (t + 1))
                dst = d["y_prompt"][0, t * P:t * P + P, :] if t < PT else d["y_sample"].rearrange("b q n -> (b q) n")
                sp.dma_start(dst, y[0:n_of(t), t % 2, :]).then_inc(y_out[t % 2], 16)
            for u in range(2):
                sp.wait_ge(y_out[u], 16 * ((PT + 2 - u) // 2))

        @block.tensor
        def _(pe):
            for t in range(PT + 1):
                n = n_of(t)
                if t >= 2:
                    pe.wait_ge(copied, 2 * (t - 1))
                for c in range(KC):
                    ins = pe.transpose(pt[0:n, 2 * (t % 2) + c // 4, c % 4 * P:c % 4 * P + P], k.x1T[:, c, t * P:t * P + n], k.c("ident"))
                ins.then_inc(turned, 1)

        def copy_out(eng, copy, half):
            for t in range(PT + 1):
                n = n_of(t)
                eng.wait_ge(turned, t + 1)
                if t:
                    eng.wait_ge(copied, 2 * t)
                if t >= 2:
                    eng.wait_ge(y_out[t % 2], 16 * (t // 2))
                copy(y[0:n, t % 2, half * 512:(half + 1) * 512], pt[0:n, 2 * (t % 2) + half, :]).then_inc(copied, 1)

        @block.scalar
        def _(act):
            copy_out(act, lambda o, i: act.activation(o, i, ACT.Copy), 0)

        @block.vector
        def _(dve):
            copy_out(dve, lambda o, i: dve.tensor_copy(o, i), 1)


def layer(nc, d):
    k = Core(nc, d)
    k.const = k.put("const", [P, CONSTS.shape[1]], M_CONST)
    sb = k.area("small", M_SMALL, M_H)
    k.qw, k.kw = (sb(n, [P, 64]) for n in ("qw", "kw"))
    k.alog, k.dtb = (sb(n, [P, H]) for n in ("alog", "dtb"))
    k.wmix, k.wffn = (sb(n, [P, KC]) for n in ("wmix", "wffn"))
    k.onorm, k.subln, k.lam = (sb(n, [P, 1]) for n in ("onorm", "subln", "lam"))
    k.g, k.beta = (k.put(n, [P, PT + 1, H], M_BIAS + 5216 + 160 * i) for i, n in enumerate(("g", "beta")))
    k.bias = k.put("bias", [P, H, 2 * P], M_BIAS)
    k.sbias = k.put("sbias", [P, PAST + QN], M_BIAS + 4096)
    dram = lambda name, shape: nc.dram_tensor(name, shape, F32, kind="Internal").ap()
    k.xT_dram, k.qkvT_dram, k.gate_dram = dram("xT_rows", (KC, P, T)), dram("qkvT_rows", (CA, P, T)), dram("gate_rows", (2 * KC, P, T))

    load_stage(k)
    k.hH, k.hL = (k.put(n, [P, KC, TPAD], M_H + i * KC * TPAD * 4, F32R) for i, n in enumerate(("hH", "hL")))
    k.xT = k.put("xT", [P, KC, T], M_QKV)
    turn_stage(k)
    norm_stage(k, "n1", k.xT, k.wmix, k.hH, k.hL, k.area("n1", M_QKV + KC * ROW, M_BIAS), True)
    k.qT, k.kT = (k.put(n, [P, H, T], M_QKV + i * H * ROW) for i, n in enumerate(("qT", "kT")))
    k.v = k.put("v", [P, PT + 1, W], M_QKV + 2 * H * ROW)
    qkv_stage(k)
    k.zT = k.put("zT", [P, H, T], M_Z)
    conv_proj_stage(k)
    k.clear()
    gates_stage(k)
    gate_proj_stage(k)
    k.oaH, k.oaL = (k.put(n, [P, H, T], M_OA + i * H * ROW, F32R) for i, n in enumerate(("oaH", "oaL")))
    delta_stage(k, False)
    k.clear()
    delta_stage(k, True)
    k.clear()
    k.obH, k.obL = k.put("obH", [P, H, T], M_OB, F32R), k.put("obL", [P, H, T], M_Z, F32R)
    attention_stage(k)
    decode_stage(k)
    k.clear()
    k.mH, k.mL = (k.put(n, [P, KC, T], M_MIX + i * KC * ROW, F32R) for i, n in enumerate(("mH", "mL")))
    mix_stage(k)
    k.x1T = k.put("x1T", [P, KC, T], M_X1)
    out_proj_stage(k)
    k.fH, k.fL = (k.put(n, [P, KC, T], M_MIX + i * KC * ROW, F32R) for i, n in enumerate(("fH", "fL")))
    norm_stage(k, "n2", k.x1T, k.wffn, k.fH, k.fL, k.area("n2", M_FFN, M_END), False)
    k.clear()
    ffn_stage(k)
    out_stage(k)


_INS = ["x_prompt", "x_sample", "cache_k", "cache_v", "state_delta", "state_conv_a", "state_conv_ffn", "page_table",
        "rel_bias", "norm_mix", "w_in", "conv_a", "a_log", "dt_bias", "onorm_a", "qnorm_b", "knorm_b", "lam_q1",
        "lam_k1", "lam_q2", "lam_k2", "subln_b", "w_branch", "w_o", "norm_ffn", "w_up", "conv_f", "conv_f_b", "w_down"]
_OUTS = [("y_prompt", (1, SEQ, D)), ("y_sample", (NSEQ, QN, D)), ("k_prompt", (1, 1, SEQ, H, DH)),
         ("v_prompt", (1, 1, SEQ, H, DH)), ("delta_prompt", (1, 1, H, DH, DH)), ("conv_a_prompt", (1, 1, TA - 1, QKV)),
         ("conv_ffn_prompt", (1, 1, TF - 1, 2 * DFF)), ("k_sample", (1, NSEQ, QN, H, DH)),
         ("v_sample", (1, NSEQ, QN, H, DH)), ("delta_sample", (1, NSEQ, H, DH, DH)),
         ("conv_a_sample", (1, NSEQ, TA - 1, QKV)), ("conv_ffn_sample", (1, NSEQ, TF - 1, 2 * DFF))]


def kernel(**inputs):
    import concourse.bacc as _bacc
    from concourse.bass_utils import run_bass_kernel_spmd as _run

    nc = _bacc.Bacc("TRN2", target_bir_lowering=False, num_devices=1)
    arrays, d = {"in_consts": CONSTS}, {}
    for name in _INS:
        arrays[f"in_{name}"] = np.ascontiguousarray(inputs[name])
    for name, a in arrays.items():
        d[name[3:]] = nc.dram_tensor(name, a.shape, mybir.dt.from_np(a.dtype), kind="ExternalInput").ap()
    for name, shape in _OUTS:
        d[name] = nc.dram_tensor(f"out_{name}", shape, F32, kind="ExternalOutput").ap()
    layer(nc, d)
    r = _run(nc, [arrays], core_ids=[0])
    return tuple(r.results[0][f"out_{name}"] for name, _ in _OUTS)
```

```python
import math
from contextlib import ExitStack

import numpy as np

import concourse.bass as bass
from concourse import mybir

F32 = mybir.dt.float32
F32R = mybir.dt.float32r
I32 = mybir.dt.int32
ALU = mybir.AluOpType
ACT = mybir.ActivationFunctionType
AX = mybir.AxisListType

P = 128
D = 1024
KC = D // P
SEQ = 1024
NSEQ, QN = 8, 4
NS = NSEQ * QN
T = SEQ + NS
TPAD = SEQ + 128
PT = SEQ // P
NB, BW = 3, T // 3
H = 4
DH = 128
W = H * DH
QKV = 3 * W
CA = QKV // P
TA = 4
DFF = 2816
CF = DFF // P
TF = 3
PAST, PAGE = 256, 128
PAGES = PAST // PAGE
BUCKETS, MAXD = 32, 128
EPS = 1e-6
LAM0 = 0.8 - 0.6 * math.exp(-0.3 * 0)
NEG = -1e30
C_BA = QKV + W
C_Q = C_BA + 2 * H
C_K, C_V = C_Q + W, C_Q + 2 * W
C_GA = C_Q + 3 * W
C_GB = C_GA + D
LEVELS = 7
SLEVELS = 2
MLO, ML = -(PAST + QN - 1), 388
RSQRT_MAGIC = float(0x5F3759DF)
RSQRT_LINKS = 11


def rel_buckets():
    rel = -(MLO + np.arange(ML))
    n = np.maximum(rel, 0)
    half = BUCKETS // 2
    nf = np.maximum(n, 1).astype(np.float32)
    large = half + (np.log(nf / np.float32(half)) / np.float32(math.log(MAXD / half)) * (BUCKETS - half)).astype(np.int32)
    return rel, np.where(n < half, n, np.minimum(large, BUCKETS - 1))


def constants():
    i = np.arange(P)[:, None]
    j = np.arange(P)[None, :]
    blk = (i // QN == j // QN) & (i < NS) & (j < NS)
    parts = {"ident": i == j, "ones": i >= 0 * j, "triu": i <= j, "neglow": -1.0 * (j < i)}
    for b in range(LEVELS):
        low = (i >> (b + 1) == j >> (b + 1)) & (i >> b & 1 == 1) & (j >> b & 1 == 0)
        parts[f"low{b}"], parts[f"up{b}"] = low, low.T
    parts["s_triu"] = (blk & (i <= j))[:, :NS]
    parts["s_same"] = blk[:, :NS]
    parts["s_neglow"] = (-1.0 * (blk & (j < i)))[:, :NS]
    parts["s_seq"] = (i // QN == np.arange(NSEQ)[None, :]) & (i < NS)
    rel, bucket = rel_buckets()
    hot = np.zeros((P, ML), np.float32)
    seen = np.nonzero(rel >= 0)[0]
    hot[bucket[seen], seen] = 8.0
    hot[BUCKETS - 1, seen] -= 8.0
    hot[BUCKETS, rel < 0] = 8.0
    parts["hot"] = hot
    h, m, q = i // 8 % 4, i // 4 % 2, i % 4
    parts["m0"], parts["m1"] = m == 0, m == 1
    parts["spread"] = (j // 8 % 4 == i // QN) & (j % 4 == i % QN) & (i < 4 * QN)
    parts["s_cross"] = np.concatenate(
        [np.where(i // 32 + 4 * g == np.arange(NSEQ)[None, :], 0.0, 8 * NEG) for g in range(2)], 1)
    at, cols, n = {}, [], 0
    for name, a in parts.items():
        a = np.broadcast_to(a, (P, a.shape[1])).astype(np.float32)
        at[name] = (n, n + a.shape[1])
        cols.append(a)
        n += a.shape[1]
    return np.ascontiguousarray(np.concatenate(cols, 1)), at


CONSTS, CONST_AT = constants()


class Links:

    def __init__(self, eng, sem, base=0):
        self.eng, self.sem, self.base, self.n = eng, sem, base, 0

    def __call__(self, ins):
        self.n += 1
        ins.then_inc(self.sem, 1)
        self.eng.wait_ge(self.sem, self.base + self.n)


def loop(eng, n, body):
    body(0, True)
    with eng.Fori(1, n) as i:
        body(i, False)


def at(i, n=1):
    return bass.ds(i, n)


def over(ap, n):
    return ap.unsqueeze(2).to_broadcast([ap.shape[0], ap.shape[1], n])


def repeat(ap, n):
    return ap.unsqueeze(1).to_broadcast([ap.shape[0], n, ap.shape[1]])


def hd(ap, h=H):
    return ap.rearrange("p (h n) -> p h n", h=h)


def rsqrt(dve, link, out, x, work):
    link(dve.tensor_scalar(work.bitcast(I32), x.bitcast(I32), 1, None, ALU.logical_shift_right))
    link(dve.tensor_scalar(out.bitcast(I32), work.bitcast(I32), -1.0, RSQRT_MAGIC, ALU.mult, ALU.add))
    for _ in range(3):
        link(dve.scalar_tensor_tensor(work, out, -0.5, out, ALU.mult, ALU.mult))
        link(dve.tensor_tensor(work, work, x, ALU.mult))
        link(dve.scalar_tensor_tensor(out, work, 1.5, out, ALU.add, ALU.mult))


def hold(eng, sem, value, held):
    eng.wait_ge(sem, value)
    eng.sem_inc(held, 1)


SBUF = 16512
M_END = 212800
ROW = T * 4
M_CONST = 0
M_SMALL = 11776
M_H = 12800
M_QKV = M_H + 2 * KC * TPAD * 4
M_Z = M_QKV + 2 * H * ROW + (PT + 1) * W * 4
M_OA = M_Z + H * ROW
M_OB = M_OA + 2 * H * ROW
M_BIAS = M_END - 5536
M_MIX = M_H
M_U = M_MIX + 2 * KC * ROW
UPART = (6, 6, 5, 5)
M_X1 = M_U + 2 * max(UPART) * ROW
M_FFN = M_X1 + KC * ROW


class Core:

    def __init__(self, nc, dram):
        self.nc, self.d, self.sems = nc, dram, []

    def put(self, name, shape, offset, dt=F32):
        return self.nc.alloc_sbuf_tensor_at(name, shape, dt, offset=SBUF + offset)

    def area(self, pre, offset, end):
        at = [offset]

        def sb(name, shape, dt=F32):
            t = self.put(f"{pre}_{name}", shape, at[0], dt)
            at[0] += -(-int(np.prod(shape[1:])) * 4 // 32) * 32
            assert at[0] <= end, (pre, name, at[0], end)
            return t

        return sb

    def ps(self, ctx, name, banks=1):
        shape = [P, 512] if banks == 1 else [P, banks, 512]
        return ctx.enter_context(self.nc.psum_tensor(name, shape, F32))

    def sem(self, name):
        self.sems.append(self.nc.alloc_semaphore(name=name))
        return self.sems[-1]

    def clear(self):
        self.nc.clear_and_free_semaphores(self.sems)
        self.sems = []
        self.nc.all_engine_barrier()

    def c(self, name, n=P):
        a, b = CONST_AT[name]
        return self.const[0:n, a:b]


def load_stage(k):
    nc, d = k.nc, k.d
    sb = k.area("ld", M_H, M_QKV)
    with ExitStack() as ctx:
        sem = lambda n: k.sem(n)
        const_in, small_in, bias_rows_out, bias_in = (
            sem(n) for n in ("const_in", "small_in", "bias_rows_out", "bias_in"))
        table_ready, rows_done, rows_sb, steps, lam_e, b16_done, b16_sb = (
            sem(n) for n in ("table_ready", "rows_done", "rows_sb", "ld_steps", "lam_e", "b16_done", "b16_sb"))
        rel = sb("rel", [BUCKETS + 1, H])
        relb = sb("relb", [BUCKETS + 1, H, P])
        lams = sb("lams", [P, 4, 64])
        prod = sb("prod", [P, 2, 64])
        dots = sb("dots", [P, 2])
        rows = sb("rows", [P, H, ML])
        b16 = sb("b16", [4 * QN, PAST + QN])
        prow = [k.ps(ctx, f"prow{h}") for h in range(H)]
        p16 = k.ps(ctx, "p16")
        scratch = nc.dram_tensor("bias_rows", (H, P, ML), F32, kind="Internal").ap()
        block = ctx.enter_context(nc.Block())

        @block.sync
        def _(sp):
            sp.dma_start(k.const[:, :], d["consts"]).then_inc(const_in, 16)
            xp = d["x_prompt"].rearrange("a (t p) n -> p (a t) n", p=P)
            for u in range(PT // 2):
                sp.dma_start(k.x[:, 2 * u:2 * u + 2, :], xp[:, 2 * u:2 * u + 2, :]).then_inc(k.x_in[u], 16)
            sp.dma_start(k.x[0:NS, PT, :], d["x_sample"].rearrange("b q n -> (b q) n")).then_inc(k.x_in[PT // 2], 16)
            w_cols = d["w_in"].rearrange("a (c p) n -> p (a c) n", p=P)
            sp.dma_start(k.wq[:, :, :], w_cols[:, :, C_Q:C_Q + W]).then_inc(k.wq_in, 16)
            sp.dma_start(k.wba[:, :, :], w_cols[:, :, C_BA:C_BA + 2 * H]).then_inc(k.wba_in, 16)

        @block.scalar
        def _(act):
            act.dma_start(rel[0:BUCKETS, :], d["rel_bias"]).then_inc(small_in, 16)
            for n, name in enumerate(("lam_q1", "lam_k1", "lam_q2", "lam_k2")):
                act.dma_start(lams[:, n, :], d[name].partition_broadcast(P).rearrange("p a n -> p (a n)")).then_inc(small_in, 16)
            for buf, name in ((k.qw, "qnorm_b"), (k.kw, "knorm_b"), (k.alog, "a_log"), (k.dtb, "dt_bias")):
                act.dma_start(buf[:, :], d[name].partition_broadcast(P).rearrange("p a n -> p (a n)")).then_inc(small_in, 16)
            with nc.allow_non_contiguous_dma(reason="a few columns"):
                act.dma_start(k.wmix[:, :], d["norm_mix"].rearrange("a (c p) -> p (a c)", p=P)).then_inc(small_in, 16)
                act.dma_start(k.wffn[:, :], d["norm_ffn"].rearrange("a (c p) -> p (a c)", p=P)).then_inc(small_in, 16)
                act.dma_start(k.onorm[:, :], d["onorm_a"].rearrange("a (c p) -> p (a c)", p=P)).then_inc(small_in, 16)
                act.dma_start(k.subln[:, :], d["subln_b"].rearrange("a (c p) -> p (a c)", p=P)).then_inc(small_in, 16)
            act.wait_ge(small_in, 16 * 13)
            act.wait_ge(steps, 4)
            act.activation(dots[:, :], dots[:, :], ACT.Exp).then_inc(lam_e, 1)
            for h in range(H):
                act.wait_ge(rows_done, h + 1)
                act.activation(rows[:, h, :], prow[h][:, 0:ML], ACT.Copy).then_inc(rows_sb, 1)
            for h in range(H):
                act.wait_ge(rows_sb, H)
                act.dma_start(scratch[h], rows[:, h, :]).then_inc(bias_rows_out, 16)
            act.wait_ge(bias_rows_out, 16 * H)
            with nc.allow_non_contiguous_dma(reason="a skewed read"):
                for h in range(H):
                    skew = bass.AP(scratch.tensor, h * P * ML + (-P - MLO), [[ML - 1, P], [1, 2 * P]])
                    act.dma_start(k.bias[:, h, :], skew).then_inc(bias_in, 16)
                for h in range(H):
                    skew = bass.AP(scratch.tensor, h * P * ML + (-PAST - MLO), [[ML - 1, QN], [1, PAST + QN]])
                    act.dma_start(b16[QN * h:QN * h + QN, :], skew).then_inc(bias_in, 16)
            act.wait_ge(bias_in, 16 * 2 * H)
            act.wait_ge(b16_done, 1)
            act.activation(k.sbias[:, :], p16[:, 0:PAST + QN], ACT.Copy).then_inc(b16_sb, 1)

        @block.vector
        def _(dve):
            link = Links(dve, steps)
            link(dve.memset(rel[BUCKETS:BUCKETS + 1, :], NEG))
            dve.wait_ge(small_in, 16 * 13)
            link(dve.tensor_tensor(prod[:, :, :], lams[:, 0:4:2, :], lams[:, 1:4:2, :], ALU.mult))
            link(dve.tensor_reduce(dots[:, :], prod[:, :, :], AX.X, ALU.add))
            link(dve.tensor_copy(relb[:, :, :], over(rel[:, :], P)))
            dve.wait_ge(lam_e, 1)
            link(dve.scalar_tensor_tensor(k.lam[:, :], dots[:, 1:2], -1.0, dots[:, 0:1], ALU.mult, ALU.add))
            link(dve.tensor_scalar(k.lam[:, :], k.lam[:, :], LAM0, None, ALU.add))
            link(dve.tensor_scalar(k.subln[:, :], k.subln[:, :], 1.0 - LAM0, None, ALU.mult))

        @block.tensor
        def _(pe):
            pe.wait_ge(const_in, 16)
            pe.wait_ge(steps, 4)
            for h in range(H):
                pe.matmul(prow[h][:, 0:ML], relb[:, h, :], k.c("hot", BUCKETS + 1), start=True, stop=True).then_inc(rows_done, 1)
            pe.wait_ge(bias_in, 16 * 2 * H)
            pe.matmul(p16[:, 0:PAST + QN], k.c("spread", 4 * QN), b16[:, :], start=True, stop=True).then_inc(b16_done, 1)


def loop3(eng, n, body):
    body(0, True, n == 1)
    if n > 2:
        with eng.Fori(1, n - 1) as i:
            body(i, False, False)
    if n > 1:
        body(n - 1, False, True)


def flat(ap):
    return ap.rearrange("p a n -> p (a n)")


class Stream:

    def __init__(self, k, pre, sb, used, begun=None):
        self.raw = begun[0] if begun else [sb(f"raw{u}", [P, KC, P]) for u in range(2)]
        self.hi, self.lo = ([sb(f"{s}{u}", [P, KC, P], F32R) for u in range(2)] for s in ("hi", "lo"))
        self.raw_in, self.hi_ready, self.lo_ready = ([k.sem(f"{pre}_{s}{u}") for u in range(2)]
                                                     for s in ("raw_in", "hi_ready", "lo_ready"))
        self.sp_held = k.sem(f"{pre}_sp_held")
        self.used = used
        if begun:
            self.raw_in = begun[1]

    def load(self, sp, u, i, src, first):
        if not first:
            hold(sp, self.lo_ready[u], i, self.sp_held)
        sp.dma_start(self.raw[u][:, 0:src.shape[1], :], src).then_inc(self.raw_in[u], 16)

    def high(self, act, u, i, kc, first):
        act.wait_ge(self.raw_in[u], 16 * i + 16)
        if not first:
            act.wait_ge(self.used[u], i)
        act.activation(self.hi[u][:, 0:kc, :], self.raw[u][:, 0:kc, :], ACT.Copy).then_inc(self.hi_ready[u], 1)

    def low(self, dve, u, i, kc):
        dve.wait_ge(self.hi_ready[u], i + 1)
        dve.tensor_tensor(self.lo[u][:, 0:kc, :], self.raw[u][:, 0:kc, :], self.hi[u][:, 0:kc, :].bitcast(F32),
                          ALU.subtract).then_inc(self.lo_ready[u], 1)

    def multiply(self, pe, u, i, ps, actH, actL, kc, part=None):
        pe.wait_ge(self.lo_ready[u], i + 1)
        for b in range(NB):
            cols = slice(b * BW, (b + 1) * BW)
            for c in part or range(kc):
                three(pe, ps[:, b, 0:BW], (self.hi[u][:, c, :], self.lo[u][:, c, :]), (actH[:, c, cols], actL[:, c, cols]),
                      c == 0, c == kc - 1, self.used[u] if b == NB - 1 else None)


def three(pe, out, w, a, start, stop, done=None):
    pe.matmul(out, w[0], a[0], start=start, stop=False)
    pe.matmul(out, w[0], a[1], start=False, stop=False)
    ins = pe.matmul(out, w[1], a[0], start=False, stop=stop)
    if stop and done is not None:
        ins.then_inc(done, 1)


def turn_stage(k):
    nc, d = k.nc, k.d
    with ExitStack() as ctx:
        sem = lambda n: k.sem(f"tx_{n}")
        turned, stored = (sem(s) for s in ("turned", "stored"))
        pt = k.ps(ctx, "tx_pt", 4)
        block = ctx.enter_context(nc.Block())
        n_of = lambda t: P if t < PT else NS

        @block.sync
        def _(sp):
            sp.wait_ge(stored, 2 * (PT + 1))
            sp.dma_start(k.xT_dram.rearrange("c p n -> p c n"), k.xT[:, :, :]).then_inc(k.x_spilled, 16)

        @block.tensor
        def _(pe):
            for t in range(PT + 1):
                n = n_of(t)
                pe.wait_ge(k.x_in[t // 2], 16)
                if t >= 2:
                    pe.wait_ge(stored, 2 * (t - 1))
                for c in range(KC):
                    ins = pe.transpose(pt[:, 2 * (t % 2) + c // 4, c % 4 * P:c % 4 * P + n], k.x[0:n, t, c * P:c * P + P], k.c("ident", n)[:, 0:n])
                ins.then_inc(turned, 1)

        def store(eng, copy, half):
            for t in range(PT + 1):
                n = n_of(t)
                eng.wait_ge(turned, t + 1)
                if t:
                    eng.wait_ge(stored, 2 * t)
                copy(k.xT[:, 4 * half:4 * half + 4, t * P:t * P + n], hd(pt[:, 2 * (t % 2) + half, :])[:, :, 0:n]).then_inc(stored, 1)

        @block.scalar
        def _(act):
            store(act, lambda o, i: act.activation(o, i, ACT.Copy), 0)

        @block.vector
        def _(dve):
            store(dve, lambda o, i: dve.tensor_copy(o, i), 1)


def norm_stage(k, pre, xT, weight, hH, hL, sb, pad):
    nc = k.nc
    with ExitStack() as ctx:
        sem = lambda n: k.sem(f"{pre}_{n}")
        squared, summed, steps, rooted, scaled, high, low, low_pool, padded = (
            sem(n) for n in ("squared", "summed", "steps", "rooted", "scaled", "high", "low", "low_pool", "padded"))
        sq = sb("sq", [P, 2, T])
        rb = sb("rb", [P, T])
        ps = k.ps(ctx, f"{pre}_ps", 3)
        block = ctx.enter_context(nc.Block())
        banks = lambda ap: ap.rearrange("p (b n) -> p b n", b=NB)

        if pad:
            @block.sync
            def _(sp):
                sp.wait_ge(k.x_spilled, 16)

        @block.scalar
        def _(act):
            for c in range(KC):
                if c >= 2:
                    act.wait_ge(summed, c - 1)
                act.activation(sq[:, c % 2, :], xT[:, c, :], ACT.Square).then_inc(squared, 1)
            act.wait_ge(steps, 1)
            act.activation(rb[:, :], rb[:, :], ACT.Sqrt).then_inc(rooted, 1)
            for c in range(KC):
                act.wait_ge(scaled, c + 1)
                act.activation(hH[:, c, 0:T], sq[:, c % 2, :], ACT.Copy).then_inc(high, 1)

        @block.tensor
        def _(pe):
            for c in range(KC):
                pe.wait_ge(squared, c + 1)
                for b in range(NB):
                    ins = pe.matmul(ps[:, b, 0:BW], k.c("ones"), sq[:, c % 2, b * BW:(b + 1) * BW], start=(c == 0), stop=(c == KC - 1))
                ins.then_inc(summed, 1)

        @block.gpsimd
        def _(pool):
            if pad:
                for buf in (hH, hL):
                    pool.memset(buf[:, :, T:TPAD].bitcast(F32), 0.0).then_inc(padded, 1)
            for c in range(1, KC, 2):
                pool.wait_ge(high, c + 1)
                pool.tensor_tensor(hL[:, c, 0:T], sq[:, 1, :], hH[:, c, 0:T].bitcast(F32), ALU.subtract).then_inc(low_pool, 1)

        @block.vector
        def _(dve):
            link = Links(dve, steps)
            dve.wait_ge(summed, KC)
            link(dve.tensor_scalar(banks(rb[:, :]), ps[:, :, 0:BW], 1.0 / D, EPS, ALU.mult, ALU.add))
            dve.wait_ge(rooted, 1)
            link(dve.reciprocal(rb[:, :], rb[:, :]))

            def lower(c):
                dve.wait_ge(high, c + 1)
                dve.tensor_tensor(hL[:, c, 0:T], sq[:, 0, :], hH[:, c, 0:T].bitcast(F32), ALU.subtract).then_inc(low, 1)

            for c in range(KC):
                if c >= 2:
                    dve.wait_ge(*((low_pool, c // 2) if c % 2 else (low, c // 2)))
                dve.scalar_tensor_tensor(sq[:, c % 2, :], xT[:, c, :], weight[:, c:c + 1], rb[:, :], ALU.mult, ALU.mult).then_inc(scaled, 1)
                if c % 2:
                    lower(c - 1)


def conv_proj_stage(k):
    nc, d = k.nc, k.d
    R = TA - 1
    RAW = R + SEQ + NSEQ * (R + QN)
    OUT = RAW - R
    NH = NSEQ * R
    LAST = R + NSEQ * R
    with ExitStack() as ctx:
        sem = lambda n: k.sem(f"cv_{n}")
        proj_done = [sem(f"proj{u}") for u in range(2)]
        evac_done = [sem(f"evac{u}") for u in range(2)]
        conv_done = [sem(f"conv{u}") for u in range(2)]
        act_done = [sem(f"silu{u}") for u in range(2)]
        rows_out = [sem(f"rows_out{u}") for u in range(2)]
        saved, taps_in, taps_turned, taps_sb, zeroed, last_turned, last_sb, last_out, chain, pool_held = (
            sem(n) for n in ("saved", "taps_in", "taps_turned", "taps_sb", "zeroed", "last_turned", "last_sb", "last_out", "chain", "pool_held"))
        sb = k.area("cv", M_OA, M_BIAS)
        w = Stream(k, "cv", sb, proj_done)
        k.gate_raw = w.raw
        raw = [sb(f"conv_in{u}", [P, RAW]) for u in range(2)]
        acc = [sb(f"acc{u}", [P, RAW]) for u in range(2)]
        nat = sb("nat", [NH + TA, QKV])
        taps = sb("taps", [P, CA, NH + TA])
        last = sb("last", [P, CA, LAST])
        ps = [k.ps(ctx, f"cv_ps{u}", 3) for u in range(2)]
        pt = k.ps(ctx, "cv_pt", 2)
        samp = [raw[u][:, R + SEQ:RAW].rearrange("p (s c) -> p s c", s=NSEQ) for u in range(2)]
        samp_out = [acc[u][:, R + SEQ:RAW].rearrange("p (s c) -> p s c", s=NSEQ) for u in range(2)]
        w_cols = d["w_in"].rearrange("a (c p) n -> p (a c) n", p=P)
        rows = k.qkvT_dram.rearrange("c p n -> p c n")
        NPAIR = (CA + H) // 2
        CPAIR = CA // 2
        block = ctx.enter_context(nc.Block())

        @block.sync
        def _(sp):
            sp.dma_start(nat[0:NH, :], d["state_conv_a"].rearrange("a s r n -> (a s r) n")).then_inc(taps_in, 16)
            sp.dma_start(nat[NH:NH + TA, :], d["conv_a"].rearrange("a w n -> (a w) n")).then_inc(taps_in, 16)
            for u in range(2):
                w.load(sp, u, 0, w_cols[:, :, u * P:u * P + P], True)

            def step(i, first, last_step):
                for u in range(2):
                    if not last_step:
                        w.load(sp, u, i + 1, w_cols[:, :, at((2 * i + 2 + u) * P, P)], False)

            def out(i):
                for u in range(2):
                    hold(sp, act_done[u], i + 1, w.sp_held)
                    c = 2 * i + u
                    sp.dma_start(flat(rows[:, at(c), 0:SEQ]), acc[u][:, 0:SEQ]).then_inc(rows_out[u], 16)
                    sp.dma_start(rows[:, at(c), SEQ:T].rearrange("p a (s c) -> p (a s) c", s=NSEQ),
                                 samp_out[u][:, :, 0:QN]).then_inc(rows_out[u], 16)

            def both(i, first):
                step(i, first, False)
                out(i)

            loop(sp, CPAIR, both)
            step(CPAIR, False, False)
            for u in range(2):
                sp.wait_ge(w.lo_ready[u], NPAIR)
                sp.dma_start(w.raw[u][:, :, :], w_cols[:, :, C_GA + u * D:C_GA + u * D + P]).then_inc(k.gate_w_in[u], 16)
            for u in range(2):
                sp.wait_ge(rows_out[u], 32 * CPAIR)
            sp.wait_ge(last_sb, 3)
            sp.dma_start(d["conv_a_prompt"].rearrange("a b r n -> (a b r) n"), nat[0:R, :]).then_inc(last_out, 16)
            sp.dma_start(d["conv_a_sample"].rearrange("a s r n -> (a s r) n"), nat[R:LAST, :]).then_inc(last_out, 16)
            sp.wait_ge(last_out, 32)

        @block.tensor
        def _(pe):
            pe.wait_ge(taps_in, 32)
            for c in range(CA):
                if c >= 2:
                    pe.wait_ge(taps_sb, c - 1)
                pe.transpose(pt[:, c % 2, 0:NH + TA], nat[:, c * P:(c + 1) * P], k.c("ident", NH + TA)[:, 0:NH + TA]).then_inc(taps_turned, 1)

            def chunks(i, first):
                for u in range(2):
                    if not first:
                        pe.wait_ge(evac_done[u], i)
                    w.multiply(pe, u, i, ps[u], k.hH, k.hL, KC)

            loop(pe, NPAIR, chunks)
            pe.wait_ge(saved, 2 * CA)
            for c in range(CA):
                if c >= 8:
                    pe.wait_ge(last_sb, 1)
                ins = pe.transpose(pt[0:LAST, c // 4 % 2, c % 4 * P:c % 4 * P + P], last[:, c, :], k.c("ident"))
                if c % 4 == 3:
                    ins.then_inc(last_turned, 1)

        @block.scalar
        def _(act):
            for u in range(2):
                w.high(act, u, 0, KC, True)

            def conv(i, first, final):
                for u in range(2):
                    act.wait_ge(proj_done[u], i + 1)
                    w.high(act, u, i + 1, KC, False)
                    if not first:
                        act.wait_ge(conv_done[u], i)
                        act.wait_ge(saved, 2 * (2 * i + u - 1))
                    for b in range(NB):
                        lo, hi = b * BW, min(SEQ, (b + 1) * BW)
                        act.activation(raw[u][:, R + lo:R + hi], ps[u][:, b, 0:hi - lo], ACT.Copy)
                    act.activation(samp[u][:, :, R:R + QN], ps[u][:, NB - 1, BW - NS:BW].rearrange("p (s c) -> p s c", s=NSEQ),
                                   ACT.Copy).then_inc(evac_done[u], 1)
                for u in range(2):
                    act.wait_ge(conv_done[u], i + 1)
                    act.activation(acc[u][:, 0:OUT], acc[u][:, 0:OUT], ACT.Silu).then_inc(act_done[u], 1)

            loop3(act, CPAIR, conv)
            for j in range(H // 2):
                i = j + CPAIR
                for u in range(2):
                    act.wait_ge(proj_done[u], i + 1)
                    if i + 1 < NPAIR:
                        w.high(act, u, i + 1, KC, False)
                    for b in range(NB):
                        ins = act.activation(k.zT[:, 2 * j + u, b * BW:(b + 1) * BW], ps[u][:, b, 0:BW], ACT.Silu)
                    ins.then_inc(evac_done[u], 1)

        @block.gpsimd
        def _(pool):
            def save(i, first):
                for u in range(2):
                    hold(pool, evac_done[u], i + 1, pool_held)
                    c = 2 * i + u
                    pool.tensor_copy(flat(last[:, at(c), 0:R]), raw[u][:, SEQ:SEQ + R]).then_inc(saved, 1)
                    pool.tensor_copy(last[:, at(c), R:LAST].rearrange("p a (s c) -> p (a s) c", s=NSEQ),
                                     samp[u][:, :, QN:QN + R]).then_inc(saved, 1)

            loop(pool, CPAIR, save)

        @block.vector
        def _(dve):
            for u in range(2):
                dve.memset(raw[u][:, 0:R], 0.0).then_inc(zeroed, 1)
                w.low(dve, u, 0, KC)
            for c in range(CA):
                dve.wait_ge(taps_turned, c + 1)
                dve.tensor_copy(taps[:, c, :], pt[:, c % 2, 0:NH + TA]).then_inc(taps_sb, 1)
            dve.wait_ge(taps_sb, CA)
            dve.wait_ge(zeroed, 2)

            def conv(i, first):
                link = Links(dve, chain, 2 * (TA + 1) * i)
                for u in range(2):
                    c = 2 * i + u
                    w.low(dve, u, i + 1, KC)
                    dve.wait_ge(evac_done[u], i + 1)
                    if not first:
                        dve.wait_ge(rows_out[u], 32 * i)
                    link(dve.tensor_copy(samp[u][:, :, 0:R], taps[:, at(c), 0:NH].rearrange("p a (s r) -> p (a s) r", s=NSEQ)))
                    link(dve.tensor_scalar(acc[u][:, 0:OUT], raw[u][:, 0:OUT], flat(taps[:, at(c), NH:NH + 1]), None, ALU.mult))
                    for t in range(1, TA):
                        link(dve.scalar_tensor_tensor(acc[u][:, 0:OUT], raw[u][:, t:t + OUT], flat(taps[:, at(c), NH + t:NH + t + 1]),
                                                      acc[u][:, 0:OUT], ALU.mult, ALU.add))
                    dve.sem_inc(conv_done[u], 1)

            loop(dve, CPAIR, conv)
            for u in range(2):
                w.low(dve, u, CPAIR + 1, KC)
            for g in range(CA // 4):
                dve.wait_ge(last_turned, g + 1)
                dve.tensor_copy(nat[0:LAST, g * W:(g + 1) * W], pt[0:LAST, g % 2, :]).then_inc(last_sb, 1)


def gate_proj_stage(k):
    nc, d = k.nc, k.d
    with ExitStack() as ctx:
        sem = lambda n: k.sem(f"gp_{n}")
        proj_done = [sem(f"proj{u}") for u in range(2)]
        evac_done = [sem(f"evac{u}") for u in range(2)]
        rows_out = [sem(f"rows_out{u}") for u in range(2)]
        sb = k.area("gp", M_OA + 2 * KC * P * 4, M_BIAS)
        w = Stream(k, "gp", sb, proj_done, (k.gate_raw, k.gate_w_in))
        sig = [sb(f"sig{u}", [P, T]) for u in range(2)]
        ps = [k.ps(ctx, f"gp_ps{u}", 3) for u in range(2)]
        w_cols = d["w_in"].rearrange("a (c p) n -> p (a c) n", p=P)
        rows = k.gate_dram.rearrange("c p n -> p c n")
        block = ctx.enter_context(nc.Block())

        @block.sync
        def _(sp):
            def step(i, first, final):
                if not final:
                    for u in range(2):
                        w.load(sp, u, i + 1, w_cols[:, :, at(i * P + (C_GA + u * D + P), P)], False)
                for u in range(2):
                    hold(sp, evac_done[u], i + 1, w.sp_held)
                    sp.dma_start(flat(rows[:, at(i + u * KC), :]), sig[u][:, :]).then_inc(rows_out[u], 16)

            loop3(sp, KC, step)
            for u in range(2):
                sp.wait_ge(rows_out[u], 16 * KC)

        @block.tensor
        def _(pe):
            def step(i, first):
                for u in range(2):
                    if not first:
                        pe.wait_ge(evac_done[u], i)
                    w.multiply(pe, u, i, ps[u], k.hH, k.hL, KC)

            loop(pe, KC, step)

        @block.scalar
        def _(act):
            for u in range(2):
                w.high(act, u, 0, KC, True)

            def step(i, first, final):
                for u in range(2):
                    act.wait_ge(proj_done[u], i + 1)
                    if not final:
                        w.high(act, u, i + 1, KC, False)
                    if not first:
                        act.wait_ge(rows_out[u], 16 * i)
                    for b in range(NB):
                        ins = act.activation(sig[u][:, b * BW:(b + 1) * BW], ps[u][:, b, 0:BW], ACT.Sigmoid)
                    ins.then_inc(evac_done[u], 1)

            loop3(act, KC, step)

        @block.vector
        def _(dve):
            for u in range(2):
                w.low(dve, u, 0, KC)

            def step(i):
                for u in range(2):
                    w.low(dve, u, i, KC)

            with dve.Fori(1, KC) as i:
                step(i)


def gates_stage(k):
    nc, d = k.nc, k.d
    with ExitStack() as ctx:
        sem = lambda n: k.sem(f"gt_{n}")
        proj_done, steps, acts = (sem(n) for n in ("proj", "steps", "acts"))
        sb = k.area("gt", M_OA, M_BIAS)
        wb, w_loaded = k.wba, k.wba_in
        wH, wL = (sb(s, [P, KC, P], F32R) for s in ("wH", "wL"))
        baT = sb("baT", [P, TPAD])
        split, turned_in, padded = (sem(s) for s in ("split", "turned_in", "padded"))
        ba = sb("ba", [P, PT + 1, 2 * H])
        th, aa, mod = (sb(s, [P, PT + 1, H]) for s in ("th", "aa", "mod"))
        psT = k.ps(ctx, "gt_psT", 3)
        ps = k.ps(ctx, "gt_ps")
        psv = ps[:, 0:(PT + 1) * 2 * H].rearrange("p (t n) -> p t n", t=PT + 1)
        block = ctx.enter_context(nc.Block())

        @block.tensor
        def _(pe):
            pe.wait_ge(split, 2)
            for b in range(NB):
                cols = slice(b * BW, (b + 1) * BW)
                for c in range(KC):
                    three(pe, psT[:, b, 0:BW], (wH[:, c, :], wL[:, c, :]), (k.hH[:, c, cols], k.hL[:, c, cols]), c == 0, c == KC - 1,
                          turned_in)
            pe.wait_ge(padded, 3 + NB)
            for t in range(PT + 1):
                ins = pe.transpose(psv[:, t, :], baT[0:2 * H, t * P:t * P + P], k.c("ident", 2 * H)[:, 0:2 * H])
            ins.then_inc(proj_done, 1)

        @block.scalar
        def _(act):
            for b in range(NB):
                act.wait_ge(turned_in, b + 1)
                act.activation(baT[:, b * BW:(b + 1) * BW], psT[:, b, 0:BW], ACT.Copy).then_inc(padded, 1)
            act.wait_ge(steps, 1)
            act.activation(th[:, :, :], ba[:, :, 0:H], ACT.Tanh, scale=0.5).then_inc(acts, 1)
            act.activation(k.alog[:, :], k.alog[:, :], ACT.Exp).then_inc(acts, 1)
            act.wait_ge(steps, 4)
            act.activation(mod[:, :, :], mod[:, :, :], ACT.Exp, scale=-1.0).then_inc(acts, 1)
            act.wait_ge(acts, 3)
            act.activation(mod[:, :, :], mod[:, :, :], ACT.Ln, bias=1.0).then_inc(acts, 1)

        @block.vector
        def _(dve):
            link = Links(dve, steps)
            dve.memset(baT[:, T:TPAD], 0.0).then_inc(padded, 1)
            for buf in (wH, wL):
                dve.memset(buf[:, :, 2 * H:P].bitcast(F32), 0.0).then_inc(padded, 1)
            dve.wait_ge(w_loaded, 16)
            dve.tensor_copy(wH[:, :, 0:2 * H], wb[:, :, :]).then_inc(split, 1)
            dve.wait_ge(split, 1)
            dve.wait_ge(padded, 3)
            dve.tensor_tensor(wL[:, :, 0:2 * H], wb[:, :, :], wH[:, :, 0:2 * H].bitcast(F32), ALU.subtract).then_inc(split, 1)
            dve.wait_ge(proj_done, 1)
            link(dve.tensor_copy(ba[:, :, :], psv[:, :, :]))
            link(dve.tensor_tensor(aa[:, :, :], ba[:, :, H:2 * H], repeat(k.dtb[:, :], PT + 1), ALU.add))
            link(dve.tensor_scalar(mod[:, :, :], aa[:, :, :], -1.0, None, ALU.mult))
            link(dve.tensor_tensor(mod[:, :, :], mod[:, :, :], aa[:, :, :], ALU.max))
            dve.wait_ge(acts, 4)
            link(dve.tensor_scalar(k.beta[:, :, :], th[:, :, :], 0.5, 0.5, ALU.mult, ALU.add))
            link(dve.scalar_tensor_tensor(mod[:, :, :], aa[:, :, :], 0.0, mod[:, :, :], ALU.max, ALU.add))
            link(dve.tensor_tensor(mod[:, :, :], mod[:, :, :], repeat(k.alog[:, :], PT + 1), ALU.mult))
            link(dve.tensor_scalar(k.g[:, :, :], mod[:, :, :], -1.0, None, ALU.mult))


def delta_stage(k, sample):
    nc, d = k.nc, k.d
    pre = "ds" if sample else "dp"
    n = NS if sample else P
    levels = SLEVELS if sample else LEVELS
    steps = 1 if sample else PT
    HN = H * n
    tri, neglow = ("s_triu", "s_neglow") if sample else ("triu", "neglow")
    tot = "s_same" if sample else "ones"
    with ExitStack() as ctx:
        sem = lambda s: k.sem(f"{pre}_{s}")
        (staged, gb_staged, identity_set, raw_turned, sums_done, gp_ready, row_done, gc_done, negd_ready, kdx_ready, exps_done,
         masks_done, qk_scaled, kv_scaled, qk_turned, qkT_ready, qg_ready, kk_done, m_ready, a_ready, x_done,
         xs_ready, zu_done, zl_done, level_done, w_done, w_ready, v_done, v_ready, o_done, su_done, s_ready,
         osum_done, o_scaled, o_turned, out_ready, chain, pchain, achain, upd_done, state_in, state_out, held, pool_held) = (sem(s) for s in (
             "staged", "gb_staged", "identity_set", "raw_turned", "sums", "gp", "row", "gc", "negd", "kdx", "exps", "masks",
             "qk_scaled", "kv_scaled", "qk_turned", "qkT", "qg", "kk", "m", "a", "x", "xs", "zu", "zl", "level",
             "w", "w_ready", "v", "v_ready", "o", "su", "s", "osum", "o_scaled", "o_turned", "out", "chain",
             "pchain", "achain", "upd", "state_in", "state_out", "held", "pool_held"))
        sb = k.area(pre, M_H, M_QKV)
        stage_in = sem("stage_in")
        on_split = sem("on_split")
        stage = sb("stage", [P, CA, n])
        gb = sb("gb", [n, 2 * H])
        gp = sb("gp", [n, HN])
        gcs = sb("gcs", [n, 2 * H])
        kdx, eg, ekd, nbe = (sb(s, [n, H]) for s in ("kdx", "eg", "ekd", "nbe"))
        negd, es, esl, esu = (sb(s, [n, HN]) for s in ("negd", "es", "esl", "esu"))
        er = sb("er", [P, HN])
        ss, r, work = (sb(s, [n, 2 * H]) for s in ("ss", "r", "work"))
        junk = sb("junk", [P, 2, P])
        qn, kn, vb, kbg, kd = (sb(s, [n, W]) for s in ("qn", "kn", "vb", "kbg", "kd"))
        qT, kT, qgT, wT = (sb(s, [P, HN]) for s in ("qT", "kT", "qgT", "wT"))
        m, aT, U, L, xs = (sb(s, [n, HN]) for s in ("m", "aT", "U", "L", "xs"))
        vn = sb("vn", [n, W])
        B = [k.ps(ctx, f"{pre}_b{i}") for i in range(8)]
        S = sb("S", [P, NSEQ * H if sample else H, DH])
        egl = sb("egl", [P, NSEQ * H if sample else H])
        if sample:
            gm = sb("gm", [n, NSEQ, H])
            uT, vnT, oT, sq = (sb(s, [P, HN]) for s in ("uT", "vnT", "oT", "sq"))
            rT, workT = (sb(s, [P, HN]) for s in ("rT", "workT"))
            vm = sb("vm", [n, H, NSEQ * DH])
        else:
            on = sb("on", [n, W])
            so, ro, worko = (sb(s, [n, H]) for s in ("so", "ro", "worko"))
        ident = k.c("ident")
        block = ctx.enter_context(nc.Block())

        def tiles(eng, body):
            if sample:
                body(PT, 0, True)
            else:
                body(0, 0, True)
                with eng.Fori(1, steps) as t:
                    body(t, t, False)

        def cols(t):
            return at(t * P, n)

        @block.sync
        def _(sp):
            rows = k.qkvT_dram.rearrange("c p n -> p c n")

            def stage_load(t, i, first):
                if not first:
                    hold(sp, raw_turned, i, staged)
                sp.dma_start(stage[:, :, :], rows[:, :, cols(t)]).then_inc(stage_in, 16)

            tiles(sp, stage_load)
            if sample:
                sp.dma_start(S[:, :, :], d["state_delta"].rearrange("a s h p n -> p (a s h) n")).then_inc(state_in, 16)
                sp.wait_ge(s_ready, 1)
                sp.dma_start(d["delta_sample"].rearrange("a s h p n -> p (a s h) n"), S[:, :, :]).then_inc(state_out, 16)
            else:
                sp.wait_ge(s_ready, steps)
                sp.dma_start(d["delta_prompt"].rearrange("a b h p n -> p (a b h) n"), S[:, :, :]).then_inc(state_out, 16)
            sp.wait_ge(state_out, 16)

        @block.gpsimd
        def _(pool):
            def tile(t, i, first):
                if not first:
                    pool.wait_ge(kv_scaled, i)
                    hold(pool, gc_done, i, pool_held)
                pool.tensor_copy(gb[:, 0:H], k.g[0:n, at(t), :].rearrange("p a n -> p (a n)")).then_inc(gb_staged, 1)
                pool.tensor_copy(gb[:, H:2 * H], k.beta[0:n, at(t), :].rearrange("p a n -> p (a n)")).then_inc(gb_staged, 1)
                if not first:
                    hold(pool, v_done, i, pool_held)
                for buf in (U, L):
                    pool.tensor_copy(hd(buf[:, :]), repeat(ident[0:n, 0:n], H)).then_inc(identity_set, 1)
                pool.wait_ge(exps_done, i + 1)
                link = Links(pool, pchain, 3 * i)
                if not first:
                    pool.wait_ge(m_ready, i)
                link(pool.tensor_tensor(hd(esl[:, :]), hd(es[:, :]), repeat(k.c(neglow, n), H), ALU.mult))
                link(pool.tensor_tensor(hd(esl[:, :]), hd(esl[:, :]), over(gb[:, H:2 * H], n), ALU.mult))
                if not first:
                    pool.wait_ge(a_ready, i)
                link(pool.tensor_tensor(hd(esu[:, :]), hd(es[:, :]), repeat(k.c(tri, n), H), ALU.mult))
                pool.sem_inc(masks_done, 1)
                pool.wait_ge(qkT_ready, i + 1)
                if not first:
                    pool.wait_ge(o_done, i)
                pool.tensor_tensor(qgT[:, :], qT[:, :], er[:, :], ALU.mult).then_inc(qg_ready, 1)

            tiles(pool, tile)

        @block.tensor
        def _(pe):
            if sample:
                pe.wait_ge(state_in, 16)

            def tile(t, i, first):
                pe.wait_ge(stage_in, 16 * i + 16)
                pe.wait_ge(gb_staged, 2 * i + 2)
                if not first:
                    pe.wait_ge(level_done, (2 * levels - 1) * i)
                    pe.wait_ge(v_ready, i)
                    pe.wait_ge(out_ready, i)
                    pe.wait_ge(s_ready, i)
                for c in range(CA):
                    ins = pe.transpose(B[c // H][0:n, c % H * P:c % H * P + P], stage[:, c, :], ident)
                ins.then_inc(raw_turned, 1)
                pe.wait_ge(gp_ready, i + 1)
                pe.matmul(B[3][:, 0:HN], k.c("ones", n), gp[:, :], start=True, stop=True).then_inc(row_done, 1)
                pe.matmul(B[4][0:n, 0:H], k.c(tri, n)[:, 0:n], gb[:, 0:H], start=True, stop=True)
                ins = pe.matmul(B[4][0:n, H:2 * H], k.c(tot, n)[:, 0:n], gb[:, 0:H], start=True, stop=True)
                if sample:
                    ins = pe.matmul(B[4][:, 2 * H:2 * H + NSEQ * H], k.c("ones", n), gm[:, :, :].rearrange("p s h -> p (s h)"), start=True, stop=True)
                ins.then_inc(gc_done, 1)
                pe.wait_ge(qk_scaled, i + 1)
                for h in range(H):
                    pe.transpose(B[5][:, h * n:h * n + n], qn[:, h * P:h * P + P], ident[0:n, 0:n])
                for h in range(H):
                    ins = pe.transpose(B[6][:, h * n:h * n + n], kn[:, h * P:h * P + P], ident[0:n, 0:n])
                ins.then_inc(qk_turned, 1)
                pe.wait_ge(qkT_ready, i + 1)
                for h in range(H):
                    s = slice(h * n, h * n + n)
                    pe.matmul(B[0][0:n, s], kT[:, s], kT[:, s], start=True, stop=True)
                for h in range(H):
                    s = slice(h * n, h * n + n)
                    ins = pe.matmul(B[1][0:n, s], kT[:, s], qT[:, s], start=True, stop=True)
                ins.then_inc(kk_done, 1)
                pe.wait_ge(m_ready, i + 1)
                pe.wait_ge(kv_scaled, i + 1)
                for l in range(levels):
                    if l:
                        pe.wait_ge(level_done, (2 * levels - 1) * i + 2 * l)
                    if l == 1:
                        pe.wait_ge(a_ready, i + 1)
                    for h in range(H):
                        s = slice(h * n, h * n + n)
                        ins = pe.matmul(B[2][0:n, s], m[:, s], U[:, s] if l else ident[0:n, 0:n], start=True, stop=True)
                    ins.then_inc(x_done, 1)
                    if l:
                        pe.wait_ge(xs_ready, (levels - 1) * i + l)
                        for h in range(H):
                            s = slice(h * n, h * n + n)
                            ins = pe.matmul(B[0][0:n, s], L[:, s], xs[:, s], start=True, stop=True)
                        ins.then_inc(zu_done, 1)
                        if l < levels - 1:
                            for h in range(H):
                                s = slice(h * n, h * n + n)
                                ins = pe.matmul(B[1][0:n, s], xs[:, s], L[:, s], start=True, stop=True)
                            ins.then_inc(zl_done, 1)
                pe.wait_ge(level_done, (2 * levels - 1) * (i + 1))
                for h in range(H):
                    ins = pe.matmul(B[3][:, h * n:h * n + n], kbg[:, h * P:h * P + P], U[:, h * n:h * n + n], start=True, stop=True)
                ins.then_inc(w_done, 1)
                if not sample:
                    pe.wait_ge(w_ready, i + 1)
                    if not first:
                        pe.wait_ge(s_ready, i)
                    else:
                        pe.wait_ge(chain, 1)
                    for h in range(H):
                        s = slice(h * P, h * P + P)
                        pe.matmul(B[4][:, s], U[:, s], vb[:, s], start=True, stop=False)
                        ins = pe.matmul(B[4][:, s], wT[:, s], S[:, h, :], start=False, stop=True)
                    ins.then_inc(v_done, 1)
                    pe.wait_ge(v_ready, i + 1)
                    pe.wait_ge(qg_ready, i + 1)
                    for h in range(H):
                        s = slice(h * P, h * P + P)
                        pe.matmul(B[5][:, s], qgT[:, s], S[:, h, :], start=True, stop=False)
                        ins = pe.matmul(B[5][:, s], aT[:, s], vn[:, s], start=False, stop=True)
                    ins.then_inc(o_done, 1)
                    for h in range(H):
                        s = slice(h * P, h * P + P)
                        ins = pe.matmul(B[6][:, s], kd[:, s], vn[:, s], start=True, stop=True)
                    ins.then_inc(su_done, 1)
                    pe.wait_ge(o_scaled, i + 1)
                    for h in range(H):
                        s = slice(h * P, h * P + P)
                        ins = pe.transpose(B[7][:, s], on[:, s], ident)
                    ins.then_inc(o_turned, 1)
                else:
                    for h in range(H):
                        pe.matmul(B[7][:, h * n:h * n + n], vb[:, h * P:h * P + P], U[:, h * n:h * n + n], start=True, stop=True)
                    pe.wait_ge(w_ready, 1)
                    pe.wait_ge(qg_ready, 1)
                    for h in range(H):
                        for s in range(NSEQ):
                            c = h * n + s * QN
                            pe.matmul(B[2][:, c:c + QN], S[:, s * H + h, :], wT[:, c:c + QN], start=True, stop=True)
                            ins = pe.matmul(B[2][:, HN + c:HN + c + QN], S[:, s * H + h, :], qgT[:, c:c + QN], start=True, stop=True)
                    ins.then_inc(v_done, 1)
                    pe.wait_ge(v_ready, 1)
                    for h in range(H):
                        ins = pe.transpose(B[3][0:n, h * P:h * P + P], vnT[:, h * n:h * n + n], ident)
                    ins.then_inc(x_done, 1)
                    pe.wait_ge(v_ready, 2)
                    for h in range(H):
                        ins = pe.matmul(B[7][:, h * n:h * n + n], vn[:, h * P:h * P + P], aT[:, h * n:h * n + n], start=True, stop=True)
                    ins.then_inc(o_done, 1)
                    pe.wait_ge(o_scaled, 1)
                    pe.matmul(B[4][:, 0:HN], k.c("ones"), sq[:, :], start=True, stop=True).then_inc(o_turned, 1)
                    pe.wait_ge(v_ready, 3)
                    for h in range(H):
                        for half in range(2):
                            u = 2 * h + half
                            if u >= 2:
                                pe.wait_ge(upd_done, u - 1)
                            pe.matmul(B[5 + half][:, :], kd[:, h * P:h * P + P], vm[:, h, half * 512:half * 512 + 512],
                                      start=True, stop=True).then_inc(su_done, 1)

            tiles(pe, tile)

        @block.scalar
        def _(act):
            def tile(t, i, first):
                link = Links(act, achain, (2 * H + (0 if sample else H)) * i)
                act.wait_ge(raw_turned, i + 1)
                if not first:
                    act.wait_ge(kv_scaled, i)
                for h in range(2 * H):
                    link(act.activation(junk[0:n, 0, :], B[h // H][0:n, h % H * P:h % H * P + P], ACT.Square, accum_out=ss[:, h:h + 1]))
                act.sem_inc(sums_done, 1)
                act.wait_ge(negd_ready, i + 1)
                if not first:
                    act.wait_ge(s_ready, i)
                act.activation(er[:, :], B[3][:, 0:HN], ACT.Exp)
                act.activation(eg[:, :], B[4][0:n, 0:H], ACT.Exp)
                if sample:
                    act.activation(egl[:, :], B[4][:, 2 * H:2 * H + NSEQ * H], ACT.Exp)
                else:
                    act.activation(egl[:, :], B[4][:, H:2 * H], ACT.Exp)
                if not first:
                    act.wait_ge(masks_done, i)
                act.activation(es[:, :], negd[:, :], ACT.Exp)
                act.wait_ge(kdx_ready, i + 1)
                act.activation(ekd[:, :], kdx[:, :], ACT.Exp).then_inc(exps_done, 1)
                act.wait_ge(qk_turned, i + 1)
                act.activation(qT[:, :], B[5][:, 0:HN], ACT.Copy)
                act.activation(kT[:, :], B[6][:, 0:HN], ACT.Copy).then_inc(qkT_ready, 1)
                for l in range(1, levels):
                    act.wait_ge(x_done, levels * i + l + 1)
                    if l >= 2:
                        act.wait_ge(zl_done, (levels - 2) * i + l - 1)
                    act.activation(xs[:, :], B[2][0:n, 0:HN], ACT.Copy).then_inc(xs_ready, 1)
                act.wait_ge(w_done, i + 1)
                act.activation(wT[:, :], B[3][:, 0:HN], ACT.Copy).then_inc(w_ready, 1)
                if not sample:
                    act.wait_ge(v_done, i + 1)
                    act.activation(vn[:, :], B[4][:, :], ACT.Copy).then_inc(v_ready, 1)
                    act.wait_ge(o_done, i + 1)
                    for h in range(H):
                        link(act.activation(junk[:, 0, :], B[5][:, h * P:h * P + P], ACT.Square, accum_out=so[:, h:h + 1]))
                    act.sem_inc(osum_done, 1)

            tiles(act, tile)

        @block.vector
        def _(dve):
            pr = 0 if sample else 1
            if not sample:
                dve.memset(S[:, :, :], 0.0).then_inc(chain, 1)
            per_tile = [0]

            def tile(t, i, first):
                link = Links(dve, chain, pr + per_tile[0] * i)
                dve.wait_ge(gb_staged, 2 * i + 2)
                dve.tensor_tensor(hd(gp[:, :]), repeat(k.c(tri, n)[:, 0:n], H), over(gb[:, 0:H], n), ALU.mult)
                if sample:
                    dve.tensor_tensor(gm[:, :, :], over(k.c("s_seq", n), H), repeat(gb[:, 0:H], NSEQ), ALU.mult).then_inc(gp_ready, 1)
                else:
                    dve.tensor_scalar(nbe[:, :], gb[:, H:2 * H], -1.0, None, ALU.mult).then_inc(gp_ready, 1)
                dve.wait_ge(gc_done, i + 1)
                link(dve.tensor_copy(gcs[:, :], B[4][0:n, 0:2 * H]))
                link(dve.tensor_tensor(hd(negd[:, :]), hd(B[3][0:n, 0:HN]), over(gcs[:, 0:H], n), ALU.subtract))
                link(dve.scalar_tensor_tensor(negd[:, :], negd[:, :], -1.0, negd[:, :], ALU.mult, ALU.min))
                dve.sem_inc(negd_ready, 1)
                link(dve.tensor_tensor(kdx[:, :], gcs[:, H:2 * H], gcs[:, 0:H], ALU.subtract))
                dve.sem_inc(kdx_ready, 1)
                dve.wait_ge(sums_done, i + 1)
                link(dve.tensor_scalar(ss[:, :], ss[:, :], EPS, None, ALU.add))
                rsqrt(dve, link, r[:, :], ss[:, :], work[:, :])
                link(dve.tensor_scalar(r[:, 0:H], r[:, 0:H], DH ** -0.5, None, ALU.mult))
                link(dve.tensor_tensor(hd(qn[:, :]), hd(B[0][0:n, :]), over(r[:, 0:H], P), ALU.mult))
                link(dve.tensor_tensor(hd(kn[:, :]), hd(B[1][0:n, :]), over(r[:, H:2 * H], P), ALU.mult))
                dve.sem_inc(qk_scaled, 1)
                link(dve.tensor_tensor(hd(vb[:, :]), hd(B[2][0:n, :]), over(gb[:, H:2 * H], P), ALU.mult))
                dve.wait_ge(exps_done, i + 1)
                link(dve.scalar_tensor_tensor(nbe[:, :], gb[:, H:2 * H], -1.0, eg[:, :], ALU.mult, ALU.mult))
                link(dve.tensor_tensor(hd(kbg[:, :]), hd(kn[:, :]), over(nbe[:, :], P), ALU.mult))
                link(dve.tensor_tensor(hd(kd[:, :]), hd(kn[:, :]), over(ekd[:, :], P), ALU.mult))
                dve.sem_inc(kv_scaled, 1)
                dve.wait_ge(kk_done, i + 1)
                dve.wait_ge(masks_done, i + 1)
                dve.tensor_tensor(m[:, :], B[0][0:n, 0:HN], esl[:, :], ALU.mult).then_inc(m_ready, 1)
                dve.tensor_tensor(aT[:, :], B[1][0:n, 0:HN], esu[:, :], ALU.mult).then_inc(a_ready, 1)
                dve.wait_ge(m_ready, i + 1)
                dve.wait_ge(identity_set, 2 * i + 2)
                for l in range(levels):
                    up = repeat(k.c(f"up{l}", n)[:, 0:n].bitcast(I32), H)
                    low = repeat(k.c(f"low{l}", n)[:, 0:n].bitcast(I32), H)
                    if l == 0:
                        hold(dve, x_done, levels * i + 1, held)
                        dve.copy_predicated(hd(U[:, :]), up, hd(B[2][0:n, 0:HN])).then_inc(level_done, 1)
                        dve.copy_predicated(hd(L[:, :]), low, hd(m[:, :])).then_inc(level_done, 1)
                    else:
                        dve.wait_ge(level_done, (2 * levels - 1) * i + 2 * l)
                        hold(dve, zu_done, (levels - 1) * i + l, held)
                        dve.copy_predicated(hd(U[:, :]), up, hd(B[0][0:n, 0:HN])).then_inc(level_done, 1)
                        if l < levels - 1:
                            hold(dve, zl_done, (levels - 2) * i + l, held)
                            dve.copy_predicated(hd(L[:, :]), low, hd(B[1][0:n, 0:HN])).then_inc(level_done, 1)
                if not sample:
                    dve.wait_ge(o_done, i + 1)
                    link(dve.tensor_tensor(S[:, :, :], S[:, :, :], over(egl[:, :], DH), ALU.mult))
                    dve.wait_ge(su_done, i + 1)
                    link(dve.tensor_tensor(S[:, :, :], S[:, :, :], hd(B[6][:, :]), ALU.add))
                    dve.sem_inc(s_ready, 1)
                    dve.wait_ge(osum_done, i + 1)
                    link(dve.tensor_scalar(so[:, :], so[:, :], 1.0 / DH, EPS, ALU.mult, ALU.add))
                    rsqrt(dve, link, ro[:, :], so[:, :], worko[:, :])
                    link(dve.tensor_tensor(hd(on[:, :]), hd(B[5][:, :]), over(ro[:, :], P), ALU.mult))
                    dve.sem_inc(o_scaled, 1)
                    dve.wait_ge(o_turned, i + 1)
                    link(dve.tensor_scalar(on[:, :], B[7][:, :], k.onorm[:, 0:1], None, ALU.mult))
                    link(dve.tensor_tensor(hd(on[:, :]), hd(on[:, :]), k.zT[:, :, cols(t)], ALU.mult))
                    link(dve.tensor_copy(k.oaH[:, :, cols(t)], hd(on[:, :])))
                    link(dve.tensor_tensor(k.oaL[:, :, cols(t)], hd(on[:, :]), k.oaH[:, :, cols(t)].bitcast(F32), ALU.subtract))
                    dve.sem_inc(out_ready, 1)
                    per_tile[0] = link.n
                    return
                dve.wait_ge(v_done, 1)
                link(dve.tensor_copy(uT[:, :], B[7][:, 0:HN]))
                dve.tensor_tensor(vnT[:, :], uT[:, :], B[2][:, 0:HN], ALU.add).then_inc(v_ready, 1)
                dve.wait_ge(x_done, levels + 1)
                dve.tensor_copy(vn[:, :], B[3][0:n, :]).then_inc(v_ready, 1)
                dve.wait_ge(v_ready, 2)
                for h in range(H):
                    ins = dve.tensor_tensor(hd(vm[:, h, :], NSEQ), repeat(vn[:, h * P:h * P + P], NSEQ), over(k.c("s_seq", n), DH), ALU.mult)
                ins.then_inc(v_ready, 1)
                dve.wait_ge(o_done, 1)
                link(dve.tensor_copy(oT[:, :], B[7][:, 0:HN]))
                link(dve.tensor_tensor(oT[:, :], oT[:, :], B[2][:, HN:2 * HN], ALU.add))
                dve.tensor_tensor(sq[:, :], oT[:, :], oT[:, :], ALU.mult).then_inc(o_scaled, 1)
                dve.wait_ge(o_turned, 1)
                link(dve.tensor_scalar(rT[:, :], B[4][:, 0:HN], 1.0 / DH, EPS, ALU.mult, ALU.add))
                link(dve.tensor_copy(sq[:, :], rT[:, :]))
                rsqrt(dve, link, rT[:, :], sq[:, :], workT[:, :])
                link(dve.tensor_tensor(oT[:, :], oT[:, :], rT[:, :], ALU.mult))
                link(dve.scalar_tensor_tensor(hd(oT[:, :]), hd(oT[:, :]), k.onorm[:, 0:1], k.zT[:, :, SEQ:T], ALU.mult, ALU.mult))
                link(dve.tensor_copy(k.oaH[:, :, SEQ:T], hd(oT[:, :])))
                link(dve.tensor_tensor(k.oaL[:, :, SEQ:T], hd(oT[:, :]), k.oaH[:, :, SEQ:T].bitcast(F32), ALU.subtract))
                link(dve.tensor_tensor(S[:, :, :], S[:, :, :], over(egl[:, :], DH), ALU.mult))
                for u in range(2 * H):
                    h, half = u // 2, u % 2
                    st = S[:, 4 * H * half + h:4 * H * (half + 1):H, :]
                    dve.wait_ge(su_done, u + 1)
                    ins = dve.tensor_tensor(st, st, hd(B[5 + half][:, :]), ALU.add)
                    ins.then_inc(upd_done, 1) if u < 2 * H - 1 else ins.then_inc(s_ready, 1)

            tiles(dve, tile)


def qkv_stage(k):
    nc, d = k.nc, k.d
    G = 2 * H
    with ExitStack() as ctx:
        sem = lambda s: k.sem(f"qk_{s}")
        w_high, w_low = (sem(s) for s in ("w_high", "w_low"))
        k_out = [sem(f"k_out{u}") for u in range(2)]
        proj_done, copied, steps, normed, turned, stored, v_out, squared, passed = (
            sem(s) for s in ("proj", "copied", "steps", "normed", "turned", "stored", "v_out", "squared", "passed"))
        sb = k.area("qk", M_Z + KC * W * 4, M_BIAS)
        wb, w_loaded = k.wq, k.wq_in
        wH, wL = (sb(s, [P, KC, W], F32R) for s in ("wH", "wL"))
        raw = sb("raw", [P, 2, W])
        sq = sb("sq", [P, W])
        ss, r, work = (sb(s, [P, G]) for s in ("ss", "r", "work"))
        nrm = sb("nrm", [P, 2, W])
        ps = [k.ps(ctx, f"qk_ps{u}") for u in range(4)]
        pt = [k.ps(ctx, f"qk_pt{u}") for u in range(2)]
        w_cols = d["w_in"].rearrange("a (c p) n -> p (a c) n", p=P)
        kp = d["k_prompt"].rearrange("a b t h n -> (a b t) (h n)")
        vp = d["v_prompt"].rearrange("a b t h n -> (a b t) (h n)")
        ks = d["k_sample"].rearrange("a b t h n -> (a b t) (h n)")
        vs = d["v_sample"].rearrange("a b t h n -> (a b t) (h n)")
        block = ctx.enter_context(nc.Block())
        NT = PT + 1
        n_of = lambda t: P if t < PT else NS

        @block.sync
        def _(sp):
            for g in range(1, 3):
                sp.wait_ge(w_low, KC * g)
                sp.dma_start(wb[:, :, :], w_cols[:, :, C_Q + g * W:C_Q + (g + 1) * W]).then_inc(w_loaded, 16)
            for t in range(NT):
                sp.wait_ge(normed, NT + t + 1)
                src = nrm[0:n_of(t), (NT + t) % 2, :]
                sp.dma_start(kp[t * P:t * P + P, :] if t < PT else ks, src).then_inc(k_out[(NT + t) % 2], 16)
            sp.wait_ge(copied, 3 * NT)
            sp.dma_start(vp.rearrange("(t p) n -> p t n", p=P), k.v[:, 0:PT, :]).then_inc(v_out, 16)
            sp.dma_start(vs, k.v[0:NS, PT, :]).then_inc(v_out, 16)
            sp.wait_ge(v_out, 32)
            for u in range(2):
                sp.wait_ge(k_out[u], 16 * ((NT + u) // 2))

        @block.tensor
        def _(pe):
            def turn(j):
                n = n_of(j % NT)
                pe.wait_ge(normed, j + 1)
                if j >= 2:
                    pe.wait_ge(stored, j - 1)
                for h in range(H):
                    ins = pe.transpose(pt[j % 2][:, h * P:h * P + n], nrm[0:n, j % 2, h * P:h * P + P], k.c("ident", n)[:, 0:n])
                ins.then_inc(turned, 1)

            for g in range(3):
                for t in range(NT):
                    j = g * NT + t
                    n = n_of(t)
                    if j >= 4:
                        pe.wait_ge(copied, j - 3)
                    cols = slice(t * P, t * P + P)
                    for c in range(KC):
                        if t == 0:
                            pe.wait_ge(w_low, KC * g + c + 1)
                        three(pe, ps[j % 4][:, :], (k.hH[:, c, cols], k.hL[:, c, cols]), (wH[:, c, :], wL[:, c, :]),
                              c == 0, c == KC - 1, proj_done)
                    if 2 <= j < 2 * NT + 2:
                        turn(j - 2)

        @block.scalar
        def _(act):
            def high(g):
                act.wait_ge(w_loaded, 16 * g + 16)
                if g:
                    act.wait_ge(proj_done, NT * g)
                for c in range(KC):
                    act.activation(wH[:, c, :], wb[:, c, :], ACT.Copy).then_inc(w_high, 1)

            high(0)
            for j in range(3 * NT):
                n = n_of(j % NT)
                act.wait_ge(proj_done, j + 1)
                if j % NT == NT - 1 and j < 2 * NT:
                    high(j // NT + 1)
                if j < 2 * NT:
                    if j >= 2:
                        act.wait_ge(normed, j - 1)
                    act.activation(raw[0:n, j % 2, :], ps[j % 4][0:n, :], ACT.Copy).then_inc(copied, 1)
                    act.wait_ge(copied, j + 1)
                    if j:
                        act.wait_ge(passed, j)
                    act.activation(sq[0:n, :], raw[0:n, j % 2, :], ACT.Square).then_inc(squared, 1)
                else:
                    act.activation(k.v[0:n, j % NT, :], ps[j % 4][0:n, :], ACT.Copy).then_inc(copied, 1)

        @block.vector
        def _(dve):
            def store(j):
                n, t = n_of(j % NT), j % NT
                dst = k.qT if j < NT else k.kT
                dve.wait_ge(turned, j + 1)
                dve.tensor_copy(dst[:, :, t * P:t * P + n], hd(pt[j % 2][:, :])[:, :, 0:n]).then_inc(stored, 1)

            def low(g):
                for c in range(KC):
                    dve.wait_ge(w_high, KC * g + c + 1)
                    dve.tensor_tensor(wL[:, c, :], wb[:, c, :], wH[:, c, :].bitcast(F32), ALU.subtract).then_inc(w_low, 1)

            link = Links(dve, steps)
            low(0)
            for j in range(2 * NT):
                n = n_of(j % NT)
                if j % NT == NT - 1:
                    low(j // NT + 1)
                weight = k.qw if j < NT else k.kw
                dve.wait_ge(squared, j + 1)
                dve.tensor_reduce(ss[0:n, :], sq[0:n, :].rearrange("p (g n) -> p g n", g=G), AX.X, ALU.add).then_inc(passed, 1)
                dve.wait_ge(passed, j + 1)
                link(dve.tensor_scalar(ss[0:n, :], ss[0:n, :], 1.0 / 64, EPS, ALU.mult, ALU.add))
                rsqrt(dve, link, r[0:n, :], ss[0:n, :], work[0:n, :])
                if j >= 2:
                    dve.wait_ge(turned, j - 1)
                if j >= NT + 2:
                    dve.wait_ge(k_out[j % 2], 16 * ((j - NT) // 2))
                out = nrm[0:n, j % 2, :].rearrange("p (g n) -> p g n", g=G)
                link(dve.tensor_tensor(out, raw[0:n, j % 2, :].rearrange("p (g n) -> p g n", g=G), over(r[0:n, :], 64), ALU.mult))
                dve.tensor_tensor(out, out, repeat(weight[0:n, :], G), ALU.mult).then_inc(normed, 1)
                if j >= 1:
                    store(j - 1)
            store(2 * NT - 1)


def attention_steps():
    steps = [("idle",)]
    for i in range(PT):
        steps.append(("scores", i, 0))
        if i:
            steps.append(("turn", i - 1, 0))
        steps.append(("scores", i, 1))
        if i > 4:
            steps.append(("turn", i - 1, 1))
        if i:
            steps.append(("values", i - 1))
    steps += [("turn", PT - 1, 0), ("turn", PT - 1, 1), ("values", PT - 1), ("idle",), ("norm",), ("out", 0), ("out", 1), ("store",)]
    return steps


def mixers_stage(k):
    nc, d = k.nc, k.d
    HN = H * P
    SHARE = (1,1,1,1, 1,1,1,1,1,1,1,1,1,1,1,1,1, 1,1,1,1)
    STEPS = sum(SHARE)
    TPH = PT // H
    attn = attention_steps()
    assert len(attn) <= TPH * STEPS
    GROUPS = [(i, g) for i in range(PT) for g in range(0, i + 1, 4)]
    NG = len(GROUPS)
    first_group = [GROUPS.index((i, 0)) for i in range(PT)]
    ngroups = [(i + 4) // 4 for i in range(PT)]
    with ExitStack() as ctx:
        sem = lambda s: k.sem(f"dp_{s}")
        (staged, stage_in, gb_staged, identity_set, raw_turned, sums_done, gp_ready, gc_done, gc_read, row_done, negd_ready, exps_done,
         masks_done, qk_scaled, kv_scaled, qk_turned, qkT_ready, qg_ready, kk_done, m_ready, a_ready, x_done,
         xs_ready, zu_done, zl_done, level_done, w_done, w_ready, v_done, v_ready, o_done, su_done, s_ready,
         osum_done, o_scaled, o_turned, out_ready, chain, pchain, achain, state_out, held, pool_held) = (sem(s) for s in (
             "staged", "stage_in", "gb_staged", "identity_set", "raw_turned", "sums", "gp", "gc", "gc_read", "row", "negd", "exps",
             "masks", "qk_scaled", "kv_scaled", "qk_turned", "qkT", "qg", "kk", "m", "a", "x", "xs", "zu", "zl", "level",
             "w", "w_ready", "v", "v_ready", "o", "su", "s", "osum", "o_scaled", "o_turned", "out", "chain",
             "pchain", "achain", "state_out", "held", "pool_held"))
        atsem = lambda s: k.sem(f"at_{s}")
        (at_staged, scored, maxed, exped, weighed, turned, moved, summed, o_saved, squared, o_normed, ob_turned,
         ob_ready, ob_out, at_chain, at_held) = (atsem(s) for s in (
             "staged", "scored", "maxed", "exped", "weighed", "turned", "moved", "summed", "o_saved", "squared",
             "o_normed", "ob_turned", "ob_ready", "ob_out", "chain", "held"))
        sb = k.area("dp", M_H, M_QKV)
        stage = sb("stage", [P, CA, P])
        gb = sb("gb", [P, 2 * H])
        gp = sb("gp", [P, HN])
        gcs = sb("gcs", [P, 2 * H])
        kdx, eg, ekd, nbe, egl = (sb(s, [P, H]) for s in ("kdx", "eg", "ekd", "nbe", "egl"))
        negd, es, esl, esu, er = (sb(s, [P, HN]) for s in ("negd", "es", "esl", "esu", "er"))
        ss, r, work = (sb(s, [P, 2 * H]) for s in ("ss", "r", "work"))
        junk = sb("junk", [P, 2, P])
        qn, kn, vb, kbg, kd = (sb(s, [P, W]) for s in ("qn", "kn", "vb", "kbg", "kd"))
        qT, kT, qgT, wT = (sb(s, [P, HN]) for s in ("qT", "kT", "qgT", "wT"))
        m, aT, U, L, xs = (sb(s, [P, HN]) for s in ("m", "aT", "U", "L", "xs"))
        vn, on = (sb(s, [P, W]) for s in ("vn", "on"))
        so, ro, worko = (sb(s, [P, H]) for s in ("so", "ro", "worko"))
        S = sb("S", [P, H, DH])
        B = [k.ps(ctx, f"dp_b{i}") for i in range(4)]
        qh, kh = (sb(s, [P, SEQ]) for s in ("qh", "kh"))
        prT = sb("prT", [P, 2, 512])
        o = sb("o", [P, PT, DH])
        mx, nmx, sums, rs = (sb(s, [P, 2]) for s in ("mx", "nmx", "sums", "rs"))
        sob, rob, workb = (sb(s, [P, PT]) for s in ("sob", "rob", "workb"))
        sb = k.area("at", M_OB, M_BIAS)
        E = [sb(f"e{n}", [P, SEQ]) for n in range(2)]
        pr = sb("pr", [P, 2, SEQ])
        obn = pr[:, 0, :].rearrange("p (i n) -> p i n", n=DH)
        ps = k.ps(ctx, "at_ps", 2)[:, :, :].rearrange("p a n -> p (a n)")
        pt, po = (k.ps(ctx, s) for s in ("at_pt", "at_po"))
        ident = k.c("ident")
        block = ctx.enter_context(nc.Block())

        def srow(i, n):
            nk = (i + 1) * P
            return ps[:, n * 512:n * 512 + nk] if nk <= 512 else ps[:, 0:nk]

        def halves(eng, tile, beside, begin=None):
            def body(h, first):
                if begin:
                    begin(h, first)
                for n in range(TPH):
                    def side(s):
                        for q in range(n * STEPS + sum(SHARE[:s]), n * STEPS + sum(SHARE[:s + 1])):
                            if q < len(attn):
                                beside(h, first, q)
                    tile(h * TPH + n, first and n == 0, side)

            loop(eng, H, body)

        def cols(t):
            return at(t * P, P)

        @block.sync
        def _(sp):
            rows = k.qkvT_dram.rearrange("c p n -> p c n")

            def stage_load(t, first, side):
                if not first:
                    hold(sp, raw_turned, t, staged)
                sp.dma_start(stage[:, :, :], rows[:, :, cols(t)]).then_inc(stage_in, 16)

            halves(sp, stage_load, None)
            sp.wait_ge(s_ready, PT)
            sp.dma_start(d["delta_prompt"].rearrange("a b h p n -> p (a b h) n"), S[:, :, :]).then_inc(state_out, 16)
            sp.wait_ge(state_out, 16)

        @block.gpsimd
        def _(pool):
            def tile(t, first, side):
                if not first:
                    pool.wait_ge(kv_scaled, t)
                    hold(pool, gc_done, t, pool_held)
                pool.tensor_copy(gb[:, 0:H], flat(k.g[:, at(t), :])).then_inc(gb_staged, 1)
                pool.tensor_copy(gb[:, H:2 * H], flat(k.beta[:, at(t), :])).then_inc(gb_staged, 1)
                if not first:
                    hold(pool, v_done, t, pool_held)
                for buf in (U, L):
                    pool.tensor_copy(hd(buf[:, :]), repeat(ident, H)).then_inc(identity_set, 1)
                pool.wait_ge(exps_done, t + 1)
                link = Links(pool, pchain, 3 * t)
                if not first:
                    pool.wait_ge(m_ready, t)
                link(pool.tensor_tensor(hd(esl[:, :]), hd(es[:, :]), repeat(k.c("neglow"), H), ALU.mult))
                link(pool.tensor_tensor(hd(esl[:, :]), hd(esl[:, :]), over(gb[:, H:2 * H], P), ALU.mult))
                if not first:
                    pool.wait_ge(a_ready, t)
                link(pool.tensor_tensor(hd(esu[:, :]), hd(es[:, :]), repeat(k.c("triu"), H), ALU.mult))
                pool.sem_inc(masks_done, 1)
                pool.wait_ge(qkT_ready, t + 1)
                if not first:
                    pool.wait_ge(o_done, t)
                pool.tensor_tensor(qgT[:, :], qT[:, :], er[:, :], ALU.mult).then_inc(qg_ready, 1)

            def stage_head(h, first):
                if not first:
                    hold(pool, scored, 2 * PT * h, at_held)
                pool.tensor_copy(qh[:, :], flat(k.qT[:, at(h), 0:SEQ])).then_inc(at_staged, 1)
                pool.tensor_copy(kh[:, :], flat(k.kT[:, at(h), 0:SEQ])).then_inc(at_staged, 1)

            halves(pool, tile, None, stage_head)

        @block.tensor
        def _(pe):
            def beside(h, first, q):
                kind, *w = attn[q]
                if kind == "scores":
                    i, n = w
                    if i == 0 and n == 0:
                        pe.wait_ge(at_staged, 2 * h + 2)
                    if i:
                        pe.wait_ge(exped, 2 * PT * h + 2 * i + (n if i >= 4 else n - 1))
                    elif not first:
                        pe.wait_ge(exped, 2 * PT * h)
                    rows = slice(64 * n, 64 * n + 64)
                    nk, out = (i + 1) * P, srow(i, n)
                    for b in range(0, nk, 512):
                        e = min(nk, b + 512)
                        near = [c for c in (i - 1, i) if c >= 0 and b <= c * P < e]
                        ins = pe.matmul(out[:, b:e], qh[rows, i * P:i * P + P], kh[rows, b:e], start=True, stop=not near)
                        for c in near:
                            ins = pe.matmul(out[:, c * P:c * P + P], ident, flat(k.bias[:, at(h), (c - i + 1) * P:(c - i + 2) * P]),
                                            start=False, stop=(c == near[-1]))
                    ins.then_inc(scored, 1)
                elif kind == "turn":
                    i, n = w
                    G = first_group[i] + n
                    pe.wait_ge(weighed, PT * h + i + 1)
                    if not first or G:
                        pe.wait_ge(moved, NG * h + G)
                    if not first and not G:
                        pe.wait_ge(ob_ready, 2 * h)
                    for c in range(4 * n, min(4 * n + 4, i + 1)):
                        ins = pe.transpose(pt[:, (c - 4 * n) * P:(c - 4 * n + 1) * P], pr[:, i % 2, c * P:c * P + P], ident)
                    ins.then_inc(turned, 1)
                elif kind == "values":
                    i = w[0]
                    if not first or i:
                        pe.wait_ge(o_saved, PT * h + i)
                    for n in range(ngroups[i]):
                        G = first_group[i] + n
                        pe.wait_ge(moved, NG * h + G + 1)
                        for c in range(4 * n, min(4 * n + 4, i + 1)):
                            ins = pe.matmul(po[:, 0:DH], prT[:, G % 2, (c - 4 * n) * P:(c - 4 * n + 1) * P],
                                            k.v[:, c, at(h * P, P)], start=(c == 0), stop=(c == i))
                    ins.then_inc(summed, 1)
                elif kind == "out":
                    g = w[0]
                    if g == 0:
                        pe.wait_ge(o_normed, h + 1)
                        pe.wait_ge(moved, NG * (h + 1))
                    else:
                        pe.wait_ge(ob_ready, 2 * h + 1)
                    for i in range(4):
                        ins = pe.transpose(pt[:, i * P:i * P + P], obn[:, 4 * g + i, :], ident)
                    ins.then_inc(ob_turned, 1)

            def tile(t, first, side):
                LV = LEVELS
                pe.wait_ge(gb_staged, 2 * t + 2)
                if not first:
                    pe.wait_ge(out_ready, t)
                    pe.wait_ge(s_ready, t)
                    pe.wait_ge(v_ready, t)
                pe.matmul(B[3][:, 0:H], k.c("triu"), gb[:, 0:H], start=True, stop=True)
                pe.matmul(B[3][:, H:2 * H], k.c("ones"), gb[:, 0:H], start=True, stop=True).then_inc(gc_done, 1)
                pe.wait_ge(stage_in, 16 * t + 16)
                for c in range(CA):
                    ins = pe.transpose(B[c // H][:, c % H * P:c % H * P + P], stage[:, c, :], ident)
                ins.then_inc(raw_turned, 1)
                side(0)
                pe.wait_ge(gc_read, t + 1)
                pe.wait_ge(gp_ready, t + 1)
                pe.matmul(B[3][:, 0:HN], k.c("ones"), gp[:, :], start=True, stop=True).then_inc(row_done, 1)
                side(1)
                pe.wait_ge(qk_scaled, t + 1)
                for b, nat in enumerate((qn, kn)):
                    for h in range(H):
                        ins = pe.transpose(B[b][:, h * P:h * P + P], nat[:, h * P:h * P + P], ident)
                ins.then_inc(qk_turned, 1)
                side(2)
                pe.wait_ge(qkT_ready, t + 1)
                for b, right in enumerate((kT, qT)):
                    for h in range(H):
                        s = slice(h * P, h * P + P)
                        ins = pe.matmul(B[b][:, s], kT[:, s], right[:, s], start=True, stop=True)
                ins.then_inc(kk_done, 1)
                side(3)
                pe.wait_ge(m_ready, t + 1)
                pe.wait_ge(kv_scaled, t + 1)
                for l in range(LV):
                    if l:
                        pe.wait_ge(level_done, (2 * LV - 1) * t + 2 * l - 1)
                    if l == 1:
                        pe.wait_ge(a_ready, t + 1)
                    for h in range(H):
                        s = slice(h * P, h * P + P)
                        ins = pe.matmul(B[2][:, s], m[:, s], U[:, s] if l else ident, start=True, stop=True)
                    ins.then_inc(x_done, 1)
                    side(4 if l == 0 else 3 + 2 * l)
                    if l:
                        pe.wait_ge(level_done, (2 * LV - 1) * t + 2 * l)
                        pe.wait_ge(xs_ready, (LV - 1) * t + l)
                        for h in range(H):
                            s = slice(h * P, h * P + P)
                            ins = pe.matmul(B[0][:, s], L[:, s], xs[:, s], start=True, stop=True)
                        ins.then_inc(zu_done, 1)
                        if l < LV - 1:
                            for h in range(H):
                                s = slice(h * P, h * P + P)
                                ins = pe.matmul(B[1][:, s], xs[:, s], L[:, s], start=True, stop=True)
                            ins.then_inc(zl_done, 1)
                        side(4 + 2 * l)
                pe.wait_ge(level_done, (2 * LV - 1) * (t + 1))
                for h in range(H):
                    ins = pe.matmul(B[3][:, h * P:h * P + P], kbg[:, h * P:h * P + P], U[:, h * P:h * P + P], start=True, stop=True)
                ins.then_inc(w_done, 1)
                side(17)
                pe.wait_ge(w_ready, t + 1)
                if not first:
                    pe.wait_ge(s_ready, t)
                else:
                    pe.wait_ge(chain, 1)
                for h in range(H):
                    s = slice(h * P, h * P + P)
                    pe.matmul(B[0][:, s], U[:, s], vb[:, s], start=True, stop=False)
                    ins = pe.matmul(B[0][:, s], wT[:, s], S[:, h, :], start=False, stop=True)
                ins.then_inc(v_done, 1)
                side(18)
                pe.wait_ge(v_ready, t + 1)
                pe.wait_ge(qg_ready, t + 1)
                for h in range(H):
                    s = slice(h * P, h * P + P)
                    pe.matmul(B[1][:, s], qgT[:, s], S[:, h, :], start=True, stop=False)
                    ins = pe.matmul(B[1][:, s], aT[:, s], vn[:, s], start=False, stop=True)
                ins.then_inc(o_done, 1)
                for h in range(H):
                    s = slice(h * P, h * P + P)
                    ins = pe.matmul(B[2][:, s], kd[:, s], vn[:, s], start=True, stop=True)
                ins.then_inc(su_done, 1)
                side(19)
                pe.wait_ge(o_scaled, t + 1)
                for h in range(H):
                    s = slice(h * P, h * P + P)
                    ins = pe.transpose(B[3][:, s], on[:, s], ident)
                ins.then_inc(o_turned, 1)
                side(20)

            halves(pe, tile, beside)

        @block.scalar
        def _(act):
            def beside(h, first, q):
                kind, *w = attn[q]
                before, *wb = attn[q - 1] if q else ("idle",)
                before2, *wb2 = attn[q - 2] if q > 1 else ("idle",)
                if before == "scores":
                    i, n = wb
                    act.wait_ge(maxed, 2 * PT * h + 2 * i + n + 1)
                    if not first or i:
                        act.wait_ge(weighed, PT * h + i)
                    act.activation(E[n][:, 0:(i + 1) * P], srow(i, n), ACT.Exp, bias=nmx[:, n:n + 1],
                                   scale=0.125, accum_out=sums[:, n:n + 1]).then_inc(exped, 1)
                if kind == "turn":
                    i, n = w
                    G = first_group[i] + n
                    act.wait_ge(turned, NG * h + G + 1)
                    if not first or G >= 2:
                        act.wait_ge(summed, PT * h + (GROUPS[G - 2][0] + 1 if G >= 2 else 0))
                    wide = (min(4 * n + 4, i + 1) - 4 * n) * P
                    act.activation(prT[:, G % 2, 0:wide], pt[:, 0:wide], ACT.Copy).then_inc(moved, 1)
                if before2 == "values":
                    i = wb2[0]
                    act.wait_ge(o_saved, PT * h + i + 1)
                    if not first or i:
                        act.wait_ge(squared, PT * h + i)
                    act.activation(junk[:, 1, :], o[:, i, :], ACT.Square, accum_out=sob[:, i:i + 1]).then_inc(squared, 1)
                if kind == "store":
                    act.wait_ge(ob_ready, 2 * h + 2)
                    act.dma_start(flat(k.ob_dram[at(h), :, :].rearrange("h p n -> p h n")), flat(o[:, :, :])).then_inc(ob_out, 16)

            def tile(t, first, side):
                LV = LEVELS
                link = Links(act, achain, 3 * H * t)
                act.wait_ge(raw_turned, t + 1)
                if not first:
                    act.wait_ge(kv_scaled, t)
                for h in range(2 * H):
                    link(act.activation(junk[:, 0, :], B[h // H][:, h % H * P:h % H * P + P], ACT.Square, accum_out=ss[:, h:h + 1]))
                act.sem_inc(sums_done, 1)
                act.wait_ge(gc_read, t + 1)
                if not first:
                    act.wait_ge(s_ready, t)
                act.activation(eg[:, :], gcs[:, 0:H], ACT.Exp)
                act.activation(egl[:, :], gcs[:, H:2 * H], ACT.Exp)
                side(0)
                act.wait_ge(negd_ready, t + 1)
                if not first:
                    act.wait_ge(masks_done, t)
                    act.wait_ge(qg_ready, t)
                act.activation(es[:, :], negd[:, :], ACT.Exp)
                act.activation(ekd[:, :], kdx[:, :], ACT.Exp)
                act.activation(er[:, :], B[3][:, 0:HN], ACT.Exp).then_inc(exps_done, 1)
                side(1)
                act.wait_ge(qk_turned, t + 1)
                act.activation(qT[:, :], B[0][:, 0:HN], ACT.Copy)
                act.activation(kT[:, :], B[1][:, 0:HN], ACT.Copy).then_inc(qkT_ready, 1)
                side(2)
                side(3)
                side(4)
                for l in range(1, LV):
                    act.wait_ge(x_done, LV * t + l + 1)
                    if l >= 2:
                        act.wait_ge(zl_done, (LV - 2) * t + l - 1)
                    act.activation(xs[:, :], B[2][:, 0:HN], ACT.Copy).then_inc(xs_ready, 1)
                    side(3 + 2 * l)
                    side(4 + 2 * l)
                act.wait_ge(w_done, t + 1)
                act.activation(wT[:, :], B[3][:, 0:HN], ACT.Copy).then_inc(w_ready, 1)
                side(17)
                act.wait_ge(v_done, t + 1)
                act.activation(vn[:, :], B[0][:, :], ACT.Copy).then_inc(v_ready, 1)
                side(18)
                act.wait_ge(o_done, t + 1)
                for h in range(H):
                    link(act.activation(junk[:, 0, :], B[1][:, h * P:h * P + P], ACT.Square, accum_out=so[:, h:h + 1]))
                act.sem_inc(osum_done, 1)
                side(19)
                side(20)

            halves(act, tile, beside)
            act.wait_ge(ob_out, 16 * H)

        @block.vector
        def _(dve):
            dve.memset(S[:, :, :], 0.0).then_inc(chain, 1)
            per_tile, per_head = [0], [0]
            head_link = [None]

            def begin(h, first):
                head_link[0] = Links(dve, at_chain, per_head[0] * h)

            def beside(h, first, q):
                link = head_link[0]
                kind, *w = attn[q]
                before, *wb = attn[q - 1] if q else ("idle",)
                before2, *wb2 = attn[q - 2] if q > 1 else ("idle",)
                if kind == "scores":
                    i, n = w
                    dve.wait_ge(scored, 2 * PT * h + 2 * i + n + 1)
                    if n == 0 and (i or not first):
                        dve.wait_ge(exped, 2 * PT * h + 2 * i)
                    link(dve.tensor_reduce(mx[:, n:n + 1], srow(i, n), AX.X, ALU.max))
                    link(dve.tensor_scalar(nmx[:, n:n + 1], mx[:, n:n + 1], -0.125, None, ALU.mult))
                    dve.sem_inc(maxed, 1)
                if before2 == "scores" and wb2[1] == 1:
                    i = wb2[0]
                    nk = (i + 1) * P
                    dve.wait_ge(exped, 2 * PT * h + 2 * i + 2)
                    link(dve.reciprocal(rs[:, :], sums[:, :]))
                    link(dve.scalar_tensor_tensor(rs[:, 1:2], rs[:, 1:2], -1.0, k.lam[:, :], ALU.mult, ALU.mult))
                    if not first or i >= 2:
                        dve.wait_ge(turned, NG * h + (first_group[i - 2] + ngroups[i - 2] if i >= 2 else 0))
                    if not first and i == 0:
                        dve.wait_ge(ob_turned, 2 * h)
                    link(dve.tensor_scalar(pr[:, i % 2, 0:nk], E[0][:, 0:nk], rs[:, 0:1], None, ALU.mult))
                    link(dve.scalar_tensor_tensor(pr[:, i % 2, 0:nk], E[1][:, 0:nk], rs[:, 1:2], pr[:, i % 2, 0:nk], ALU.mult, ALU.add))
                    dve.sem_inc(weighed, 1)
                if before == "values":
                    i = wb[0]
                    dve.wait_ge(summed, PT * h + i + 1)
                    if not first and i == 0:
                        dve.wait_ge(ob_out, 16 * h)
                    dve.tensor_copy(o[:, i, :], po[:, 0:DH]).then_inc(o_saved, 1)
                if kind == "norm":
                    dve.wait_ge(squared, PT * (h + 1))
                    link(dve.tensor_scalar(sob[:, :], sob[:, :], 1.0 / DH, EPS, ALU.mult, ALU.add))
                    rsqrt(dve, link, rob[:, :], sob[:, :], workb[:, :])
                    dve.wait_ge(turned, NG * (h + 1))
                    link(dve.tensor_tensor(obn[:, :, :], o[:, :, :], over(rob[:, :], DH), ALU.mult))
                    dve.sem_inc(o_normed, 1)
                if kind == "out":
                    g = w[0]
                    dve.wait_ge(ob_turned, 2 * h + g + 1)
                    link(dve.tensor_scalar(flat(o[:, 4 * g:4 * g + 4, :]), pt[:, :], k.subln[:, 0:1], None, ALU.mult))
                    dve.sem_inc(ob_ready, 1)
                per_head[0] = link.n

            def tile(t, first, side):
                LV = LEVELS
                link = Links(dve, chain, 1 + per_tile[0] * t)
                dve.wait_ge(gb_staged, 2 * t + 2)
                dve.tensor_tensor(hd(gp[:, :]), repeat(k.c("triu"), H), over(gb[:, 0:H], P), ALU.mult).then_inc(gp_ready, 1)
                dve.wait_ge(gc_done, t + 1)
                link(dve.tensor_copy(gcs[:, :], B[3][:, 0:2 * H]))
                dve.sem_inc(gc_read, 1)
                link(dve.tensor_tensor(kdx[:, :], gcs[:, H:2 * H], gcs[:, 0:H], ALU.subtract))
                side(0)
                dve.wait_ge(row_done, t + 1)
                link(dve.tensor_tensor(hd(negd[:, :]), hd(B[3][:, 0:HN]), over(gcs[:, 0:H], P), ALU.subtract))
                link(dve.scalar_tensor_tensor(negd[:, :], negd[:, :], -1.0, negd[:, :], ALU.mult, ALU.min))
                dve.sem_inc(negd_ready, 1)
                dve.wait_ge(sums_done, t + 1)
                link(dve.tensor_scalar(ss[:, :], ss[:, :], EPS, None, ALU.add))
                rsqrt(dve, link, r[:, :], ss[:, :], work[:, :])
                link(dve.tensor_scalar(r[:, 0:H], r[:, 0:H], DH ** -0.5, None, ALU.mult))
                link(dve.tensor_tensor(hd(qn[:, :]), hd(B[0][:, :]), over(r[:, 0:H], P), ALU.mult))
                link(dve.tensor_tensor(hd(kn[:, :]), hd(B[1][:, :]), over(r[:, H:2 * H], P), ALU.mult))
                dve.sem_inc(qk_scaled, 1)
                link(dve.tensor_tensor(hd(vb[:, :]), hd(B[2][:, :]), over(gb[:, H:2 * H], P), ALU.mult))
                side(1)
                dve.wait_ge(exps_done, t + 1)
                link(dve.scalar_tensor_tensor(nbe[:, :], gb[:, H:2 * H], -1.0, eg[:, :], ALU.mult, ALU.mult))
                link(dve.tensor_tensor(hd(kbg[:, :]), hd(kn[:, :]), over(nbe[:, :], P), ALU.mult))
                link(dve.tensor_tensor(hd(kd[:, :]), hd(kn[:, :]), over(ekd[:, :], P), ALU.mult))
                dve.sem_inc(kv_scaled, 1)
                side(2)
                dve.wait_ge(kk_done, t + 1)
                dve.wait_ge(masks_done, t + 1)
                dve.tensor_tensor(m[:, :], B[0][:, 0:HN], esl[:, :], ALU.mult).then_inc(m_ready, 1)
                dve.tensor_tensor(aT[:, :], B[1][:, 0:HN], esu[:, :], ALU.mult).then_inc(a_ready, 1)
                side(3)
                dve.wait_ge(m_ready, t + 1)
                dve.wait_ge(identity_set, 2 * t + 2)
                for l in range(LV):
                    up = repeat(k.c(f"up{l}").bitcast(I32), H)
                    low = repeat(k.c(f"low{l}").bitcast(I32), H)
                    if l == 0:
                        hold(dve, x_done, LV * t + 1, held)
                        dve.copy_predicated(hd(U[:, :]), up, hd(B[2][:, 0:HN])).then_inc(level_done, 1)
                        dve.copy_predicated(hd(L[:, :]), low, hd(m[:, :])).then_inc(level_done, 1)
                        side(4)
                    else:
                        side(3 + 2 * l)
                        dve.wait_ge(level_done, (2 * LV - 1) * t + 2 * l)
                        hold(dve, zu_done, (LV - 1) * t + l, held)
                        dve.copy_predicated(hd(U[:, :]), up, hd(B[0][:, 0:HN])).then_inc(level_done, 1)
                        if l < LV - 1:
                            hold(dve, zl_done, (LV - 2) * t + l, held)
                            dve.copy_predicated(hd(L[:, :]), low, hd(B[1][:, 0:HN])).then_inc(level_done, 1)
                        side(4 + 2 * l)
                side(17)
                side(18)
                dve.wait_ge(o_done, t + 1)
                link(dve.tensor_tensor(S[:, :, :], S[:, :, :], over(egl[:, :], DH), ALU.mult))
                dve.wait_ge(su_done, t + 1)
                link(dve.tensor_tensor(S[:, :, :], S[:, :, :], hd(B[2][:, :]), ALU.add))
                dve.sem_inc(s_ready, 1)
                dve.wait_ge(osum_done, t + 1)
                link(dve.tensor_scalar(so[:, :], so[:, :], 1.0 / DH, EPS, ALU.mult, ALU.add))
                rsqrt(dve, link, ro[:, :], so[:, :], worko[:, :])
                link(dve.tensor_tensor(hd(on[:, :]), hd(B[1][:, :]), over(ro[:, :], P), ALU.mult))
                dve.sem_inc(o_scaled, 1)
                side(19)
                dve.wait_ge(o_turned, t + 1)
                link(dve.tensor_scalar(on[:, :], B[3][:, :], k.onorm[:, 0:1], None, ALU.mult))
                link(dve.tensor_tensor(hd(on[:, :]), hd(on[:, :]), k.zT[:, :, cols(t)], ALU.mult))
                link(dve.tensor_copy(k.oaH[:, :, cols(t)], hd(on[:, :])))
                link(dve.tensor_tensor(k.oaL[:, :, cols(t)], hd(on[:, :]), k.oaH[:, :, cols(t)].bitcast(F32), ALU.subtract))
                dve.sem_inc(out_ready, 1)
                side(20)
                per_tile[0] = link.n

            halves(dve, tile, beside, begin)


def decode_stage(k):
    nc, d = k.nc, k.d
    NK = PAST + NS
    RG = 2
    with ExitStack() as ctx:
        sem = lambda s: k.sem(f"de_{s}")
        (table_in, v_in, q_set, k_turned, k_moved, scored, new_scored, sc_moved, row_turned, biased, exped, weighed, steps,
         back, back_moved, pt_ready, summed, sq_ready, norm_done, bias_set) = (sem(s) for s in (
             "table_in", "v_in", "q_set", "k_turned", "k_moved", "scored", "new_scored", "sc_moved", "row_turned", "biased", "exped",
             "weighed", "steps", "back", "back_moved", "pt_ready", "summed", "sq_ready", "norm_done", "bias_set"))
        k_in = [sem(f"k_in{u}") for u in range(4)]
        ob_in = sem("ob_in")
        sb = k.area("de", M_H, M_QKV)
        table = sb("table", [1, NSEQ * PAGES], I32)
        kpg = sb("kpg", [P, 4, W])
        vpg = sb("vpg", [P, NSEQ * PAGES, W])
        kpT = sb("kpT", [P, 2, W])
        Q = sb("q", [P, NSEQ, H, 2, QN])
        sc = sb("sc", [P, PAGES, 256])
        scn = sb("scn", [NS, 256])
        bnew = sb("bnew", [P, RG, NSEQ, QN])
        X = sb("x", [P, RG, NK])
        mx, nmx, sums, rs = (sb(s, [P, RG]) for s in ("mx", "nmx", "sums", "rs"))
        sgn = sb("sgn", [P, 1])
        pb = sc
        pbn = sb("pbn", [NS, 256])
        prT = sb("prT", [P, PAGES, NSEQ * H, QN])
        prTn = sb("prTn", [NS, NSEQ * H, QN])
        oT, sq, ro, work = (sb(s, [P, P]) for s in ("oT", "sq", "ro", "work"))
        ob = sb("ob", [P, H, SEQ])
        pk = [k.ps(ctx, f"de_pk{u}") for u in range(2)]
        psc, psn, po, pss = (k.ps(ctx, f"de_{s}") for s in ("psc", "psn", "po", "pss"))
        prow = [k.ps(ctx, f"de_prow{u}") for u in range(RG)]
        block = ctx.enter_context(nc.Block())
        ck = d["cache_k"].rearrange("a g p h n -> p (a g) (h n)")
        cv = d["cache_v"].rearrange("a g p h n -> p (a g) (h n)")
        pool_pages = ck.shape[1]
        NPG = NSEQ * PAGES

        @block.sync
        def _(sp):
            sp.dma_start(table[:, :], d["page_table"].rearrange("(a s) g -> a (s g)", a=1)).then_inc(table_in, 16)
            sp.dma_start(ob[:, :, :], k.ob_dram.rearrange("h p n -> p h n")).then_inc(ob_in, 16)
            sp.wait_ge(table_in, 16)
            for j in range(NPG):
                page = sp.value_load(table[0:1, j:j + 1], min_val=0, max_val=pool_pages - 1)
                if j >= 4:
                    sp.wait_ge(k_turned, j - 3)
                sp.dma_start(kpg[:, j % 4, :], ck[:, at(page), :].rearrange("p a n -> p (a n)")).then_inc(k_in[j % 4], 16)
                sp.dma_start(vpg[:, j, :], cv[:, at(page), :].rearrange("p a n -> p (a n)")).then_inc(v_in, 16)

        @block.tensor
        def _(pe):
            ident = k.c("ident")

            def turn(j):
                pe.wait_ge(k_in[j % 4], 16 * (j // 4 + 1))
                if j >= 2:
                    pe.wait_ge(k_moved, j - 1)
                for h in range(H):
                    ins = pe.transpose(pk[j % 2][:, h * P:h * P + P], kpg[:, j % 4, h * P:h * P + P], ident)
                ins.then_inc(k_turned, 1)

            def score(j):
                s, g = j // PAGES, j % PAGES
                pe.wait_ge(k_moved, j + 1)
                for h in range(H):
                    c = g * 256 + (s * H + h) * 8
                    ins = pe.matmul(psc[:, c:c + 8], kpT[:, j % 2, h * P:h * P + P], Q[:, s, h, :, :].rearrange("p m q -> p (m q)"),
                                    start=True, stop=True)
                ins.then_inc(scored, 1)

            turn(0)
            pe.wait_ge(q_set, 9)
            for h in range(H):
                ins = pe.matmul(psn[0:NS, 0:256].rearrange("p (s h n) -> p s h n", s=NSEQ, h=H)[:, :, h, :],
                                k.kT[:, h, SEQ:T], Q[:, :, h, :, :].rearrange("p s m q -> p s (m q)"), start=True, stop=True)
            ins.then_inc(new_scored, 1)
            for j in range(NPG):
                if j + 1 < NPG:
                    turn(j + 1)
                score(j)
            pe.wait_ge(sc_moved, 2)
            for r in range(RG):
                for g in range(PAGES):
                    pe.transpose(prow[r][:, g * P:g * P + P], sc[:, g, r * P:r * P + P], ident)
                pe.transpose(prow[r][:, PAST:NK], scn[:, r * P:r * P + P], ident[0:NS, 0:NS]).then_inc(row_turned, 1)
            pe.wait_ge(weighed, 1)
            for r in range(RG):
                for g in range(PAGES):
                    pe.transpose(psc[:, g * 256 + r * P:g * 256 + r * P + P], X[:, r, g * P:g * P + P], ident)
                ins = pe.transpose(psn[0:NS, r * P:r * P + P], X[:, r, PAST:NK], ident)
            ins.then_inc(back, 1)
            pe.wait_ge(pt_ready, 2)
            pe.wait_ge(v_in, 16 * NPG)
            for h in range(H):
                for s in range(NSEQ):
                    out = po[:, (h * NSEQ + s) * QN:(h * NSEQ + s + 1) * QN]
                    for g in range(PAGES):
                        pe.matmul(out, vpg[:, s * PAGES + g, h * P:h * P + P], prT[:, g, s * H + h, :], start=(g == 0), stop=False)
                    ins = pe.matmul(out, k.v[0:NS, PT, h * P:h * P + P], prTn[:, s * H + h, :], start=False, stop=True)
            ins.then_inc(summed, 1)
            pe.wait_ge(sq_ready, 1)
            pe.matmul(pss[:, 0:P], k.c("ones"), sq[:, :], start=True, stop=True).then_inc(norm_done, 1)

        @block.scalar
        def _(act):
            for j in range(NPG):
                act.wait_ge(k_turned, j + 1)
                if j >= 2:
                    act.wait_ge(scored, j - 1)
                act.activation(kpT[:, j % 2, :], pk[j % 2][:, :], ACT.Copy).then_inc(k_moved, 1)
            act.wait_ge(biased, 1)
            for r in range(RG):
                act.activation(X[:, r, :], X[:, r, :], ACT.Exp, bias=nmx[:, r:r + 1], scale=0.125,
                               accum_out=sums[:, r:r + 1]).then_inc(exped, 1)

        @block.vector
        def _(dve):
            link = Links(dve, steps)
            dve.memset(Q[:, :, :, :, :], 0.0).then_inc(q_set, 1)
            dve.wait_ge(q_set, 1)
            for m in range(2):
                rows = slice(64 * m, 64 * m + 64)
                for h in range(H):
                    dve.tensor_copy(Q[rows, :, h, m, :], k.qT[rows, h, SEQ:T].rearrange("p (s q) -> p s q", s=NSEQ)).then_inc(q_set, 1)
            link(dve.scalar_tensor_tensor(sgn[:, :], k.c("m1"), -1.0, k.lam[:, :], ALU.mult, ALU.mult))
            link(dve.tensor_tensor(sgn[:, :], sgn[:, :], k.c("m0"), ALU.add))
            for r in range(RG):
                cross = k.c("s_cross")[:, r * NSEQ:(r + 1) * NSEQ]
                link(dve.tensor_tensor(bnew[:, r, :, :], repeat(k.sbias[:, PAST:PAST + QN], NSEQ), over(cross, QN), ALU.add))
            dve.wait_ge(ob_in, 16)
            link(dve.tensor_copy(k.obH[:, :, 0:SEQ], ob[:, :, :]))
            link(dve.tensor_tensor(k.obL[:, :, 0:SEQ], ob[:, :, :], k.obH[:, :, 0:SEQ].bitcast(F32), ALU.subtract))
            dve.wait_ge(new_scored, 1)
            dve.tensor_copy(scn[:, :], psn[0:NS, 0:256]).then_inc(sc_moved, 1)
            dve.wait_ge(scored, NPG)
            dve.tensor_copy(sc[:, :, :], psc[:, :].rearrange("p (g n) -> p g n", g=PAGES)).then_inc(sc_moved, 1)
            for r in range(RG):
                dve.wait_ge(row_turned, r + 1)
                link(dve.tensor_tensor(X[:, r, 0:PAST], prow[r][:, 0:PAST], k.sbias[:, 0:PAST], ALU.add))
                link(dve.tensor_tensor(X[:, r, PAST:NK], prow[r][:, PAST:NK], bnew[:, r, :, :].rearrange("p s q -> p (s q)"), ALU.add))
            link(dve.tensor_reduce(mx[:, :], X[:, :, :], AX.X, ALU.max))
            dve.tensor_scalar(nmx[:, :], mx[:, :], -0.125, None, ALU.mult).then_inc(biased, 1)
            dve.wait_ge(exped, RG)
            link(dve.reciprocal(rs[:, :], sums[:, :]))
            link(dve.tensor_scalar(rs[:, :], rs[:, :], sgn[:, 0:1], None, ALU.mult))
            dve.tensor_tensor(X[:, :, :], X[:, :, :], over(rs[:, :], NK), ALU.mult).then_inc(weighed, 1)
            dve.wait_ge(back, 1)
            link(dve.tensor_copy(pb[:, :, :], psc[:, :].rearrange("p (g n) -> p g n", g=PAGES)))
            link(dve.tensor_copy(pbn[:, :], psn[0:NS, 0:256]))
            pv = pb[:, :, :].rearrange("p g (s m q) -> p (g s) m q", m=2, q=QN)
            dve.tensor_tensor(prT[:, :, :, :].rearrange("p g s q -> p (g s) q"), pv[:, :, 0, :], pv[:, :, 1, :], ALU.add).then_inc(pt_ready, 1)
            pn = pbn[:, :].rearrange("p (s m q) -> p s m q", m=2, q=QN)
            dve.tensor_tensor(prTn[:, :, :], pn[:, :, 0, :], pn[:, :, 1, :], ALU.add).then_inc(pt_ready, 1)
            dve.wait_ge(summed, 1)
            link(dve.tensor_copy(oT[:, :], po[:, 0:P]))
            dve.tensor_tensor(sq[:, :], oT[:, :], oT[:, :], ALU.mult).then_inc(sq_ready, 1)
            dve.wait_ge(norm_done, 1)
            link(dve.tensor_scalar(sq[:, :], pss[:, 0:P], 1.0 / DH, EPS, ALU.mult, ALU.add))
            rsqrt(dve, link, ro[:, :], sq[:, :], work[:, :])
            link(dve.tensor_tensor(oT[:, :], oT[:, :], ro[:, :], ALU.mult))
            link(dve.tensor_scalar(oT[:, :], oT[:, :], k.subln[:, 0:1], None, ALU.mult))
            link(dve.tensor_copy(k.obH[:, :, SEQ:T], hd(oT[:, :])))
            link(dve.tensor_tensor(k.obL[:, :, SEQ:T], hd(oT[:, :]), k.obH[:, :, SEQ:T].bitcast(F32), ALU.subtract))


def mix_stage(k):
    nc, d = k.nc, k.d
    with ExitStack() as ctx:
        sem = lambda s: k.sem(f"mx_{s}")
        proj_done = [sem(f"proj{u}") for u in range(2)]
        gate_in = [sem(f"gate_in{u}") for u in range(2)]
        gated = [sem(f"gated{u}") for u in range(2)]
        added, high, low = (sem(s) for s in ("added", "high", "low"))
        sb = k.area("mx", M_U, M_Z)
        w = Stream(k, "mx", sb, proj_done)
        sg = [sb(f"sg{u}", [P, T]) for u in range(2)]
        mixed = [sb(f"mixed{u}", [P, T]) for u in range(2)]
        ps = [k.ps(ctx, f"mx_ps{u}", 3) for u in range(2)]
        b_cols = d["w_branch"].rearrange("a b (c p) n -> p (a b) c n", p=P)
        gates = k.gate_dram.rearrange("c p n -> p c n")
        block = ctx.enter_context(nc.Block())
        act_in = ((k.oaH, k.oaL), (k.obH, k.obL))

        @block.sync
        def _(sp):
            for u in range(2):
                w.load(sp, u, 0, b_cols[:, u, :, 0:P], True)

            def step(i, first, final):
                for u in range(2):
                    if not first:
                        hold(sp, gated[u], i, w.sp_held)
                    sp.dma_start(sg[u][:, :], flat(gates[:, at(i + u * KC), :])).then_inc(gate_in[u], 16)
                if not final:
                    for u in range(2):
                        w.load(sp, u, i + 1, b_cols[:, u, :, at(i * P + P, P)], False)

            loop3(sp, KC, step)

        @block.tensor
        def _(pe):
            def step(i, first):
                for u in range(2):
                    if not first:
                        pe.wait_ge(gated[u], i)
                    w.multiply(pe, u, i, ps[u], *act_in[u], H)

            loop(pe, KC, step)

        @block.scalar
        def _(act):
            for u in range(2):
                w.high(act, u, 0, H, True)

            def step(i, first, final):
                if not final:
                    for u in range(2):
                        w.high(act, u, i + 1, H, False)
                act.wait_ge(added, i + 1)
                act.activation(flat(k.mH[:, at(i), :]), mixed[0][:, :], ACT.Copy).then_inc(high, 1)

            loop3(act, KC, step)

        @block.vector
        def _(dve):
            for u in range(2):
                w.low(dve, u, 0, H)
            banks = lambda ap: ap.rearrange("p (b n) -> p b n", b=NB)

            def step(i, first, final):
                for u in range(2):
                    dve.wait_ge(proj_done[u], i + 1)
                    dve.wait_ge(gate_in[u], 16 * i + 16)
                    if u == 0 and not first:
                        dve.wait_ge(low, i)
                    if u and not first:
                        dve.wait_ge(added, i)
                    dve.tensor_tensor(banks(mixed[u][:, :]), banks(sg[u][:, :]), ps[u][:, :, 0:BW], ALU.mult).then_inc(gated[u], 1)
                    if not final:
                        w.low(dve, u, i + 1, H)
                for u in range(2):
                    dve.wait_ge(gated[u], i + 1)
                dve.tensor_tensor(mixed[0][:, :], mixed[0][:, :], mixed[1][:, :], ALU.add).then_inc(added, 1)
                dve.wait_ge(high, i + 1)
                dve.tensor_tensor(flat(k.mL[:, at(i), :]), mixed[0][:, :], flat(k.mH[:, at(i), :]).bitcast(F32), ALU.subtract).then_inc(low, 1)

            loop3(dve, KC, step)


def out_proj_stage(k):
    nc, d = k.nc, k.d
    with ExitStack() as ctx:
        sem = lambda s: k.sem(f"wo_{s}")
        proj_done = [sem(f"proj{u}") for u in range(2)]
        added = [sem(f"added{u}") for u in range(2)]
        x_in = sem("x_in")
        w = Stream(k, "wo", k.area("wo", M_FFN, M_END), proj_done)
        ps = [k.ps(ctx, f"wo_ps{u}", 3) for u in range(2)]
        w_cols = d["w_o"].rearrange("a (c p) n -> p (a c) n", p=P)
        block = ctx.enter_context(nc.Block())
        NP = KC // 2

        @block.sync
        def _(sp):
            for u in range(2):
                w.load(sp, u, 0, w_cols[:, :, u * P:u * P + P], True)
            sp.dma_start(k.x1T[:, :, :], k.xT_dram.rearrange("c p n -> p c n")).then_inc(x_in, 16)
            with sp.Fori(1, NP) as i:
                for u in range(2):
                    w.load(sp, u, i, w_cols[:, :, at((2 * i + u) * P, P)], False)

        @block.tensor
        def _(pe):
            def step(i, first):
                for u in range(2):
                    if not first:
                        pe.wait_ge(added[u], i)
                    w.multiply(pe, u, i, ps[u], k.mH, k.mL, KC)

            loop(pe, NP, step)

        @block.scalar
        def _(act):
            def step(i, first):
                for u in range(2):
                    w.high(act, u, i, KC, first)

            loop(act, NP, step)

        @block.vector
        def _(dve):
            for u in range(2):
                w.low(dve, u, 0, KC)
            dve.wait_ge(x_in, 16)

            def step(i, first, final):
                for u in range(2):
                    dve.wait_ge(proj_done[u], i + 1)
                    if not final:
                        w.low(dve, u, i + 1, KC)
                    x = k.x1T[:, at(2 * i + u), :].rearrange("p a (b n) -> p (a b) n", b=NB)
                    dve.tensor_tensor(x, x, ps[u][:, :, 0:BW], ALU.add).then_inc(added[u], 1)

            loop3(dve, NP, step)


def ffn_stage(k):
    nc, d = k.nc, k.d
    R = TF - 1
    RAW = R + SEQ + NSEQ * (R + QN)
    OUT = RAW - R
    NH = NSEQ * R
    NR = NH + TF + 1
    LAST = R + NSEQ * R
    NC = 2 * CF
    ND = KC // 2
    with ExitStack() as ctx:
        sem = lambda n: k.sem(f"ff_{n}")
        proj_done = [sem(f"proj{u}") for u in range(2)]
        evac_done = [sem(f"evac{u}") for u in range(2)]
        conv_done = [sem(f"conv{u}") for u in range(2)]
        taps_in = [sem(f"taps_in{u}") for u in range(2)]
        last_out = [sem(f"last_out{u}") for u in range(2)]
        saved, taps_turned, taps_sb, last_turned, last_sb, zeroed, chain, silu_done, made, high, u_done, pool_held, dve_held = (
            sem(n) for n in ("saved", "taps_turned", "taps_sb", "last_turned", "last_sb", "zeroed", "chain", "silu", "made", "high",
                             "u", "pool_held", "dve_held"))
        UMAX = max(UPART)
        uH, uL = (k.put(f"ff_u{s}", [P, UMAX, T], M_U + i * UMAX * ROW, F32R) for i, s in enumerate("HL"))
        sb = k.area("ff", M_FFN, M_END)
        w = Stream(k, "ff", sb, proj_done)
        raw = [sb(f"conv_in{u}", [P, RAW]) for u in range(2)]
        acc = [sb(f"acc{u}", [P, RAW]) for u in range(2)]
        last = sb("last", [P, NC, LAST])
        sb = k.area("ff", M_CONST + 1024, M_SMALL)
        nat = sb("nat", [NR, 2, 4 * P])
        taps = sb("taps", [P, NC, NR])
        ps = [k.ps(ctx, f"ff_ps{u}", 3) for u in range(2)]
        pt = k.ps(ctx, "ff_pt", 2)
        samp = [raw[u][:, R + SEQ:RAW].rearrange("p (s c) -> p s c", s=NSEQ) for u in range(2)]
        samp_out = [acc[u][:, R + SEQ:RAW].rearrange("p (s c) -> p s c", s=NSEQ) for u in range(2)]
        w_up = d["w_up"].rearrange("a (c p) n -> p (a c) n", p=P)
        w_down = d["w_down"].rearrange("a (c p) n -> p (a c) n", p=P)
        NQ = NC // 4
        hist = d["state_conv_ffn"].rearrange("a s r n -> (a s r) n")
        cf = d["conv_f"].rearrange("a w n -> (a w) n")
        block = ctx.enter_context(nc.Block())
        parts, c0, i0 = [], 0, 0
        for n in UPART:
            parts.append((c0, n, i0))
            c0, i0 = c0 + n, i0 + n + ND
        pairs = i0

        def rest(eng, part, up, body):
            c, n, i = part
            steps, base = (n, i) if up else (ND, i + n)
            body(0, base, base == 0, steps == 1)
            if steps > 2:
                with eng.Fori(1, steps - 1) as j:
                    body(j, j + base, False, False)
            body(steps - 1, base + steps - 1, False, True)

        def kc_next(part, up, final):
            if not final:
                return KC if up else part[1]
            return part[1] if up else KC

        @block.sync
        def _(sp):
            for q in range(NQ):
                if q >= 2:
                    sp.wait_ge(taps_turned, q - 1)
                c = slice(q * 512, (q + 1) * 512)
                sp.dma_start(nat[0:NH, q % 2, :], hist[:, c]).then_inc(taps_in[q % 2], 16)
                sp.dma_start(nat[NH:NH + TF, q % 2, :], cf[:, c]).then_inc(taps_in[q % 2], 16)
                sp.dma_start(nat[NH + TF:NR, q % 2, :], d["conv_f_b"][:, c]).then_inc(taps_in[q % 2], 16)
                if q == 0:
                    for u in range(2):
                        w.load(sp, u, 0, w_up[:, :, u * DFF:u * DFF + P], True)
            for p, (c0, n, i0) in enumerate(parts):
                if p:
                    for u in range(2):
                        w.load(sp, u, i0, w_up[:, :, u * DFF + c0 * P:u * DFF + (c0 + 1) * P], False)
                with sp.Fori(1, n) as j:
                    for u in range(2):
                        w.load(sp, u, j + i0, w_up[:, :, at(j * P + (u * DFF + c0 * P), P)], False)
                for u in range(2):
                    w.load(sp, u, i0 + n, w_down[:, c0:c0 + n, u * P:u * P + P], False)
                with sp.Fori(1, ND) as j:
                    for u in range(2):
                        w.load(sp, u, j + (i0 + n), w_down[:, c0:c0 + n, at(j * 2 * P + u * P, P)], False)
            for q in range(NQ):
                sp.wait_ge(last_sb, q + 1)
                c = slice(q * 512, (q + 1) * 512)
                sp.dma_start(d["conv_ffn_prompt"].rearrange("a b r n -> (a b r) n")[:, c], nat[0:R, q % 2, :]).then_inc(last_out[q % 2], 16)
                sp.dma_start(d["conv_ffn_sample"].rearrange("a s r n -> (a s r) n")[:, c], nat[R:LAST, q % 2, :]).then_inc(last_out[q % 2], 16)
            for u in range(2):
                sp.wait_ge(last_out[u], 32 * ((NQ + 1 - u) // 2))

        @block.tensor
        def _(pe):
            for q in range(NQ):
                pe.wait_ge(taps_in[q % 2], 48 * (q // 2 + 1))
                if q >= 2:
                    pe.wait_ge(taps_sb, q - 1)
                for c in range(4):
                    ins = pe.transpose(pt[:, q % 2, c * P:c * P + NR], nat[:, q % 2, c * P:(c + 1) * P], k.c("ident", NR)[:, 0:NR])
                ins.then_inc(taps_turned, 1)

            for part in parts:
                c0, n, i0 = part

                def up(j, i, first, final):
                    for u in range(2):
                        if not first:
                            pe.wait_ge(evac_done[u], i)
                        w.multiply(pe, u, i, ps[u], k.fH, k.fL, KC)

                def down(j, i, first, final):
                    if type(j) is int and j == 0:
                        pe.wait_ge(u_done, 4 * (c0 + n - 1))
                        for u in range(2):
                            pe.wait_ge(evac_done[u], i)
                            w.multiply(pe, u, i, ps[u], uH, uL, n, range(n - 1))
                        pe.wait_ge(u_done, 4 * (c0 + n))
                        for u in range(2):
                            w.multiply(pe, u, i, ps[u], uH, uL, n, range(n - 1, n))
                        return
                    for u in range(2):
                        pe.wait_ge(evac_done[u], i)
                        w.multiply(pe, u, i, ps[u], uH, uL, n)

                rest(pe, part, True, up)
                rest(pe, part, False, down)
            for q in range(NQ):
                if q == 0:
                    pe.wait_ge(saved, 4 * CF)
                if q >= 2:
                    pe.wait_ge(last_sb, q - 1)
                for c in range(4):
                    ins = pe.transpose(pt[0:LAST, q % 2, c * P:c * P + P], last[:, 4 * q + c, :], k.c("ident"))
                ins.then_inc(last_turned, 1)

        @block.scalar
        def _(act):
            for u in range(2):
                w.high(act, u, 0, KC, True)
            for part in parts:
                c0, n, i0 = part

                def up(j, i, first, final):
                    for u in range(2):
                        act.wait_ge(proj_done[u], i + 1)
                        w.high(act, u, i + 1, kc_next(part, True, final), False)
                        if not first:
                            act.wait_ge(conv_done[u], j + c0)
                            act.wait_ge(saved, (j + c0) * 4 - 2 + 2 * u)
                        for b in range(NB):
                            lo, hi = b * BW, min(SEQ, (b + 1) * BW)
                            act.activation(raw[u][:, R + lo:R + hi], ps[u][:, b, 0:hi - lo], ACT.Copy)
                        act.activation(samp[u][:, :, R:R + QN], ps[u][:, NB - 1, BW - NS:BW].rearrange("p (s c) -> p s c", s=NSEQ),
                                       ACT.Copy).then_inc(evac_done[u], 1)
                    act.wait_ge(conv_done[0], j + (c0 + 1))
                    act.activation(acc[0][:, 0:OUT], acc[0][:, 0:OUT], ACT.Silu).then_inc(silu_done, 1)
                    act.wait_ge(made, j + (c0 + 1))
                    act.activation(flat(uH[:, at(j), 0:SEQ]), acc[0][:, 0:SEQ], ACT.Copy)
                    act.activation(uH[:, at(j), SEQ:T].rearrange("p a (s c) -> p (a s) c", s=NSEQ), samp_out[0][:, :, 0:QN],
                                   ACT.Copy).then_inc(high, 1)

                def down(j, i, first, final):
                    for u in range(2):
                        act.wait_ge(proj_done[u], i + 1)
                        if not final or part is not parts[-1]:
                            w.high(act, u, i + 1, kc_next(part, False, final), False)

                rest(act, part, True, up)
                rest(act, part, False, down)

        @block.gpsimd
        def _(pool):
            for part in parts:
                c0, n, i0 = part

                def save(j, i, first, final):
                    for u in range(2):
                        hold(pool, evac_done[u], i + 1, pool_held)
                        c = j + (c0 + u * CF)
                        pool.tensor_copy(flat(last[:, at(c), 0:R]), raw[u][:, SEQ:SEQ + R]).then_inc(saved, 1)
                        pool.tensor_copy(last[:, at(c), R:LAST].rearrange("p a (s c) -> p (a s) c", s=NSEQ),
                                         samp[u][:, :, QN:QN + R]).then_inc(saved, 1)

                rest(pool, part, True, save)

        @block.vector
        def _(dve):
            for u in range(2):
                dve.memset(raw[u][:, 0:R], 0.0).then_inc(zeroed, 1)
                w.low(dve, u, 0, KC)
            for q in range(NQ):
                dve.wait_ge(taps_turned, q + 1)
                dve.tensor_copy(taps[:, 4 * q:4 * q + 4, :], hd(pt[:, q % 2, :])[:, :, 0:NR]).then_inc(taps_sb, 1)
            dve.wait_ge(taps_sb, NQ)
            dve.wait_ge(zeroed, 2)
            per = [0]

            def tap(c, t):
                return flat(taps[:, at(c), NH + t:NH + t + 1])

            for part in parts:
                c0, n, i0 = part

                def up(j, i, first, final):
                    link = Links(dve, chain, (j + c0) * per[0])
                    for u in range(2):
                        c = j + (c0 + u * CF)
                        w.low(dve, u, i + 1, kc_next(part, True, final))
                        dve.wait_ge(evac_done[u], i + 1)
                        if not first:
                            dve.wait_ge(u_done, (j + c0) * 4)
                        link(dve.tensor_copy(samp[u][:, :, 0:R], taps[:, at(c), 0:NH].rearrange("p a (s r) -> p (a s) r", s=NSEQ)))
                        link(dve.tensor_scalar(acc[u][:, 0:OUT], raw[u][:, 0:OUT], tap(c, 0), tap(c, TF), ALU.mult, ALU.add))
                        for t in range(1, TF):
                            link(dve.scalar_tensor_tensor(acc[u][:, 0:OUT], raw[u][:, t:t + OUT], tap(c, t), acc[u][:, 0:OUT], ALU.mult, ALU.add))
                        dve.sem_inc(conv_done[u], 1)
                    dve.wait_ge(silu_done, j + (c0 + 1))
                    if type(j) is int and j == 0 and c0:
                        for u in range(2):
                            dve.wait_ge(proj_done[u], i)
                    link(dve.tensor_tensor(acc[0][:, 0:OUT], acc[0][:, 0:OUT], acc[1][:, 0:OUT], ALU.mult))
                    dve.sem_inc(made, 1)
                    dve.wait_ge(high, j + (c0 + 1))
                    low = lambda o, a, b: dve.tensor_tensor(o, a, b.bitcast(F32), ALU.subtract).then_inc(u_done, 2)
                    low(flat(uL[:, at(j), 0:SEQ]), acc[0][:, 0:SEQ], flat(uH[:, at(j), 0:SEQ]))
                    tail = lambda buf: buf[:, at(j), SEQ:T].rearrange("p a (s c) -> p (a s) c", s=NSEQ)
                    low(tail(uL), samp_out[0][:, :, 0:QN], tail(uH))
                    per[0] = link.n

                def down(j, i, first, final):
                    for u in range(2):
                        if not final or part is not parts[-1]:
                            w.low(dve, u, i + 1, kc_next(part, False, final))
                        dve.wait_ge(proj_done[u], i + 1)
                        x = k.x1T[:, at(j * 2 + u), :].rearrange("p a (b n) -> p (a b) n", b=NB)
                        dve.tensor_tensor(x, x, ps[u][:, :, 0:BW], ALU.add).then_inc(evac_done[u], 1)

                rest(dve, part, True, up)
                rest(dve, part, False, down)
            for q in range(NQ):
                dve.wait_ge(last_turned, q + 1)
                if q >= 2:
                    dve.wait_ge(last_out[q % 2], 32 * (q // 2))
                dve.tensor_copy(nat[0:LAST, q % 2, :], pt[0:LAST, q % 2, :]).then_inc(last_sb, 1)


def out_stage(k):
    nc, d = k.nc, k.d
    with ExitStack() as ctx:
        turned, copied = k.sem("y_turned"), k.sem("y_copied")
        y_out = [k.sem(f"y_out{u}") for u in range(2)]
        y = k.put("y", [P, 2, D], M_U)
        pt = k.ps(ctx, "y_pt", 4)
        block = ctx.enter_context(nc.Block())
        n_of = lambda t: P if t < PT else NS

        @block.sync
        def _(sp):
            for t in range(PT + 1):
                sp.wait_ge(copied, 2 * (t + 1))
                dst = d["y_prompt"][0, t * P:t * P + P, :] if t < PT else d["y_sample"].rearrange("b q n -> (b q) n")
                sp.dma_start(dst, y[0:n_of(t), t % 2, :]).then_inc(y_out[t % 2], 16)
            for u in range(2):
                sp.wait_ge(y_out[u], 16 * ((PT + 2 - u) // 2))

        @block.tensor
        def _(pe):
            for t in range(PT + 1):
                n = n_of(t)
                if t >= 2:
                    pe.wait_ge(copied, 2 * (t - 1))
                for c in range(KC):
                    ins = pe.transpose(pt[0:n, 2 * (t % 2) + c // 4, c % 4 * P:c % 4 * P + P], k.x1T[:, c, t * P:t * P + n], k.c("ident"))
                ins.then_inc(turned, 1)

        def copy_out(eng, copy, half):
            for t in range(PT + 1):
                n = n_of(t)
                eng.wait_ge(turned, t + 1)
                if t:
                    eng.wait_ge(copied, 2 * t)
                if t >= 2:
                    eng.wait_ge(y_out[t % 2], 16 * (t // 2))
                copy(y[0:n, t % 2, half * 512:(half + 1) * 512], pt[0:n, 2 * (t % 2) + half, :]).then_inc(copied, 1)

        @block.scalar
        def _(act):
            copy_out(act, lambda o, i: act.activation(o, i, ACT.Copy), 0)

        @block.vector
        def _(dve):
            copy_out(dve, lambda o, i: dve.tensor_copy(o, i), 1)


def layer(nc, d):
    k = Core(nc, d)
    k.const = k.put("const", [P, CONSTS.shape[1]], M_CONST)
    sb = k.area("small", M_SMALL, M_H)
    k.qw, k.kw = (sb(n, [P, 64]) for n in ("qw", "kw"))
    k.alog, k.dtb = (sb(n, [P, H]) for n in ("alog", "dtb"))
    k.wmix, k.wffn = (sb(n, [P, KC]) for n in ("wmix", "wffn"))
    k.wba = sb("wba", [P, KC, 2 * H])
    k.onorm, k.subln, k.lam = (sb(n, [P, 1]) for n in ("onorm", "subln", "lam"))
    k.g, k.beta = (k.put(n, [P, PT + 1, H], M_BIAS + 5216 + 160 * i) for i, n in enumerate(("g", "beta")))
    k.bias = k.put("bias", [P, H, 2 * P], M_BIAS)
    k.sbias = k.put("sbias", [P, PAST + QN], M_BIAS + 4096)
    dram = lambda name, shape: nc.dram_tensor(name, shape, F32, kind="Internal").ap()
    k.ob_dram = dram("obT_rows", (H, P, SEQ))
    k.xT_dram, k.qkvT_dram, k.gate_dram = dram("xT_rows", (KC, P, T)), dram("qkvT_rows", (CA, P, T)), dram("gate_rows", (2 * KC, P, T))

    k.x = k.put("x", [P, PT + 1, D], M_Z + KC * W * 4)
    k.wq = k.put("wq", [P, KC, W], M_Z)
    k.x_in = [k.sem(f"x_in{u}") for u in range(PT // 2 + 1)]
    k.wq_in, k.wba_in, k.x_spilled = (k.sem(n) for n in ("wq_in", "wba_in", "x_spilled"))
    load_stage(k)
    k.hH, k.hL = (k.put(n, [P, KC, TPAD], M_H + i * KC * TPAD * 4, F32R) for i, n in enumerate(("hH", "hL")))
    k.xT = k.put("xT", [P, KC, T], M_QKV)
    turn_stage(k)
    norm_stage(k, "n1", k.xT, k.wmix, k.hH, k.hL, k.area("n1", M_QKV + KC * ROW, M_Z), True)
    k.qT, k.kT = (k.put(n, [P, H, T], M_QKV + i * H * ROW) for i, n in enumerate(("qT", "kT")))
    k.v = k.put("v", [P, PT + 1, W], M_QKV + 2 * H * ROW)
    qkv_stage(k)
    gates_stage(k)
    k.clear()
    k.zT = k.put("zT", [P, H, T], M_Z)
    k.gate_w_in = [k.sem(f"gate_w_in{u}") for u in range(2)]
    conv_proj_stage(k)
    gate_proj_stage(k)
    k.oaH, k.oaL = (k.put(n, [P, H, T], M_OA + i * H * ROW, F32R) for i, n in enumerate(("oaH", "oaL")))
    k.clear()
    mixers_stage(k)
    k.clear()
    delta_stage(k, True)
    k.clear()
    k.obH, k.obL = k.put("obH", [P, H, T], M_OB, F32R), k.put("obL", [P, H, T], M_Z, F32R)
    decode_stage(k)
    k.clear()
    k.mH, k.mL = (k.put(n, [P, KC, T], M_MIX + i * KC * ROW, F32R) for i, n in enumerate(("mH", "mL")))
    mix_stage(k)
    k.x1T = k.put("x1T", [P, KC, T], M_X1)
    out_proj_stage(k)
    k.fH, k.fL = (k.put(n, [P, KC, T], M_MIX + i * KC * ROW, F32R) for i, n in enumerate(("fH", "fL")))
    norm_stage(k, "n2", k.x1T, k.wffn, k.fH, k.fL, k.area("n2", M_FFN, M_END), False)
    k.clear()
    ffn_stage(k)
    out_stage(k)


_INS = ["x_prompt", "x_sample", "cache_k", "cache_v", "state_delta", "state_conv_a", "state_conv_ffn", "page_table",
        "rel_bias", "norm_mix", "w_in", "conv_a", "a_log", "dt_bias", "onorm_a", "qnorm_b", "knorm_b", "lam_q1",
        "lam_k1", "lam_q2", "lam_k2", "subln_b", "w_branch", "w_o", "norm_ffn", "w_up", "conv_f", "conv_f_b", "w_down"]
_OUTS = [("y_prompt", (1, SEQ, D)), ("y_sample", (NSEQ, QN, D)), ("k_prompt", (1, 1, SEQ, H, DH)),
         ("v_prompt", (1, 1, SEQ, H, DH)), ("delta_prompt", (1, 1, H, DH, DH)), ("conv_a_prompt", (1, 1, TA - 1, QKV)),
         ("conv_ffn_prompt", (1, 1, TF - 1, 2 * DFF)), ("k_sample", (1, NSEQ, QN, H, DH)),
         ("v_sample", (1, NSEQ, QN, H, DH)), ("delta_sample", (1, NSEQ, H, DH, DH)),
         ("conv_a_sample", (1, NSEQ, TA - 1, QKV)), ("conv_ffn_sample", (1, NSEQ, TF - 1, 2 * DFF))]


def kernel(**inputs):
    import concourse.bacc as _bacc
    from concourse.bass_utils import run_bass_kernel_spmd as _run

    nc = _bacc.Bacc("TRN2", target_bir_lowering=False, num_devices=1)
    arrays, d = {"in_consts": CONSTS}, {}
    for name in _INS:
        arrays[f"in_{name}"] = np.ascontiguousarray(inputs[name])
    for name, a in arrays.items():
        d[name[3:]] = nc.dram_tensor(name, a.shape, mybir.dt.from_np(a.dtype), kind="ExternalInput").ap()
    for name, shape in _OUTS:
        d[name] = nc.dram_tensor(f"out_{name}", shape, F32, kind="ExternalOutput").ap()
    layer(nc, d)
    r = _run(nc, [arrays], core_ids=[0])
    return tuple(r.results[0][f"out_{name}"] for name, _ in _OUTS)
```
